# Optimizing a Trainium2 kernel written in Bass

```python
import math
import jax, jax.numpy as jnp
from jax import lax
import numpy as np

D_MODEL = 1024
BATCH = 1
SEQ = 256
DEPTH = 2
DEC_BATCH = 8
DEC_SEQ = 4
PAST_LEN = 2048
PAGE_SIZE = 128

N_EVEN = (DEPTH + 1) // 2
N_ODD = DEPTH // 2
CONV_W = 4
EPS = 1e-6
D_RNN = D_MODEL
LRU_BLOCKS = 8
LRU_BW = D_RNN // LRU_BLOCKS
LRU_C = 8.0
D_INNER = 2 * D_MODEL
SSD_HEADDIM = 64
SSD_HEADS = D_INNER // SSD_HEADDIM
SSD_GROUPS = 4
SSD_HPG = SSD_HEADS // SSD_GROUPS
SSD_STATE = 128
SSD_CONV_DIM = D_INNER + 2 * SSD_GROUPS * SSD_STATE
SSD_IN_DIM = D_INNER + SSD_CONV_DIM + SSD_HEADS
SSD_CHUNK = 128
N_MEM = 256
MEM_HEADS = 4
MEM_HD = D_MODEL // MEM_HEADS
D_FF = 2816
N_EXPERTS = 8
TOP_K = 2
D_FF_EXPERT = 3584

kernel_name = 'hybrid_rglru_ssd_memxattn_decode_step'

def rms_norm(x, g):
    xf = x.astype(jnp.float32)
    y = xf * lax.rsqrt(jnp.mean(xf * xf, axis=-1, keepdims=True) + EPS)
    return (y * g.astype(jnp.float32)).astype(x.dtype)

def causal_conv(x, prev, w, b):
    T = x.shape[1]
    xp = jnp.concatenate([prev.astype(x.dtype), x], axis=1)
    y = xp[:, 0:T] * w[0]
    for k in range(1, CONV_W):
        y = y + xp[:, k:k + T] * w[k]
    return y + b, xp[:, -(CONV_W - 1):]

def rglru_block(h, conv_prev, h_prev, w_in, conv_w, conv_b, w_a, b_a, w_x, b_x, lam, w_out):
    B, T, _ = h.shape
    proj = h @ w_in
    gate_branch, xb = jnp.split(proj, 2, axis=-1)
    xc, conv_new = causal_conv(xb, conv_prev, conv_w, conv_b)
    xblk = xc.reshape(B, T, LRU_BLOCKS, LRU_BW)
    r = jax.nn.sigmoid(jnp.einsum('btki,kij->btkj', xblk, w_a).reshape(B, T, D_RNN) + b_a)
    ig = jax.nn.sigmoid(jnp.einsum('btki,kij->btkj', xblk, w_x).reshape(B, T, D_RNN) + b_x)
    log_a = (-LRU_C * r.astype(jnp.float32)) * jax.nn.softplus(-lam.astype(jnp.float32))
    a = jnp.exp(log_a)
    u = jnp.sqrt(-jnp.expm1(2.0 * log_a)) * (ig * xc).astype(jnp.float32)
    u = u.at[:, 0].add(a[:, 0] * h_prev.astype(jnp.float32))

    def combine(left, right):
        a1, b1 = left
        a2, b2 = right
        return a1 * a2, a2 * b1 + b2

    _, hs = lax.associative_scan(combine, (a, u), axis=1)
    y = hs.astype(h.dtype) * jax.nn.gelu(gate_branch)
    return y @ w_out, hs[:, -1].astype(h_prev.dtype), conv_new

def segsum(a):
    l = a.shape[-1]
    cs = jnp.cumsum(a, axis=-1)
    diff = cs[..., :, None] - cs[..., None, :]
    mask = jnp.tril(jnp.ones((l, l), dtype=bool))
    return jnp.where(mask, diff, -jnp.inf)

def ssd_chunked(X, Adt, Bm, Cm, h0):
    b, T = X.shape[:2]
    Q = min(SSD_CHUNK, T)
    nc = -(-T // Q)
    pad = nc * Q - T
    if pad:
        padT = lambda t: jnp.pad(t, [(0, 0), (0, pad)] + [(0, 0)] * (t.ndim - 2))
        X, Adt, Bm, Cm = padT(X), padT(Adt), padT(Bm), padT(Cm)
    g, e, p = X.shape[2:]
    n = Bm.shape[-1]
    X = X.reshape(b, nc, Q, g, e, p)
    Bm = Bm.reshape(b, nc, Q, g, n)
    Cm = Cm.reshape(b, nc, Q, g, n)
    A = Adt.reshape(b, nc, Q, g, e).transpose(0, 3, 4, 1, 2)
    A_cs = jnp.cumsum(A, axis=-1)
    L = jnp.exp(segsum(A))
    CB = jnp.einsum('bclgn,bcsgn->bcgls', Cm, Bm)
    y_diag = jnp.einsum('bcgls,bgecls,bcsgep->bclgep', CB, L, X)
    decay_states = jnp.exp(A_cs[..., -1:] - A_cs)
    states = jnp.einsum('bclgn,bgecl,bclgep->bcgepn', Bm, decay_states, X)
    states = jnp.concatenate([h0[:, None], states], axis=1)
    chunk_decay = jnp.exp(segsum(jnp.pad(A_cs[..., -1], ((0, 0), (0, 0), (0, 0), (1, 0)))))
    new_states = jnp.einsum('bgezc,bcgepn->bzgepn', chunk_decay, states)
    states, final = new_states[:, :-1], new_states[:, -1]
    y_off = jnp.einsum('bclgn,bcgepn,bgecl->bclgep', Cm, states, jnp.exp(A_cs))
    y = (y_diag + y_off).reshape(b, nc * Q, g, e, p)[:, :T]
    return y, final

def ssd_block(h, conv_prev, s_prev, w_in, conv_w, conv_b, dt_bias, a_log, d_skip, norm_g, w_out):
    B, T, _ = h.shape
    proj = h @ w_in
    z = proj[..., :D_INNER]
    xbc = proj[..., D_INNER:D_INNER + SSD_CONV_DIM]
    dt = proj[..., D_INNER + SSD_CONV_DIM:]
    xbc, conv_new = causal_conv(xbc, conv_prev, conv_w, conv_b)
    xbc = jax.nn.silu(xbc).astype(jnp.float32)
    gn = SSD_GROUPS * SSD_STATE
    xs = xbc[..., :D_INNER].reshape(B, T, SSD_GROUPS, SSD_HPG, SSD_HEADDIM)
    Bm = xbc[..., D_INNER:D_INNER + gn].reshape(B, T, SSD_GROUPS, SSD_STATE)
    Cm = xbc[..., D_INNER + gn:].reshape(B, T, SSD_GROUPS, SSD_STATE)
    dt = jax.nn.softplus(dt.astype(jnp.float32) + dt_bias.astype(jnp.float32)).reshape(B, T, SSD_GROUPS, SSD_HPG)
    A = -jnp.exp(a_log.astype(jnp.float32)).reshape(SSD_GROUPS, SSD_HPG)
    h0 = s_prev.astype(jnp.float32).reshape(B, SSD_GROUPS, SSD_HPG, SSD_HEADDIM, SSD_STATE)
    y, s_new = ssd_chunked(xs * dt[..., None], A * dt, Bm, Cm, h0)
    y = y + d_skip.astype(jnp.float32).reshape(SSD_GROUPS, SSD_HPG, 1) * xs
    y = y.reshape(B, T, D_INNER) * jax.nn.silu(z.astype(jnp.float32))
    yg = y.reshape(B, T, SSD_GROUPS, D_INNER // SSD_GROUPS)
    yg = yg * lax.rsqrt(jnp.mean(yg * yg, axis=-1, keepdims=True) + EPS)
    y = (yg.reshape(B, T, D_INNER) * norm_g.astype(jnp.float32)).astype(h.dtype)
    s_new = s_new.reshape(B, SSD_HEADS, SSD_HEADDIM, SSD_STATE).astype(s_prev.dtype)
    return y @ w_out, s_new, conv_new

def mem_kv(mem, g, w_k, w_v):
    B = mem.shape[0]
    m = rms_norm(mem, g)
    k = (m @ w_k).reshape(B, N_MEM, MEM_HEADS, MEM_HD)
    v = (m @ w_v).reshape(B, N_MEM, MEM_HEADS, MEM_HD)
    return k, v

def mem_attend(h, k, v, w_q, w_o):
    B, T, _ = h.shape
    q = (h @ w_q).reshape(B, T, MEM_HEADS, MEM_HD)
    s = jnp.einsum('bthd,bmhd->bhtm', q, k).astype(jnp.float32) * (MEM_HD ** -0.5)
    pr = jax.nn.softmax(s, axis=-1).astype(h.dtype)
    o = jnp.einsum('bhtm,bmhd->bthd', pr, v).reshape(B, T, D_MODEL)
    return o @ w_o

def swiglu(h, w1, w3, w2):
    return (jax.nn.silu(h @ w1) * (h @ w3)) @ w2

def moe_swiglu(h, w_router, w1, w3, w2):
    logits = (h @ w_router).astype(jnp.float32)
    top_vals, top_idx = lax.top_k(logits, TOP_K)
    gates = jax.nn.softmax(top_vals, axis=-1)
    dense_gate = jnp.sum(jax.nn.one_hot(top_idx, N_EXPERTS, dtype=jnp.float32) * gates[..., None], axis=-2)
    dense_gate = dense_gate.astype(h.dtype)
    out = dense_gate[..., 0:1] * swiglu(h, w1[0], w3[0], w2[0])
    for ex in range(1, N_EXPERTS):
        out = out + dense_gate[..., ex:ex + 1] * swiglu(h, w1[ex], w3[ex], w2[ex])
    return out

def setup_inputs(seed: int = 0) -> dict:
    key = jax.random.key(seed)
    keys = iter(jax.random.split(key, 64))

    def nrm(shape, scale):
        return jax.random.normal(next(keys), shape, jnp.float32) * scale

    def uni(shape, lo, hi):
        return jax.random.uniform(next(keys), shape, jnp.float32, lo, hi)

    x_prompt = nrm((BATCH, SEQ, D_MODEL), 1.0)
    x_sample = nrm((DEC_BATCH, DEC_SEQ, D_MODEL), 1.0)
    state_lru_h = nrm((N_EVEN, DEC_BATCH, D_RNN), 1.0)
    state_lru_conv = nrm((N_EVEN, DEC_BATCH, CONV_W - 1, D_RNN), 1.0)
    state_ssd = nrm((N_ODD, DEC_BATCH, SSD_HEADS, SSD_HEADDIM, SSD_STATE), 0.1)
    state_ssd_conv = nrm((N_ODD, DEC_BATCH, CONV_W - 1, SSD_CONV_DIM), 1.0)
    cache_mem_k = nrm((DEPTH, DEC_BATCH, N_MEM, MEM_HEADS, MEM_HD), 1.0)
    cache_mem_v = nrm((DEPTH, DEC_BATCH, N_MEM, MEM_HEADS, MEM_HD), 1.0)
    mem_prompt = nrm((BATCH, N_MEM, D_MODEL), 1.0)
    norm_mix = 1.0 + nrm((DEPTH, D_MODEL), 0.01)
    norm_mem = 1.0 + nrm((DEPTH, D_MODEL), 0.01)
    norm_memkv = 1.0 + nrm((DEPTH, D_MODEL), 0.01)
    norm_ffn = 1.0 + nrm((DEPTH, D_MODEL), 0.01)
    norm_final = 1.0 + nrm((D_MODEL,), 0.01)
    lru_w_in = nrm((N_EVEN, D_MODEL, 2 * D_RNN), D_MODEL ** -0.5)
    lru_conv_w = nrm((N_EVEN, CONV_W, D_RNN), CONV_W ** -0.5)
    lru_conv_b = nrm((N_EVEN, D_RNN), 0.01)
    lru_w_a = nrm((N_EVEN, LRU_BLOCKS, LRU_BW, LRU_BW), LRU_BW ** -0.5)
    lru_b_a = nrm((N_EVEN, D_RNN), 0.01)
    lru_w_x = nrm((N_EVEN, LRU_BLOCKS, LRU_BW, LRU_BW), LRU_BW ** -0.5)
    lru_b_x = nrm((N_EVEN, D_RNN), 0.01)
    a_base = uni((N_EVEN, D_RNN), 0.9, 0.999) ** (1.0 / LRU_C)
    lru_lam = jnp.log(a_base) - jnp.log1p(-a_base)
    lru_w_out = nrm((N_EVEN, D_RNN, D_MODEL), D_RNN ** -0.5)
    ssd_w_in = nrm((N_ODD, D_MODEL, SSD_IN_DIM), D_MODEL ** -0.5)
    ssd_conv_w = nrm((N_ODD, CONV_W, SSD_CONV_DIM), CONV_W ** -0.5)
    ssd_conv_b = nrm((N_ODD, SSD_CONV_DIM), 0.01)
    dt0 = jnp.exp(uni((N_ODD, SSD_HEADS), math.log(1e-3), math.log(1e-1)))
    ssd_dt_bias = dt0 + jnp.log(-jnp.expm1(-dt0))
    ssd_a_log = jnp.log(uni((N_ODD, SSD_HEADS), 1.0, 16.0))
    ssd_d = 1.0 + nrm((N_ODD, SSD_HEADS), 0.01)
    ssd_norm_g = 1.0 + nrm((N_ODD, D_INNER), 0.01)
    ssd_w_out = nrm((N_ODD, D_INNER, D_MODEL), D_INNER ** -0.5)
    mem_w_q = nrm((DEPTH, D_MODEL, D_MODEL), D_MODEL ** -0.5)
    mem_w_k = nrm((DEPTH, D_MODEL, D_MODEL), D_MODEL ** -0.5)
    mem_w_v = nrm((DEPTH, D_MODEL, D_MODEL), D_MODEL ** -0.5)
    mem_w_o = nrm((DEPTH, D_MODEL, D_MODEL), D_MODEL ** -0.5)
    ffn_w1 = nrm((N_EVEN, D_MODEL, D_FF), D_MODEL ** -0.5)
    ffn_w3 = nrm((N_EVEN, D_MODEL, D_FF), D_MODEL ** -0.5)
    ffn_w2 = nrm((N_EVEN, D_FF, D_MODEL), D_FF ** -0.5)
    moe_router = nrm((N_ODD, D_MODEL, N_EXPERTS), D_MODEL ** -0.5)
    moe_w1 = nrm((N_ODD, N_EXPERTS, D_MODEL, D_FF_EXPERT), D_MODEL ** -0.5)
    moe_w3 = nrm((N_ODD, N_EXPERTS, D_MODEL, D_FF_EXPERT), D_MODEL ** -0.5)
    moe_w2 = nrm((N_ODD, N_EXPERTS, D_FF_EXPERT, D_MODEL), D_FF_EXPERT ** -0.5)
    return {'x_prompt': x_prompt, 'x_sample': x_sample,
            'state_lru_h': state_lru_h, 'state_lru_conv': state_lru_conv,
            'state_ssd': state_ssd, 'state_ssd_conv': state_ssd_conv,
            'cache_mem_k': cache_mem_k, 'cache_mem_v': cache_mem_v,
            'mem_prompt': mem_prompt,
            'norm_mix': norm_mix, 'norm_mem': norm_mem, 'norm_memkv': norm_memkv,
            'norm_ffn': norm_ffn, 'norm_final': norm_final,
            'lru_w_in': lru_w_in, 'lru_conv_w': lru_conv_w, 'lru_conv_b': lru_conv_b,
            'lru_w_a': lru_w_a, 'lru_b_a': lru_b_a, 'lru_w_x': lru_w_x, 'lru_b_x': lru_b_x,
            'lru_lam': lru_lam, 'lru_w_out': lru_w_out,
            'ssd_w_in': ssd_w_in, 'ssd_conv_w': ssd_conv_w, 'ssd_conv_b': ssd_conv_b,
            'ssd_dt_bias': ssd_dt_bias, 'ssd_a_log': ssd_a_log, 'ssd_d': ssd_d,
            'ssd_norm_g': ssd_norm_g, 'ssd_w_out': ssd_w_out,
            'mem_w_q': mem_w_q, 'mem_w_k': mem_w_k, 'mem_w_v': mem_w_v, 'mem_w_o': mem_w_o,
            'ffn_w1': ffn_w1, 'ffn_w3': ffn_w3, 'ffn_w2': ffn_w2,
            'moe_router': moe_router, 'moe_w1': moe_w1, 'moe_w3': moe_w3, 'moe_w2': moe_w2}

def reference(x_prompt, x_sample, state_lru_h, state_lru_conv, state_ssd, state_ssd_conv,
              cache_mem_k, cache_mem_v, mem_prompt,
              norm_mix, norm_mem, norm_memkv, norm_ffn, norm_final,
              lru_w_in, lru_conv_w, lru_conv_b, lru_w_a, lru_b_a, lru_w_x, lru_b_x, lru_lam, lru_w_out,
              ssd_w_in, ssd_conv_w, ssd_conv_b, ssd_dt_bias, ssd_a_log, ssd_d, ssd_norm_g, ssd_w_out,
              mem_w_q, mem_w_k, mem_w_v, mem_w_o,
              ffn_w1, ffn_w3, ffn_w2, moe_router, moe_w1, moe_w3, moe_w2):

    def layer(i, x, conv_prev, rec_prev, mk, mv):
        j = i // 2
        h = rms_norm(x, norm_mix[i])
        if i % 2 == 0:
            y, rec_new, conv_new = rglru_block(h, conv_prev, rec_prev, lru_w_in[j], lru_conv_w[j], lru_conv_b[j],
                                               lru_w_a[j], lru_b_a[j], lru_w_x[j], lru_b_x[j], lru_lam[j], lru_w_out[j])
        else:
            y, rec_new, conv_new = ssd_block(h, conv_prev, rec_prev, ssd_w_in[j], ssd_conv_w[j], ssd_conv_b[j],
                                             ssd_dt_bias[j], ssd_a_log[j], ssd_d[j], ssd_norm_g[j], ssd_w_out[j])
        x = x + y
        x = x + mem_attend(rms_norm(x, norm_mem[i]), mk, mv, mem_w_q[i], mem_w_o[i])
        h = rms_norm(x, norm_ffn[i])
        if i % 2 == 0:
            x = x + swiglu(h, ffn_w1[j], ffn_w3[j], ffn_w2[j])
        else:
            x = x + moe_swiglu(h, moe_router[j], moe_w1[j], moe_w3[j], moe_w2[j])
        return x, rec_new, conv_new

    bp = x_prompt.shape[0]
    xp, xs = x_prompt, x_sample
    p_lru_h, p_lru_conv, p_ssd, p_ssd_conv, p_mk, p_mv = [], [], [], [], [], []
    s_lru_h, s_lru_conv, s_ssd, s_ssd_conv = [], [], [], []
    for i in range(DEPTH):
        j = i // 2
        mk, mv = mem_kv(mem_prompt, norm_memkv[i], mem_w_k[i], mem_w_v[i])
        p_mk.append(mk)
        p_mv.append(mv)
        if i % 2 == 0:
            conv0 = jnp.zeros((bp, CONV_W - 1, D_RNN), x_prompt.dtype)
            rec0 = jnp.zeros((bp, D_RNN), state_lru_h.dtype)
            xp, r, c = layer(i, xp, conv0, rec0, mk, mv)
            p_lru_h.append(r)
            p_lru_conv.append(c)
            xs, r, c = layer(i, xs, state_lru_conv[j], state_lru_h[j], cache_mem_k[i], cache_mem_v[i])
            s_lru_h.append(r)
            s_lru_conv.append(c)
        else:
            conv0 = jnp.zeros((bp, CONV_W - 1, SSD_CONV_DIM), x_prompt.dtype)
            rec0 = jnp.zeros((bp, SSD_HEADS, SSD_HEADDIM, SSD_STATE), state_ssd.dtype)
            xp, r, c = layer(i, xp, conv0, rec0, mk, mv)
            p_ssd.append(r)
            p_ssd_conv.append(c)
            xs, r, c = layer(i, xs, state_ssd_conv[j], state_ssd[j], cache_mem_k[i], cache_mem_v[i])
            s_ssd.append(r)
            s_ssd_conv.append(c)
    y_prompt = rms_norm(xp, norm_final)
    y_sample = rms_norm(xs, norm_final)
    return (y_prompt, y_sample,
            jnp.stack(p_lru_h), jnp.stack(p_lru_conv), jnp.stack(p_ssd), jnp.stack(p_ssd_conv),
            jnp.stack(p_mk), jnp.stack(p_mv),
            jnp.stack(s_lru_h), jnp.stack(s_lru_conv), jnp.stack(s_ssd), jnp.stack(s_ssd_conv))


_drawn_inputs = setup_inputs


def setup_inputs(seed=0):
    import zlib

    import numpy as np

    out = dict(_drawn_inputs(seed))
    spreads = {}
    factors = {'norm_mem': 5.23,
     'norm_memkv': 5.017,
     'norm_final': 163.356,
     'lru_b_a': 4.028,
     'lru_b_x': 4.842,
     'ssd_d': 80.992,
     'ssd_norm_g': 76.096,
     'norm_ffn': 6.754,
     'ssd_conv_b': 3.353}
    for name, (base, spread) in spreads.items():
        noise = np.random.default_rng([zlib.crc32(name.encode()), seed]).standard_normal(out[name].shape)
        drawn = base * np.exp(spread * noise) if base else spread * noise
        out[name] = __import__('jax').numpy.asarray(drawn.astype(out[name].dtype))
    for name, factor in factors.items():
        out[name] = (out[name] * factor).astype(out[name].dtype)
    return out
```

```python
from contextlib import ExitStack

import concourse.bass as bass
from concourse import mybir

F32 = mybir.dt.float32
F32R = mybir.dt.float32r
I32 = mybir.dt.int32
ALU = mybir.AluOpType
ACT = mybir.ActivationFunctionType
AX = mybir.AxisListType

P = 128
D = 1024
KD = D // P
SEQ = 256
NB = 8
TS = 4
NT = SEQ + NB * TS
TOK = [(0, 128), (128, 128), (256, 32)]
CW = 4
PADW = (SEQ + CW - 1) + NB * (TS + CW - 1)
PS0 = SEQ + CW - 1
DI = 2048
KI = DI // P
NXBC = 24
HEADS = 32
GROUPS = 4
MH = 4
NMEM = 256
FF = 2816
KF = FF // P
NE = 8
NV = 3 * NE
FE = 3584
KFE = FE // P
FB = FE // 512
EPS = 1e-6

CH = 1024
RAW = 7
HL = 7
CPE = 3 * KFE
assert CPE % RAW == 0 and CPE % HL == 0

SMALL = {}
_at = 0
for _name, _n in [("g_mix", 16), ("g_mem", 16), ("g_memkv", 16), ("g_ffn", 16), ("g_fin", 8),
                  ("lru_cw", 32), ("lru_cb", 8), ("b_a", 8), ("b_x", 8), ("lam", 8), ("h_prev", 64),
                  ("lru_prev", 192), ("ssd_cw", 96), ("ssd_cb", 24), ("ssd_g", 16), ("ssd_d", 16),
                  ("dt_b", 32), ("a_log", 32), ("router", 64), ("w_dt", 256),
                  ("ident", 128), ("tri", 128), ("tri_s", 32), ("last", 128), ("last_s", 32),
                  ("is_last", 8), ("in_seq", 8), ("ones", 128), ("before", 128), ("iota", 128),
                  ("lower", 64), ("eps", 1)]:
    SMALL[_name] = (_at, _n)
    _at += _n
NSMALL = _at


def plan():
    p = [("mem norm", "act", 0, 0)]
    for l in range(2):
        p += [(("k", l, j), "act", 1, 0) for j in range(KD)]
        for nb in range(2):
            p += [(("v", l, nb, 0), "dve", 3, 0), (("v", l, nb, 1), "dve", 1, 0)]
    p += [(("norm", 0), "act", 0, 0)]
    p += [(("gate", j), "act", 1, 0) for j in range(KD)] + [(("xb", j), "act", 1, 0) for j in range(KD)]
    p += [(("r", j), "act", int(j == 0), 0) for j in range(KD)]
    p += [(("i", j), "act", int(j == 0), 0) for j in range(KD)]
    p += [(("lru out", j), "dve", 1, 0) for j in range(KD)]

    def attention(l):
        q = [(("norm", 3 * l + 1), "act", 0, 0)]
        q += [(("q", l, j), "act", 1, 0) for j in range(KD)]
        q += [(("scores", l, h), "act", 0, 0) for h in range(MH)]
        q += [(("s scores", l), "act", 0, 2 * NB), (("s turn", l), "act", 0, 0)]
        q += [(("probs", l, i), "dve", 0, 0) for i in range(4)] + [(("s probs", l), "dve", 0, 0)]
        q += [(("o", l, j), "act", 0, 0) for j in range(KD)] + [(("s o", l), "act", 0, 2 * NB)]
        return q + [(("mem out", l, j), "dve", 1, 0) for j in range(KD)]

    p += attention(0)
    p += [(("norm", 2), "act", 0, 0)]
    for f in range(KF):
        p += [(("f1", f), "act", 1, 0), (("f3", f), "dve", 1, 0)]
    p += [(("f2", j), "dve", -(-KF * (j + 1) // 8) + KF * j // -8, 0) for j in range(KD)]
    p += [(("norm", 3), "act", 0, 0), ("dt", "dve", 0, 0)]
    p += [(("xbc", c), "act", 1, 0) for c in range(NXBC)] + [(("z", c), "act", 1, 0) for c in range(KI)]
    for t in range(3):
        p += [(("acs", t), "dve", 0, 0), (("last", t), "dve", 0, 0)]
        p += [(("xt", t, i), "dve", 0, 0) for i in range(4)]
        p += [(("bt", t), "act", 0, 0), (("cb", t), "dve", 0, 0)]
        p += [(("ab", t, 0), "dve", 0, 0)]
        for hb in range(8):
            p += [(("ab", t, hb + 1), "dve", 0, 0)] * (hb < 7) + [(("y", t, hb), "dve", 0, 0)]
        if t < 2:
            p += [(("state", t, g), "act" if t == 0 else "dve", 0, 0) for g in range(GROUPS)]
    p += [("s decay", "act", 0, 0), ("expand", "act", 0, 0)]
    for b in range(NB):
        p += [(("y off", b), "dve", 0, 2)] + [(("s state", b, g), "dve", 0, 0) for g in range(GROUPS)]
    p += [(("gn", g), "act", 0, 0) for g in range(GROUPS)]
    p += [(("ssd out", j), "dve", 2, 0) for j in range(KD)]
    p += attention(1)
    p += [(("norm", 5), "act", 0, 0), ("logits", "dve", 0, 0), ("pos", "dve", 0, 0)]
    p += [(("ht", i), "dve", 0, 0) for i in range(6)]
    return p


def stream_order():
    order = []
    for _, _, split, raw in plan():
        order += ["w"] * split
        if raw == 2 * NB:
            order += ["c"] * raw
        elif raw:
            order += ["s"] * raw
    return order


NSTAT = len(stream_order())


def build_program(nc, t):
    PLAN = plan()
    KEY = {key: g for g, (key, _, _, _) in enumerate(PLAN)}
    NEED, split_n = [], 0
    for _, _, split, _ in PLAN:
        split_n += split
        NEED.append(split_n)
    NSPLIT = split_n
    FREED = []
    freed_n = {"act": 0, "dve": 0}
    for _, eng, _, _ in PLAN:
        freed_n[eng] += 1
        FREED.append((eng, freed_n[eng]))
    ORDER = stream_order()

    with ExitStack() as ctx:
        def sem(name):
            return ctx.enter_context(nc.semaphore(name))

        base = -(-nc.sbuf_base // 64) * 64
        arena = nc.alloc_sbuf_tensor("arena", [P, (nc.sbuf_usable_end - base) // 4 - 64], F32)

        def at(name, shape, dtype, offset):
            return nc.alloc_sbuf_tensor_at(name, [P] + shape, dtype, offset=offset, align_bytes=4)

        o_raw = base
        o_hi = o_raw + RAW * CH * 4
        o_lo = o_hi + HL * CH * 4
        o_x = o_lo + HL * CH * 4
        o_small = o_x + KD * NT * 4
        area = -(-(o_small + NSMALL * 4) // 64) * 64
        SLOT = KD * NT * 4
        S = [area + i * SLOT for i in range(11)]
        tail = S[10] + SLOT
        end = nc.sbuf_usable_end
        raw = at("raw", [RAW, CH], F32, o_raw)
        w_hi = at("w_hi", [HL, CH], F32R, o_hi)
        w_lo = at("w_lo", [HL, CH], F32R, o_lo)
        x = at("x_res", [KD, NT], F32, o_x)
        small = at("small", [NSMALL], F32, o_small)

        def par(name):
            a, n = SMALL[name]
            return small[:, a:a + n]

        ident, tri, ones = par("ident"), par("tri"), par("ones")
        eps = par("eps")
        h = at("h", [KD, NT], F32, S[0])
        h_hi = at("h_hi", [KD, NT], F32R, S[1])
        h_lo = at("h_lo", [KD, NT], F32R, S[2])
        rt = at("rt", [NT], F32, tail)
        rs = at("rs", [NT], F32, tail + NT * 4)
        nc8 = at("nc8", [KD], F32, tail + 2 * NT * 4)
        sp = at("sp", [6, 96], F32, tail + 2 * NT * 4 + 64)
        dt_off = tail + 2 * NT * 4 + 64 + 6 * 96 * 4
        dt = at("dt", [3, HEADS], F32, dt_off)
        adt = at("adt", [3, HEADS], F32, dt_off + 384)
        acs = at("acs", [HEADS], F32, dt_off + 768)
        dec = at("dec", [HEADS], F32, dt_off + 896)
        cdec = at("cdec", [HEADS], F32, dt_off + 1024)
        last_dec = at("last_dec", [HEADS], F32, dt_off + 1152)
        assert dt_off + 1280 <= end, (dt_off + 1280, end)

        memx = at("memx", [KD, NMEM], F32, S[5])
        memsq = at("memsq", [KD, NMEM], F32, S[3])
        memg = at("memg", [KD, NMEM], F32, S[3])
        mem_hi = at("mem_hi", [KD, NMEM], F32R, S[6])
        mem_lo = at("mem_lo", [KD, NMEM], F32R, S[7])
        kmem = [at(f"kmem{l}", [KD, NMEM], F32, S[4 + 5 * l]) for l in range(2)]
        vmem = [at(f"vmem{l}", [2, D], F32, S[8 + 2 * l]) for l in range(2)]
        gate = at("gate", [KD, NT], F32, S[3])
        conv = at("conv", [KD, PADW], F32, S[9])
        conv_t = at("conv_t", [2, PADW], F32, S[4])
        xc = at("xc", [KD, NT], F32, S[5])
        xc_hi = at("xc_hi", [KD, NT], F32R, S[6])
        xc_lo = at("xc_lo", [KD, NT], F32R, S[7])
        rg = at("rg", [KD, NT], F32, S[8])
        ig = at("ig", [KD, NT], F32, S[1])
        decay = at("decay", [KD, NT], F32, S[0])
        expm = at("expm", [KD, NT], F32, S[9])
        tanh = at("tanh", [KD, NT], F32, S[2])
        hs = at("hs", [KD, NT], F32, S[4])
        hs_t = at("hs_t", [KD, NB], F32, dt_off)
        lru_new_h = at("lru_new_h", [KD, 1 + NB], F32, dt_off + 256)
        lru_new_c = at("lru_new_c", [KD, 3 * (1 + NB)], F32, dt_off + 256 + 320)
        assert dt_off + 576 + 8 * 27 * 4 <= end
        q = at("q", [KD, NT], F32, S[3])
        kt = at("kt", [KD, NMEM], F32, S[4])
        vt = at("vt", [2, D], F32, S[5])
        pr = at("pr", [9, NMEM], F32, S[6])
        prt = at("prt", [2, MH, SEQ], F32, S[7])
        sprt = at("sprt", [2, P], F32, S[7] + 8192)
        att = at("att", [KD, NT], F32, S[8])
        att_hi = at("att_hi", [KD, NT], F32R, S[9])
        att_lo = at("att_lo", [KD, NT], F32R, S[10])
        st = at("st", [2, P], F32, dt_off)
        mx = at("mx", [9], F32, dt_off + 1024)
        nmx = at("nmx", [9], F32, dt_off + 1024 + 64)
        rsum = at("rsum", [9], F32, dt_off + 1152)
        rinv = at("rinv", [9], F32, dt_off + 1216)
        f_hi = at("f_hi", [KF, NT], F32R, S[3])
        f_lo = at("f_lo", [KF, NT], F32R, S[3] + KF * NT * 4)
        f_s = at("f_s", [2, NT], F32, S[3] + 2 * KF * NT * 4)
        f_g = at("f_g", [2, NT], F32, S[3] + 2 * KF * NT * 4 + 2 * NT * 4)
        y = at("y", [KI, NT], F32, S[3])
        bc = at("bc", [8, NT], F32, S[5])
        zs = at("zs", [KI, NT], F32, S[6])
        cv = at("cv", [3, PADW], F32, S[8])
        cv_t = at("cv_t", [PADW], F32, S[8] + 3 * PADW * 4)
        cv_o = at("cv_o", [2, NT], F32, S[8] + 4 * PADW * 4)
        ssd_prev = at("ssd_prev", [NXBC, NB, 3], F32, S[9])
        ssd_new_c = at("ssd_new_c", [NXBC, 27], F32, S[9] + NXBC * 24 * 4)
        xt = at("xt", [DI], F32, S[0])
        xd = at("xd", [DI], F32, S[1])
        s_a = at("s_a", [DI], F32, S[2])
        s_b = at("s_b", [DI], F32, S[8])
        s_new = at("s_new", [2, CH], F32, S[8])
        bt = at("bt", [512], F32, S[9])
        cbm = at("cbm", [512], F32, S[9] + 2048)
        mt = at("mt", [2, 512], F32, S[9] + 4096)
        diff = at("diff", [2, 512], F32, S[10])
        eb = at("eb", [512], F32, S[10] + 4096)
        ce = at("ce", [512], F32, S[10] + 6144)
        btm = at("btm", [2, 512], F32, S[10])
        sdec = at("sdec", [NB * HEADS], F32, S[0] + 8192)
        ef = at("ef", [KI, 32], F32, S[10] + 4096)
        ea = at("ea", [HEADS], F32, S[1] + 8192)
        sdr = at("sdr", [NB * HEADS], F32, S[2] + 8192)
        yo_t = at("yo_t", [2, 64], F32, S[10] + 6144)
        ysq = at("ysq", [KI, NT], F32, S[6])
        y_hi = at("y_hi", [KI, NT], F32R, S[6])
        y_lo = at("y_lo", [KI, NT], F32R, S[0])
        grt = at("grt", [GROUPS, NT], F32, S[9])
        grs = at("grs", [GROUPS, NT], F32, S[9] + GROUPS * NT * 4)
        htok = at("htok", [3, D], F32, S[3])
        o_e = S[3] + 3 * D * 4
        sel = at("sel", [3, P], F32, o_e)
        selg = at("selg", [3, P], F32, o_e + 1536)
        sg = at("sg", [NT], F32, o_e + 3072)
        xe_hi = at("xe_hi", [KD * P], F32R, o_e + 3072 + 1152)
        xe_lo = at("xe_lo", [KD * P], F32R, o_e + 3072 + 1152 + 4096)
        o_g = o_e + 3072 + 1152 + 8192
        sil = at("sil", [2, 512], F32, o_g)
        ge = at("ge", [2, 512], F32, o_g + 4096)
        gt_hi = at("gt_hi", [KFE, P], F32R, o_g + 8192)
        gt_lo = at("gt_lo", [KFE, P], F32R, o_g + 8192 + KFE * 512)
        ye = at("ye", [D], F32, o_g + 8192 + KFE * 1024)
        o_r = o_g + 8192 + KFE * 1024 + 4096
        lg = at("lg", [3, NE], F32, o_r)
        cmp1 = at("cmp1", [3, NE, NE], F32, o_r + 128)
        cmp2 = at("cmp2", [3, NE, NE], F32, o_r + 896)
        rank = at("rank", [3, NE], F32, o_r + 1664)
        m1 = at("m1", [3, NE], F32, o_r + 1760)
        m2 = at("m2", [3, NE], F32, o_r + 1856)
        v12 = at("v12", [4, 3], F32, o_r + 1952)
        pos = at("pos", [3, NV + 1], F32, o_r + 2048)
        msk = at("msk", [3, NV + 1], F32, o_r + 2368)
        gts = at("gts", [3, NV + 1], F32, o_r + 2688)
        cmax = at("cmax", [1], F32, o_r + 3008)
        cmax_i = at("cmax_i", [1], I32, o_r + 3072)
        assert o_r + 3104 <= tail

        ps = ctx.enter_context(nc.psum_tensor("ps", [P, 8, 512], F32))

        small_in = sem("small_in")
        x_in = sem("x_in")
        mem_in = sem("mem_in")
        prev_in = sem("prev_in")
        landed = [sem(f"landed{s}") for s in range(RAW)]
        kv_out = sem("kv_out")
        kv_in = sem("kv_in")
        out_done = sem("out_done")
        x_out = sem("x_out")
        hi_done = sem("hi_done")
        lo_done = sem("lo_done")
        full = sem("full")
        raw_used = sem("raw_used")
        act_freed = sem("act_freed")
        dve_freed = sem("dve_freed")
        chain = sem("chain")
        sq_done = sem("sq_done")
        rt_done = sem("rt_done")
        h_done = sem("h_done")
        hh_done = sem("hh_done")
        hl_done = sem("hl_done")
        mg_done = sem("mg_done")
        mh_done = sem("mh_done")
        ml_done = sem("ml_done")
        sp_abs = sem("sp_abs")
        sp_exp = sem("sp_exp")
        sp_sum = sem("sp_sum")
        sp_ln = sem("sp_ln")
        cinit = sem("cinit")
        xc_done = sem("xc_done")
        xch_done = sem("xch_done")
        xcl_done = sem("xcl_done")
        c8_done = sem("c8_done")
        a_done = sem("a_done")
        e2_done = sem("e2_done")
        q_done = sem("q_done")
        root_done = sem("root_done")
        hs_done = sem("hs_done")
        y_done = sem("y_done")
        yh_done = sem("yh_done")
        yl_done = sem("yl_done")
        resid = sem("resid")
        state_ready = sem("state_ready")
        max_done = sem("max_done")
        pn_done = sem("pn_done")
        fh_done = sem("fh_done")
        fl_done = sem("fl_done")
        prev_done = sem("prev_done")
        save_done = sem("save_done")
        cvo_done = sem("cvo_done")
        silu_done = sem("silu_done")
        adt_done = sem("adt_done")
        alog_exp = sem("alog_exp")
        ld_done = sem("ld_done")
        dec_done = sem("dec_done")
        xt_done = sem("xt_done")
        xd_done = sem("xd_done")
        cbm_done = sem("cbm_done")
        diff_done = sem("diff_done")
        ex_done = sem("ex_done")
        eb_done = sem("eb_done")
        ce_done = sem("ce_done")
        mt_done = sem("mt_done")
        sad_done = sem("sad_done")
        sb_done = sem("sb_done")
        sdr_done = sem("sdr_done")
        btm_done = sem("btm_done")
        sn_dec = sem("sn_dec")
        sn_done = sem("sn_done")
        yz_done = sem("yz_done")
        state_out = [sem(f"state_out{i}") for i in range(3)]
        ysq_done = sem("ysq_done")
        msk_done = sem("msk_done")
        xp_done = sem("xp_done")
        xpe_done = sem("xpe_done")
        cnt_done = sem("cnt_done")
        fin_done = sem("fin_done")

        class Pass:
            def __init__(self, c):
                def s(name):
                    return sem(f"{name}_{c}")
                self.landed = landed if c == 0 else [s(f"e_landed{i}") for i in range(RAW)]
                self.hi = s("e_hi")
                self.lo = s("e_lo")
                self.used = s("e_used")
                self.sel = s("e_sel")
                self.gather = s("e_gather")
                self.xh = s("e_xh")
                self.xl = s("e_xl")
                self.silu = s("e_silu")
                self.g = s("e_g")
                self.turn = s("e_turn")
                self.gh = s("e_gh")
                self.gl = s("e_gl")
                self.ye = s("e_ye")
                self.sgt = s("e_sgt")
                self.sg = s("e_sg")
                self.scat = s("e_scat")
                self.add = s("e_add")
                self.chain = s("e_chain")

        PASSES = [Pass(c) for c in range(2)]
        VIRTUAL = [(0, NE), (NE, 2 * NE)]
        block = ctx.enter_context(nc.Block())

        SPLIT_AT = [i for i, k in enumerate(ORDER) if k == "w"]
        RAW_GROUP = [g for g, (_, _, _, rawn) in enumerate(PLAN) for _ in range(rawn)]
        RAW_INDEX = [i for i, k in enumerate(ORDER) if k != "w"]
        AHEAD = []
        for g in range(len(PLAN)):
            first = min((i for i, rg_ in zip(RAW_INDEX, RAW_GROUP) if rg_ >= g), default=NSTAT)
            AHEAD.append(min(NEED[g] + HL - 1, sum(i < first + RAW for i in SPLIT_AT)))
            assert AHEAD[g] >= NEED[g]

        RESID = [0] + [FREED[KEY[key]][1] for key in (("lru out", KD - 1), ("mem out", 0, KD - 1), ("f2", KD - 1),
                                                      ("ssd out", KD - 1), ("mem out", 1, KD - 1))]

        def bank(g, n=512, rows=P):
            return ps[0:rows, g % 8, 0:n]

        def samples(ap2, width, first, n):
            return ap2.rearrange("p (b w) -> p b w", w=width)[:, :, first:first + n]

        RELEASE = {}
        used_n = raw_n = state_n = 0
        i = 0
        CHUNK_GROUP = []
        for g, (key, _, split, rawn) in enumerate(PLAN):
            for _ in range(split):
                RELEASE[i] = [(lo_done, used_n + 1)]
                used_n += 1
                i += 1
                CHUNK_GROUP.append(g)
            for r in range(rawn):
                if r == rawn - 1:
                    RELEASE[i] = [(full, g + 1)]
                else:
                    raw_n += 1
                    RELEASE[i] = [(raw_used, raw_n)]
                if rawn == 2:
                    state_n += 1
                    RELEASE[i].append((sn_dec, state_n))
                i += 1
        for j in range(KD):
            for c in range(-(-KF * j // 8) - (1 if KF * j % 8 else 0), -(-KF * (j + 1) // 8)):
                CHUNK_GROUP[NEED[KEY["f2", 0]] - -(-KF // 8) + c] = KEY["f2", j]
        for l in range(2):
            for nb in range(2):
                for c in range(4):
                    CHUNK_GROUP[NEED[KEY["v", l, nb, 1]] - 4 + c] = KEY["v", l, nb, 1]
        for kind in ("r", "i"):
            CHUNK_GROUP[NEED[KEY[kind, 0]] - 1] = KEY[kind, KD - 1]

        def dram_chunk(i):
            return t["stream"][i, :, :]

        def overflow(eng):
            eng.wait_ge(cnt_done, 1)
            return eng.value_load(cmax_i[0:1, 0:1], min_val=0, max_val=NT)

        @block.sync
        def _(sp):
            sp.dma_start(small[:, :], t["small"]).then_inc(small_in, 16)
            sp.dma_start(memx[:, :, :], t["mem"]).then_inc(mem_in, 16)
            sp.dma_start(x[:, :, :], t["x"]).then_inc(x_in, 16)
            for i in range(NSTAT):
                if i >= RAW:
                    for s, v in RELEASE[i - RAW]:
                        sp.wait_ge(s, v)
                sp.dma_start(raw[:, i % RAW, :], t["stream"][i, :, :]).then_inc(landed[i % RAW], 16)

            def experts(c):
                s = PASSES[c]
                with sp.Fori(0, VIRTUAL[c][1] // NE) as turn:
                    with sp.Fori(0, NE) as e:
                        for p in range(CPE):
                            src = t["experts"][bass.ds(e * CPE + p, 1), :, :].rearrange("a p n -> p (a n)")
                            sp.wait_ge(s.lo, turn * (NE * CPE) + e * CPE + p + 1)
                            sp.dma_start(raw[:, (NSTAT + p) % RAW, :], src) \
                                .then_inc(s.landed[(NSTAT + p) % RAW], 16)

            sp.wait_ge(lo_done, NSPLIT)
            experts(0)
            over = overflow(sp)
            with sp.If(over > P):
                experts(1)
                sp.nop()
            sp.nop()

        @block.scalar
        def _(act):
            ptr = [0]

            def hi_upto(n):
                while ptr[0] < min(n, NSPLIT):
                    k = ptr[0]
                    i = SPLIT_AT[k]
                    act.wait_ge(landed[i % RAW], 16 * (i // RAW + 1))
                    if k >= HL:
                        act.wait_ge(full, CHUNK_GROUP[k - HL] + 1)
                    act.activation(w_hi[:, k % HL, :], raw[:, i % RAW, :], ACT.Copy).then_inc(hi_done, 1)
                    ptr[0] += 1

            def ready(key, n=512, rows=P):
                g = KEY[key]
                hi_upto(AHEAD[g])
                act.wait_ge(full, g + 1)
                return bank(g, n, rows)

            def norm(i):
                hi_upto(AHEAD[KEY["norm", i]])
                act.wait_ge(x_in, 16) if i == 0 else act.wait_ge(dve_freed, RESID[i])
                act.activation(h[:, :, :], x[:, :, :], ACT.Square).then_inc(sq_done, 1)
                b = ready(("norm", i), NT)
                act.activation(rt[:, :], b, ACT.Sqrt, bias=eps[:, 0:1], scale=1.0 / D).then_inc(act_freed, 1)
                act.wait_ge(h_done, i + 1)
                act.activation(h_hi[:, :, :], h[:, :, :], ACT.Copy).then_inc(hh_done, 1)

            act.wait_ge(mem_in, 16)
            act.wait_ge(small_in, 16)
            act.activation(memsq[:, :, :], memx[:, :, :], ACT.Square).then_inc(sq_done, 1)
            b = ready("mem norm", NMEM)
            act.activation(rt[:, 0:NMEM], b, ACT.Sqrt, bias=eps[:, 0:1], scale=1.0 / D).then_inc(act_freed, 1)
            for l in range(2):
                act.wait_ge(mg_done, l + 1)
                if l == 1:
                    act.wait_ge(full, KEY["v", 0, 1, 1] + 1)
                act.activation(mem_hi[:, :, :], memg[:, :, :], ACT.Copy).then_inc(mh_done, 1)
                for j in range(KD):
                    b = ready(("k", l, j), NMEM)
                    act.activation(kmem[l][:, j, :], b, ACT.Copy).then_inc(act_freed, 1)
                act.wait_ge(act_freed, FREED[KEY["k", l, KD - 1]][1])
                act.dma_start(t["out_k"][l], kmem[l][:, :, :]).then_inc(kv_out, 16)
                hi_upto(AHEAD[KEY["v", l, 1, 1]])
                act.wait_ge(dve_freed, FREED[KEY["v", l, 1, 1]][1])
                act.dma_start(t["out_v"][l], vmem[l][:, :, :]).then_inc(kv_out, 16)
            act.wait_ge(sp_abs, 1)
            act.activation(sp[:, 1, 0:KD], sp[:, 0, 0:KD], ACT.Exp, scale=-1.0).then_inc(sp_exp, 1)
            act.wait_ge(sp_sum, 1)
            act.activation(sp[:, 3, 0:KD], sp[:, 2, 0:KD], ACT.Ln).then_inc(sp_ln, 1)
            norm(0)
            for j in range(KD):
                b = ready(("gate", j), NT)
                act.activation(gate[:, j, :], b, ACT.Gelu_apprx_tanh).then_inc(act_freed, 1)
            act.wait_ge(cinit, 1)
            for j in range(KD):
                b = ready(("xb", j), NT)
                act.activation(conv[:, j, CW - 1:PS0], b[:, 0:SEQ], ACT.Copy)
                act.activation(samples(conv[:, j, PS0:PADW], TS + CW - 1, CW - 1, TS),
                               b[:, SEQ:NT].rearrange("p (b w) -> p b w", w=TS), ACT.Copy) \
                    .then_inc(act_freed, 1)
                if j >= 1:
                    act.wait_ge(xc_done, j)
                    act.activation(xc_hi[:, j - 1, :], xc[:, j - 1, :], ACT.Copy).then_inc(xch_done, 1)
            act.wait_ge(xc_done, KD)
            act.activation(xc_hi[:, KD - 1, :], xc[:, KD - 1, :], ACT.Copy).then_inc(xch_done, 1)
            act.wait_ge(kv_out, 64)
            for j in range(KD):
                b = ready(("r", j), NT)
                act.activation(rg[:, j, :], b, ACT.Sigmoid, bias=par("b_a")[:, j:j + 1]).then_inc(act_freed, 1)
            for j in range(KD):
                b = ready(("i", j), NT)
                act.activation(ig[:, j, :], b, ACT.Sigmoid, bias=par("b_x")[:, j:j + 1]).then_inc(act_freed, 1)
            act.wait_ge(c8_done, 1)
            act.wait_ge(act_freed, FREED[KEY["r", KD - 1]][1])
            for j in range(KD):
                act.activation(decay[:, j, :], rg[:, j, :], ACT.Exp, scale=nc8[:, j:j + 1]).then_inc(a_done, 1)
            for j in range(KD):
                act.activation(tanh[:, j, :], rg[:, j, :], ACT.Tanh, scale=nc8[:, j:j + 1])
            act.wait_ge(a_done, KD)
            act.wait_ge(state_ready, 1)
            act.activation(expm[:, :, :], decay[:, :, :], ACT.Square).then_inc(e2_done, 1)
            act.wait_ge(q_done, 1)
            act.activation(expm[:, :, :], expm[:, :, :], ACT.Sqrt, scale=-1.0).then_inc(root_done, 1)
            act.wait_ge(y_done, 1)
            act.activation(xc_hi[:, :, :], tanh[:, :, :], ACT.Copy).then_inc(yh_done, 1)

            def attention(l):
                norm(3 * l + 1)
                for j in range(KD):
                    b = ready(("q", l, j), NT)
                    act.activation(q[:, j, :], b, ACT.Copy).then_inc(act_freed, 1)
                act.wait_ge(kv_in, 32 * (l + 1))
                for hd in range(MH):
                    b = ready(("scores", l, hd))
                    act.wait_ge(max_done, 5 * l + hd + 1)
                    for tt in range(2):
                        k = 2 * hd + tt
                        a = act.activation(pr[:, k, :], b[:, tt * NMEM:(tt + 1) * NMEM], ACT.Exp,
                                           bias=nmx[:, k:k + 1], scale=1.0 / 16, accum_out=rsum[:, k:k + 1])
                    a.then_inc(act_freed, 1)
                b = ready(("s scores", l), NMEM)
                act.activation(st[:, :, :], b, ACT.Copy).then_inc(act_freed, 1)
                b = ready(("s turn", l), NMEM)
                act.wait_ge(max_done, 5 * l + 5)
                act.activation(pr[:, 8, :], b, ACT.Exp, bias=nmx[:, 8:9], scale=1.0 / 16,
                               accum_out=rsum[:, 8:9]).then_inc(act_freed, 1)
                for j in range(KD):
                    b = ready(("o", l, j), SEQ)
                    act.activation(att[:, j, 0:SEQ], b, ACT.Copy).then_inc(act_freed, 1)
                b = ready(("s o", l), NMEM)
                act.activation(att[:, :, SEQ:NT], b.rearrange("p (j s) -> p j s", j=KD), ACT.Copy) \
                    .then_inc(act_freed, 1)
                act.wait_ge(act_freed, FREED[KEY["s o", l]][1])
                act.activation(att_hi[:, :, :], att[:, :, :], ACT.Copy).then_inc(yh_done, 1)

            attention(0)
            norm(2)
            for f in range(KF):
                b = ready(("f1", f), NT)
                if f >= 2:
                    act.wait_ge(dve_freed, FREED[KEY["f3", f - 2]][1])
                act.activation(f_s[:, f % 2, :], b, ACT.Silu).then_inc(act_freed, 1)
                if f >= 1:
                    act.wait_ge(dve_freed, FREED[KEY["f3", f - 1]][1])
                    act.activation(f_hi[:, f - 1, :], f_g[:, (f - 1) % 2, :], ACT.Copy).then_inc(fh_done, 1)
                hi_upto(AHEAD[KEY["f3", f]])
            act.wait_ge(dve_freed, FREED[KEY["f3", KF - 1]][1])
            act.activation(f_hi[:, KF - 1, :], f_g[:, (KF - 1) % 2, :], ACT.Copy).then_inc(fh_done, 1)
            for j in range(KD):
                hi_upto(AHEAD[KEY["f2", j]])

            norm(3)
            act.wait_ge(sp_abs, 2)
            act.activation(sp[:, 1, :], sp[:, 0, :], ACT.Exp, scale=-1.0).then_inc(sp_exp, 1)
            act.activation(last_dec[:, :], par("a_log"), ACT.Exp).then_inc(alog_exp, 1)
            act.wait_ge(sp_sum, 2)
            act.activation(sp[:, 3, :], sp[:, 2, :], ACT.Ln).then_inc(sp_ln, 1)

            def silu_tile(c):
                act.wait_ge(cvo_done, c + 1)
                dst = y[:, c, :] if c < KI else bc[:, c - KI, :]
                act.activation(dst, cv_o[:, c % 2, :], ACT.Silu).then_inc(silu_done, 1)

            for c in range(NXBC):
                b = ready(("xbc", c), NT)
                act.wait_ge(prev_done, c + 1)
                act.activation(cv[:, c % 3, CW - 1:PS0], b[:, 0:SEQ], ACT.Copy)
                act.activation(samples(cv[:, c % 3, PS0:PADW], TS + CW - 1, CW - 1, TS),
                               b[:, SEQ:NT].rearrange("p (b w) -> p b w", w=TS), ACT.Copy) \
                    .then_inc(act_freed, 1)
                if c >= 1:
                    silu_tile(c - 1)
            silu_tile(NXBC - 1)
            for c in range(KI):
                b = ready(("z", c), NT)
                act.activation(zs[:, c, :], b, ACT.Silu).then_inc(act_freed, 1)
            act.wait_ge(out_done, 48)
            for tt, (c0, n) in enumerate(TOK):
                act.wait_ge(ld_done, tt + 1)
                act.activation(dec[0:n, :], dec[0:n, :], ACT.Exp).then_inc(dec_done, 1)
                if tt == 1:
                    act.activation(cdec[:, :], last_dec[:, :], ACT.Exp).then_inc(dec_done, 1)
                elif tt == 2:
                    act.activation(ea[0:n, :], acs[0:n, :], ACT.Exp).then_inc(dec_done, 1)
                b = ready(("bt", tt), rows=n)
                act.activation(bt[0:n, :], b, ACT.Copy).then_inc(act_freed, 1)
                for hb in range(8):
                    k = tt * 8 + hb
                    if tt == 1:
                        b = ready(("ab", tt, hb))
                        if hb:
                            act.wait_ge(ce_done, hb)
                        act.activation(eb[:, :], b, ACT.Exp).then_inc(eb_done, 1)
                    act.wait_ge(diff_done, k + 1)
                    act.activation(diff[0:n, k % 2, 0:4 * n], diff[0:n, k % 2, 0:4 * n], ACT.Exp) \
                        .then_inc(ex_done, 1)
                if tt == 0:
                    for g in range(GROUPS):
                        b = ready(("state", 0, g))
                        act.activation(s_a[:, g * 512:(g + 1) * 512], b, ACT.Copy).then_inc(act_freed, 1)
            b = ready("s decay", NB * HEADS)
            act.activation(sdec[:, :], b, ACT.Exp).then_inc(act_freed, 1)
            b = ready("expand")
            act.activation(ef[:, :, :], b.rearrange("p (i s) -> p i s", i=KI), ACT.Copy).then_inc(act_freed, 1)
            hi_upto(AHEAD[KEY["gn", 0]])
            act.wait_ge(yz_done, 1)
            act.activation(ysq[:, :, :], y[:, :, :], ACT.Square).then_inc(ysq_done, 1)
            for g in range(GROUPS):
                b = ready(("gn", g), NT)
                act.activation(grt[:, g, :], b, ACT.Sqrt, bias=eps[:, 0:1], scale=GROUPS / DI) \
                    .then_inc(act_freed, 1)
            act.wait_ge(y_done, 2)
            act.activation(y_hi[:, :, :], y[:, :, :], ACT.Copy).then_inc(yh_done, 1)
            for j in range(KD):
                hi_upto(AHEAD[KEY["ssd out", j]])
            attention(1)
            hi_upto(NSPLIT)
            norm(5)
            act.wait_ge(xp_done, 1)
            act.activation(v12[:, 3, :], v12[:, 2, :], ACT.Exp).then_inc(xpe_done, 1)

            def experts(c):
                s = PASSES[c]
                def hi(e, p):
                    slot = (NSTAT + p) % RAW
                    first = 16 * ((NSTAT + p) // RAW) if c == 0 else 16 * (p // RAW)
                    act.wait_ge(s.landed[slot], e * (16 * CPE // RAW) + first + 16)
                    act.wait_ge(s.used, e * CPE + p + 1)
                    act.activation(w_hi[:, (NSPLIT + p) % HL, :], raw[:, slot, :], ACT.Copy) \
                        .then_inc(s.hi, 1)

                nv = VIRTUAL[c][1]
                act.wait_ge(s.gather, 1)
                act.activation(xe_hi[:, :], ps[:, 0:2, :], ACT.Copy).then_inc(s.xh, 1)
                with act.Fori(0, nv) as e:
                    done = 0

                    def ahead(n):
                        nonlocal done
                        while done < min(n, CPE):
                            hi(e, done)
                            done += 1

                    ahead(HL - 1)
                    act.wait_ge(s.used, e * CPE + HL)
                    act.activation(ye[:, :], ps[:, 5:7, :], ACT.Copy).then_inc(s.ye, 1)
                    for f in range(FB):
                        ahead(8 * f + 4 + HL - 1)
                        act.wait_ge(s.used, e * CPE + 8 * f + 4 + HL)
                        act.wait_ge(s.g, e * FB + f + 1)
                        act.activation(sil[:, f % 2, :], ps[:, f % 2, :], ACT.Silu).then_inc(s.silu, 1)
                        if f >= 1:
                            ahead(8 * f + 4 + HL)
                            act.wait_ge(s.turn, e * FB + f)
                            act.activation(gt_hi[:, 4 * f - 4:4 * f, :], ps[:, 4, :], ACT.Copy) \
                                .then_inc(s.gh, 1)
                    ahead(8 * FB + 2 + HL - 1)
                    act.wait_ge(s.turn, e * FB + FB)
                    act.activation(gt_hi[:, 4 * FB - 4:4 * FB, :], ps[:, 4, :], ACT.Copy).then_inc(s.gh, 1)
                    ahead(8 * FB + 16 + HL - 1)
                    act.wait_ge(s.gather, e + 2)
                    act.activation(xe_hi[:, :], ps[:, 0:2, :], ACT.Copy).then_inc(s.xh, 1)
                    ahead(CPE)
                act.wait_ge(s.used, nv * CPE + HL)
                act.activation(ye[:, :], ps[:, 5:7, :], ACT.Copy).then_inc(s.ye, 1)

            experts(0)
            over = overflow(act)
            with act.If(over > P):
                experts(1)
                act.nop()
            act.wait_ge(resid, 1)
            act.activation(h[:, :, :], x[:, :, :], ACT.Square).then_inc(sq_done, 1)
            act.wait_ge(full, len(PLAN) + 1)
            act.activation(rt[:, :], ps[:, 0, 0:NT], ACT.Sqrt, bias=eps[:, 0:1], scale=1.0 / D) \
                .then_inc(rt_done, 1)
            act.wait_ge(fin_done, 1)
            act.dma_start(t["out_x"], h[:, :, :]).then_inc(x_out, 16)
            act.wait_ge(x_out, 16)

        @block.vector
        def _(dve):
            ptr, steps = [0], [0]

            def lo_upto(n):
                while ptr[0] < min(n, NSPLIT):
                    k = ptr[0]
                    dve.wait_ge(hi_done, k + 1)
                    dve.tensor_tensor(w_lo[:, k % HL, :], raw[:, SPLIT_AT[k] % RAW, :],
                                      w_hi[:, k % HL, :].bitcast(F32), ALU.subtract).then_inc(lo_done, 1)
                    ptr[0] += 1

            def ready(key, n=512, rows=P):
                g = KEY[key]
                lo_upto(AHEAD[g])
                dve.wait_ge(full, g + 1)
                return bank(g, n, rows)

            def act_read(key):
                lo_upto(AHEAD[KEY[key]])
                dve.wait_ge(act_freed, FREED[KEY[key]][1])

            def link(ins):
                steps[0] += 1
                ins.then_inc(chain, 1)
                dve.wait_ge(chain, steps[0])

            def lo_half(dst, src, hi, done):
                dve.tensor_tensor(dst, src, hi.bitcast(F32), ALU.subtract).then_inc(done, 1)

            def norm(i, gain):
                act_read(("norm", i))
                link(dve.reciprocal(rs[:, :], rt[:, :]))
                for k in range(KD):
                    a = dve.scalar_tensor_tensor(h[:, k, :], x[:, k, :], gain[:, k:k + 1], rs[:, :],
                                                 ALU.mult, ALU.mult)
                a.then_inc(h_done, 1)
                dve.wait_ge(hh_done, i + 1)
                lo_half(h_lo[:, :, :], h[:, :, :], h_hi[:, :, :], hl_done)

            def add_residual(key, j):
                b = ready(key, NT)
                dve.tensor_tensor(x[:, j, :], x[:, j, :], b, ALU.add).then_inc(dve_freed, 1)

            def softplus(z, n, turn):
                dve.scalar_tensor_tensor(sp[:, 0, 0:n], z, -1.0, z, ALU.mult, ALU.max).then_inc(sp_abs, 1)
                dve.wait_ge(sp_exp, turn)
                dve.tensor_scalar(sp[:, 2, 0:n], sp[:, 1, 0:n], 1.0, None, ALU.add).then_inc(sp_sum, 1)
                dve.wait_ge(sp_sum, turn)
                link(dve.tensor_scalar(sp[:, 4, 0:n], sp[:, 2, 0:n], -1.0, None, ALU.add))
                link(dve.tensor_scalar(sp[:, 5, 0:n], sp[:, 4, 0:n], 0.0, None, ALU.is_equal))
                link(dve.tensor_tensor(sp[:, 4, 0:n], sp[:, 4, 0:n], sp[:, 5, 0:n], ALU.add))
                link(dve.reciprocal(sp[:, 4, 0:n], sp[:, 4, 0:n]))
                dve.wait_ge(sp_ln, turn)
                link(dve.tensor_tensor(sp[:, 5, 0:n], sp[:, 3, 0:n], sp[:, 5, 0:n], ALU.add))
                link(dve.tensor_tensor(sp[:, 5, 0:n], sp[:, 5, 0:n], sp[:, 4, 0:n], ALU.mult))
                link(dve.tensor_tensor(sp[:, 5, 0:n], sp[:, 5, 0:n], sp[:, 1, 0:n], ALU.mult))
                link(dve.scalar_tensor_tensor(z, z, 0.0, sp[:, 5, 0:n], ALU.max, ALU.add))

            def conv_tile(out, src, tmp, w, b, done):
                n = PADW - CW + 1
                link(dve.tensor_scalar(tmp[:, 0:n], src[:, 0:n], w[:, 0:1], b, ALU.mult, ALU.add))
                for k in range(1, CW - 1):
                    link(dve.scalar_tensor_tensor(tmp[:, 0:n], src[:, k:k + n], w[:, k:k + 1], tmp[:, 0:n],
                                                  ALU.mult, ALU.add))
                k = CW - 1
                dve.scalar_tensor_tensor(out[:, 0:SEQ], src[:, k:k + SEQ], w[:, k:k + 1], tmp[:, 0:SEQ],
                                         ALU.mult, ALU.add)
                dve.scalar_tensor_tensor(out[:, SEQ:NT].rearrange("p (b w) -> p b w", w=TS),
                                         samples(src[:, PS0:PADW], TS + CW - 1, k, TS), w[:, k:k + 1],
                                         samples(tmp[:, PS0:PADW], TS + CW - 1, 0, TS),
                                         ALU.mult, ALU.add).then_inc(done, 1)

            dve.wait_ge(small_in, 16)
            act_read("mem norm")
            link(dve.reciprocal(rs[:, 0:NMEM], rt[:, 0:NMEM]))
            for l in range(2):
                if l == 1:
                    dve.wait_ge(mh_done, 1)
                gain = par("g_memkv")[:, l * KD:(l + 1) * KD]
                for k in range(KD):
                    a = dve.scalar_tensor_tensor(memg[:, k, :], memx[:, k, :], gain[:, k:k + 1],
                                                 rs[:, 0:NMEM], ALU.mult, ALU.mult)
                a.then_inc(mg_done, 1)
                dve.wait_ge(mh_done, l + 1)
                lo_half(mem_lo[:, :, :], memg[:, :, :], mem_hi[:, :, :], ml_done)
                for nb in range(2):
                    for m in range(2):
                        b = ready(("v", l, nb, m))
                        dve.tensor_copy(vmem[l][:, m, nb * 512:(nb + 1) * 512], b).then_inc(dve_freed, 1)
            link(dve.tensor_scalar(nc8[:, :], par("lam"), -1.0, None, ALU.mult))
            softplus(nc8[:, :], KD, 1)
            dve.tensor_scalar(nc8[:, :], nc8[:, :], -8.0, None, ALU.mult).then_inc(c8_done, 1)

            norm(0, par("g_mix")[:, 0:KD])
            for j in range(KD):
                act_read(("xb", j))
                conv_tile(xc[:, j, :], conv[:, j, :], conv_t[:, j % 2, :],
                          par("lru_cw")[:, 4 * j:4 * j + 4], par("lru_cb")[:, j:j + 1], xc_done)
                dve.wait_ge(xch_done, j + 1)
                lo_half(xc_lo[:, j, :], xc[:, j, :], xc_hi[:, j, :], xcl_done)
            act_read(("i", KD - 1))
            dve.wait_ge(e2_done, 1)
            dve.scalar_tensor_tensor(expm[:, :, :], expm[:, :, :], 1.0, tanh[:, :, :], ALU.add, ALU.mult) \
                .then_inc(q_done, 1)
            link(dve.tensor_tensor(xc[:, :, :], xc[:, :, :], ig[:, :, :], ALU.mult))
            dve.wait_ge(root_done, 1)
            link(dve.tensor_tensor(xc[:, :, :], xc[:, :, :], expm[:, :, :], ALU.mult))
            for j in range(KD):
                dve.tensor_tensor_scan(hs[:, j, 0:SEQ], decay[:, j, 0:SEQ], xc[:, j, 0:SEQ], 0.0,
                                       ALU.mult, ALU.add)

            def tok(buf, k):
                return buf[:, :, SEQ:NT].rearrange("p j (b w) -> p j b w", w=TS)[:, :, :, k]

            before = par("h_prev").rearrange("p (j b) -> p j b", b=NB)
            for k in range(TS):
                link(dve.tensor_tensor(hs_t[:, :, :], tok(decay, k), before, ALU.mult))
                a = dve.tensor_tensor(tok(hs, k), hs_t[:, :, :], tok(xc, k), ALU.add)
                if k < TS - 1:
                    link(a)
                else:
                    a.then_inc(hs_done, 1)
                before = tok(hs, k)
            dve.wait_ge(hs_done, 1)
            dve.tensor_tensor(tanh[:, :, :], hs[:, :, :], gate[:, :, :], ALU.mult).then_inc(y_done, 1)
            dve.wait_ge(yh_done, 1)
            lo_half(xc_lo[:, :, :], tanh[:, :, :], xc_hi[:, :, :], yl_done)
            for j in range(KD):
                add_residual(("lru out", j), j)

            def attention(l):
                norm(3 * l + 1, par("g_mem")[:, l * KD:(l + 1) * KD])
                for hd in range(MH):
                    b = ready(("scores", l, hd))
                    link(dve.tensor_reduce(mx[:, 2 * hd:2 * hd + 2],
                                           b.rearrange("p (a m) -> p a m", a=2), AX.X, ALU.max))
                    dve.tensor_scalar(nmx[:, 2 * hd:2 * hd + 2], mx[:, 2 * hd:2 * hd + 2], -1.0 / 16, None,
                                      ALU.mult).then_inc(max_done, 1)
                act_read(("scores", l, MH - 1))
                link(dve.reciprocal(rinv[:, 0:8], rsum[:, 0:8]))
                dve.tensor_tensor(pr[:, 0:8, :], pr[:, 0:8, :],
                                  rinv[:, 0:8].unsqueeze(2).broadcast_to([P, 8, NMEM]), ALU.mult) \
                    .then_inc(pn_done, 1)
                b = ready(("s turn", l), NMEM)
                link(dve.tensor_reduce(mx[:, 8:9], b, AX.X, ALU.max))
                dve.tensor_scalar(nmx[:, 8:9], mx[:, 8:9], -1.0 / 16, None, ALU.mult).then_inc(max_done, 1)
                act_read(("s turn", l))
                link(dve.reciprocal(rinv[:, 8:9], rsum[:, 8:9]))
                dve.tensor_scalar(pr[:, 8, :], pr[:, 8, :], rinv[:, 8:9], None, ALU.mult).then_inc(pn_done, 1)
                for i in range(4):
                    b = ready(("probs", l, i))
                    dve.tensor_copy(prt[:, i // 2, 2 * (i % 2):2 * (i % 2) + 2, :], b).then_inc(dve_freed, 1)
                b = ready(("s probs", l), NMEM)
                dve.tensor_copy(sprt[:, :, :], b).then_inc(dve_freed, 1)
                dve.wait_ge(yh_done, 2 + 2 * l)
                lo_half(att_lo[:, :, :], att[:, :, :], att_hi[:, :, :], yl_done)
                for j in range(KD):
                    add_residual(("mem out", l, j), j)

            attention(0)

            norm(2, par("g_ffn")[:, 0:KD])
            for f in range(KF):
                act_read(("f1", f))
                b = ready(("f3", f), NT)
                if f >= 2:
                    dve.wait_ge(fh_done, f - 1)
                dve.tensor_tensor(f_g[:, f % 2, :], f_s[:, f % 2, :], b, ALU.mult).then_inc(dve_freed, 1)
                dve.wait_ge(fh_done, f + 1)
                lo_half(f_lo[:, f, :], f_g[:, f % 2, :], f_hi[:, f, :], fl_done)
            for j in range(KD):
                add_residual(("f2", j), j)

            norm(3, par("g_mix")[:, KD:2 * KD])
            b = ready("dt", 96)
            link(dve.memset(dt[:, :, :], 0.0))
            dtb = par("dt_b")
            dve.tensor_tensor(dt[:, 0:2, :], b[:, 0:64].rearrange("p (a m) -> p a m", a=2),
                              dtb.unsqueeze(1).broadcast_to([P, 2, HEADS]), ALU.add)
            link(dve.tensor_tensor(dt[0:32, 2, :], b[0:32, 64:96], dtb[0:32, :], ALU.add))
            dve.engine_nop().then_inc(dve_freed, 1)
            softplus(dt[:, :, :].rearrange("p a m -> p (a m)"), 96, 2)
            dve.wait_ge(alog_exp, 1)
            for k in range(3):
                a = dve.scalar_tensor_tensor(adt[:, k, :], dt[:, k, :], -1.0, last_dec[:, :],
                                             ALU.mult, ALU.mult)
            a.then_inc(adt_done, 1)
            for c in range(NXBC):
                act_read(("xbc", c))
                if c >= 2:
                    dve.wait_ge(silu_done, c - 1)
                if c:
                    dve.wait_ge(cvo_done, c)
                conv_tile(cv_o[:, c % 2, :], cv[:, c % 3, :], cv_t[:, :],
                          par("ssd_cw")[:, 4 * c:4 * c + 4], par("ssd_cb")[:, c:c + 1], cvo_done)
            act_read(("z", KI - 1))
            dve.wait_ge(out_done, 48)
            for tt, (c0, n) in enumerate(TOK):
                b = ready(("acs", tt), HEADS, n)
                if tt:
                    dve.wait_ge(xd_done, tt)
                dve.tensor_copy(acs[0:n, :], b).then_inc(dve_freed, 1)
                b = ready(("last", tt), HEADS, n)
                dve.tensor_copy(last_dec[0:n, :], b)
                dve.tensor_tensor(dec[0:n, :], b, acs[0:n, :], ALU.subtract).then_inc(ld_done, 1)
                dve.engine_nop().then_inc(dve_freed, 1)
                for i in range(4):
                    b = ready(("xt", tt, i), rows=n)
                    dve.tensor_tensor(xt[0:n, i * 512:(i + 1) * 512].rearrange("p (h f) -> p h f", f=64),
                                      b.rearrange("p (h f) -> p h f", f=64),
                                      dt[0:n, tt, 8 * i:8 * i + 8].unsqueeze(2).broadcast_to([n, 8, 64]),
                                      ALU.mult).then_inc(xt_done, 1)
                    dve.engine_nop().then_inc(dve_freed, 1)
                b = ready(("cb", tt), 4 * n, n)
                mask = tri[0:n, 0:n] if tt < 2 else par("tri_s")[0:n, :]
                dve.tensor_tensor(cbm[0:n, 0:4 * n].rearrange("p (g l) -> p g l", g=4),
                                  b.rearrange("p (g l) -> p g l", g=4),
                                  mask.unsqueeze(1).broadcast_to([n, 4, n]), ALU.mult).then_inc(cbm_done, 1)
                dve.engine_nop().then_inc(dve_freed, 1)

                def exponents(hb):
                    k = tt * 8 + hb
                    b = ready(("ab", tt, hb), 4 * n, P)
                    if tt == 1:
                        dve.wait_ge(eb_done, hb + 1)
                    for j in range(4):
                        a = dve.tensor_scalar(diff[0:n, k % 2, j * n:(j + 1) * n], b[0:n, j * n:(j + 1) * n],
                                              acs[0:n, 4 * hb + j:4 * hb + j + 1], 0.0, ALU.subtract, ALU.min)
                    a.then_inc(diff_done, 1)
                    dve.engine_nop().then_inc(dve_freed, 1)

                def mix(hb):
                    k = tt * 8 + hb
                    g = hb // 2
                    dve.wait_ge(ex_done, k + 1)
                    dve.wait_ge(cbm_done, tt + 1)
                    dve.tensor_tensor(mt[0:n, k % 2, 0:4 * n].rearrange("p (h l) -> p h l", h=4),
                                      diff[0:n, k % 2, 0:4 * n].rearrange("p (h l) -> p h l", h=4),
                                      cbm[0:n, g * n:(g + 1) * n].unsqueeze(1).broadcast_to([n, 4, n]),
                                      ALU.mult).then_inc(mt_done, 1)
                    if tt == 1:
                        if hb:
                            dve.wait_ge(full, KEY["y", 1, hb - 1] + 1)
                        dve.tensor_tensor(ce[:, :].rearrange("p (h l) -> p h l", h=4),
                                          eb[:, :].rearrange("p (h l) -> p h l", h=4),
                                          bc[:, 4 + g, c0:c0 + n].unsqueeze(1).broadcast_to([P, 4, n]),
                                          ALU.mult).then_inc(ce_done, 1)

                def outputs(hb):
                    b = ready(("y", tt, hb), 2 * n)
                    for j in range(2):
                        i = 2 * hb + j
                        a = dve.scalar_tensor_tensor(y[:, i, c0:c0 + n], y[:, i, c0:c0 + n],
                                                     par("ssd_d")[:, i:i + 1], b[:, j * n:(j + 1) * n],
                                                     ALU.mult, ALU.add)
                    a.then_inc(dve_freed, 1)

                exponents(0)
                for hb in range(8):
                    mix(hb)
                    if hb + 1 < 8:
                        exponents(hb + 1)
                    outputs(hb)
                if tt == 1:
                    dve.wait_ge(sad_done, 1)
                    for g in range(GROUPS):
                        b = ready(("state", 1, g))
                        dve.tensor_tensor(s_b[:, g * 512:(g + 1) * 512], s_a[:, g * 512:(g + 1) * 512], b,
                                          ALU.add).then_inc(sb_done, 1)
                        dve.engine_nop().then_inc(dve_freed, 1)
            for bq in range(NB):
                a = dve.tensor_scalar(sdr[0:32, bq * HEADS:(bq + 1) * HEADS], acs[0:32, :],
                                      par("is_last")[0:32, bq:bq + 1], None, ALU.mult)
            a.then_inc(sdr_done, 1)
            act_read("expand")
            for bq in range(NB):
                if bq >= 2:
                    dve.wait_ge(full, KEY["s state", bq - 2, GROUPS - 1] + 1)
                dve.tensor_scalar(btm[0:32, bq % 2, :], bt[0:32, :], par("in_seq")[0:32, bq:bq + 1], None,
                                  ALU.mult).then_inc(btm_done, 1)
                b = ready(("y off", bq), 64)
                at_b = (slice(None), slice(None), slice(SEQ + bq * TS, SEQ + (bq + 1) * TS))
                yo = yo_t[:, bq % 2, :].rearrange("p (i w) -> p i w", w=TS)
                link(dve.tensor_tensor(yo, b.rearrange("p (i w) -> p i w", w=TS),
                                       ef[:, :, bq * TS:(bq + 1) * TS], ALU.mult))
                dve.tensor_tensor(y[at_b], y[at_b], yo, ALU.add).then_inc(dve_freed, 1)
                for g in range(GROUPS):
                    b = ready(("s state", bq, g))
                    dve.wait_ge(sn_dec, 2 * bq + g // 2 + 1)
                    dst = s_new[:, g // 2, (g % 2) * 512:(g % 2 + 1) * 512]
                    dve.tensor_tensor(dst, dst, b, ALU.add).then_inc(sn_done, 1)
                    dve.engine_nop().then_inc(dve_freed, 1)
            dve.wait_ge(dve_freed, FREED[KEY["y off", NB - 1]][1])
            dve.tensor_tensor(y[:, :, :], y[:, :, :], zs[:, :, :], ALU.mult).then_inc(yz_done, 1)
            for g in range(GROUPS):
                act_read(("gn", g))
                link(dve.reciprocal(grs[:, g, :], grt[:, g, :]))
                for i in range(4 * g, 4 * g + 4):
                    a = dve.scalar_tensor_tensor(y[:, i, :], y[:, i, :], par("ssd_g")[:, i:i + 1],
                                                 grs[:, g, :], ALU.mult, ALU.mult)
            a.then_inc(y_done, 1)
            dve.wait_ge(yh_done, 3)
            lo_half(y_lo[:, :, :], y[:, :, :], y_hi[:, :, :], yl_done)
            for j in range(KD):
                add_residual(("ssd out", j), j)
            attention(1)

            norm(5, par("g_ffn")[:, KD:2 * KD])
            b = ready("logits", 24)
            link(dve.memset(lg[:, :, :], 0.0))
            dve.tensor_copy(lg[:, 0:2, :], b[:, 0:16].rearrange("p (a m) -> p a m", a=2))
            link(dve.tensor_copy(lg[0:32, 2, :], b[0:32, 16:24]))
            dve.engine_nop().then_inc(dve_freed, 1)
            wide = [P, 3, NE, NE]
            mine, other = lg[:, :, :].unsqueeze(3).broadcast_to(wide), lg[:, :, :].unsqueeze(2).broadcast_to(wide)
            lower = par("lower").rearrange("p (e j) -> p e j", e=NE).unsqueeze(1).broadcast_to(wide)
            dve.tensor_tensor(cmp1[:, :, :, :], other, mine, ALU.is_gt)
            link(dve.tensor_tensor(cmp2[:, :, :, :], other, mine, ALU.is_equal))
            link(dve.tensor_tensor(cmp2[:, :, :, :], cmp2[:, :, :, :], lower, ALU.mult))
            link(dve.tensor_tensor(cmp1[:, :, :, :], cmp1[:, :, :, :], cmp2[:, :, :, :], ALU.add))
            link(dve.tensor_reduce(rank[:, :, :], cmp1[:, :, :, :], AX.X, ALU.add))
            dve.memset(msk[:, :, :], 0.0)
            dve.memset(gts[:, :, :], 0.0)
            dve.memset(pos[:, :, :], 0.0)
            dve.tensor_scalar(m1[:, :, :], rank[:, :, :], 0.0, None, ALU.is_equal)
            link(dve.tensor_scalar(m2[:, :, :], rank[:, :, :], 1.0, None, ALU.is_equal))
            dve.tensor_tensor(msk[:, :, 0:NE], m1[:, :, :], m2[:, :, :], ALU.add).then_inc(msk_done, 1)
            dve.wait_ge(msk_done, 1)
            dve.tensor_tensor(cmp1[:, :, 0, :], m1[:, :, :], lg[:, :, :], ALU.mult)
            link(dve.tensor_tensor(cmp1[:, :, 1, :], m2[:, :, :], lg[:, :, :], ALU.mult))
            dve.tensor_reduce(v12[:, 0, :], cmp1[:, :, 0, :], AX.X, ALU.add)
            link(dve.tensor_reduce(v12[:, 1, :], cmp1[:, :, 1, :], AX.X, ALU.add))
            dve.tensor_tensor(v12[:, 2, :], v12[:, 1, :], v12[:, 0, :], ALU.subtract).then_inc(xp_done, 1)
            dve.wait_ge(xpe_done, 1)
            link(dve.tensor_scalar(v12[:, 0, :], v12[:, 3, :], 1.0, None, ALU.add))
            link(dve.reciprocal(v12[:, 0, :], v12[:, 0, :]))
            link(dve.tensor_tensor(m2[:, :, :], m2[:, :, :],
                                   v12[:, 3, :].unsqueeze(2).broadcast_to([P, 3, NE]), ALU.mult))
            link(dve.tensor_tensor(m1[:, :, :], m1[:, :, :], m2[:, :, :], ALU.add))
            link(dve.tensor_tensor(gts[:, :, 0:NE], m1[:, :, :],
                                   v12[:, 0, :].unsqueeze(2).broadcast_to([P, 3, NE]), ALU.mult))
            for c in range(1, 3):
                vs = slice(c * NE, (c + 1) * NE)
                dve.tensor_copy(gts[:, :, vs], gts[:, :, 0:NE])
                dve.tensor_copy(msk[:, :, vs], msk[:, :, 0:NE])
            b = ready("pos", 4 * NE)
            for c in range(3):
                vs = slice(c * NE, (c + 1) * NE)
                dve.tensor_scalar(pos[:, 0:2, vs], b[:, 0:2 * NE].rearrange("p (a m) -> p a m", a=2),
                                  float(-c * P), None, ALU.add)
                dve.tensor_scalar(pos[0:32, 2, vs], b[0:32, 2 * NE:3 * NE], float(-c * P), None, ALU.add)
            link(dve.tensor_reduce(cmax[:, :], b[:, 3 * NE:4 * NE], AX.X, ALU.max))
            dve.tensor_copy(cmax_i[:, :], cmax[:, :]).then_inc(cnt_done, 1)
            dve.engine_nop().then_inc(dve_freed, 1)
            for i in range(6):
                rows = TOK[i // 2][1]
                b = ready(("ht", i), rows=rows)
                dve.tensor_copy(htok[0:rows, i // 2, (i % 2) * 512:(i % 2 + 1) * 512], b).then_inc(dve_freed, 1)

            def experts(c):
                s = PASSES[c]
                links = [0]

                def select(e):
                    for m, (_, n) in enumerate(TOK):
                        for dst, val in ((sel, msk), (selg, gts)):
                            a = dve.tensor_scalar(dst[0:n, m, :], par("iota")[0:n, :],
                                                  pos[0:n, m, bass.ds(e, 1)], val[0:n, m, bass.ds(e, 1)],
                                                  ALU.is_equal, ALU.mult)
                    a.then_inc(s.sel, 1)

                def lo(e, p):
                    dve.wait_ge(s.hi, e * CPE + p + 1)
                    dve.tensor_tensor(w_lo[:, (NSPLIT + p) % HL, :], raw[:, (NSTAT + p) % RAW, :],
                                      w_hi[:, (NSPLIT + p) % HL, :].bitcast(F32), ALU.subtract) \
                        .then_inc(s.lo, 1)

                def add_back(e, j):
                    dve.wait_ge(s.scat, e * KD + j + 1)
                    dve.tensor_tensor(x[:, j, :], x[:, j, :], ps[:, 5 + j % 3, 0:NT], ALU.add) \
                        .then_inc(s.add, 1)

                dve.memset(sg[:, :], 0.0).then_inc(s.sg, 1)
                v0, nv = VIRTUAL[c]
                dve.engine_nop().then_inc(s.lo, RAW)
                dve.engine_nop().then_inc(s.g, 2)
                dve.engine_nop().then_inc(s.gl, 1)
                dve.engine_nop().then_inc(s.add, 3)
                select(v0)
                dve.wait_ge(s.xh, 1)
                lo_half(xe_lo[:, :], ps[:, 0:2, :], xe_hi[:, :], s.xl)
                with dve.Fori(0, nv) as e:
                    done = 0

                    def ahead(n):
                        nonlocal done
                        while done < min(n, CPE):
                            lo(e, done)
                            done += 1

                    def turned(f):
                        dve.wait_ge(s.gh, e * FB + f + 1)
                        lo_half(gt_lo[:, 4 * f:4 * f + 4, :], ps[:, 4, :].rearrange("p (a m) -> p a m", a=4),
                                gt_hi[:, 4 * f:4 * f + 4, :], s.gl)

                    for f in range(FB):
                        if f >= 1:
                            ahead(8 * f + 4 + HL - 1)
                            turned(f - 1)
                        ahead(8 * f + 8 + HL - 1)
                        dve.wait_ge(s.used, e * CPE + 8 * f + 8 + HL)
                        dve.wait_ge(s.silu, e * FB + f + 1)
                        dve.tensor_tensor(ge[:, f % 2, :], sil[:, f % 2, :], ps[:, 2 + f % 2, :], ALU.mult) \
                            .then_inc(s.g, 1)
                        if f == 0:
                            for j in range(KD):
                                add_back(e, j)
                    ahead(8 * FB + 2 + HL - 1)
                    turned(FB - 1)
                    ahead(8 * FB + 4 + HL - 1)
                    dve.wait_ge(s.sgt, e + 1)
                    dve.tensor_copy(sg[:, :], ps[:, 2, 0:NT]).then_inc(s.sg, 1)
                    select(e + v0 + 1)
                    ahead(8 * FB + 16 + HL - 1)
                    dve.wait_ge(s.xh, e + 2)
                    lo_half(xe_lo[:, :], ps[:, 0:2, :], xe_hi[:, :], s.xl)
                    ahead(CPE)
                for j in range(KD):
                    add_back(nv, j)

            experts(0)
            over = overflow(dve)
            with dve.If(over > P):
                experts(1)
                dve.nop()
            dve.engine_nop().then_inc(resid, 1)
            dve.wait_ge(rt_done, 1)
            link(dve.reciprocal(rs[:, :], rt[:, :]))
            for k in range(KD):
                a = dve.scalar_tensor_tensor(h[:, k, :], x[:, k, :], par("g_fin")[:, k:k + 1], rs[:, :],
                                             ALU.mult, ALU.mult)
            a.then_inc(fin_done, 1)

        @block.tensor
        def _(pe):
            opened, used = [0], [0]

            def open_group(key, n=512, rows=P):
                g = KEY[key]
                assert g == opened[0], (key, g, opened[0])
                opened[0] += 1
                if g >= 8:
                    eng, v = FREED[g - 8]
                    pe.wait_ge(act_freed if eng == "act" else dve_freed, v)
                return bank(g, n, rows)

            def close(ins):
                ins.then_inc(full, 1)

            def weights(k):
                if k >= used[0]:
                    pe.wait_ge(lo_done, k + 1)
                    used[0] = k + 1
                return w_hi[:, k % HL, :], w_lo[:, k % HL, :]

            def mm3(out, l_hi, l_lo, r_hi, r_lo, start, stop):
                pe.matmul(out, l_hi, r_hi, start=start, stop=False)
                pe.matmul(out, l_hi, r_lo, start=False, stop=False)
                return pe.matmul(out, l_lo, r_hi, start=False, stop=stop)

            def product(key, tiles, a_hi, a_lo, n=NT):
                out = open_group(key, n)
                for m, (k, tl, ka) in enumerate(tiles):
                    hi, lo = weights(k)
                    a = mm3(out, hi[:, tl * P:(tl + 1) * P], lo[:, tl * P:(tl + 1) * P],
                            a_hi[:, ka, :], a_lo[:, ka, :], m == 0, m == len(tiles) - 1)
                close(a)

            def square(key, a_hi, a_lo, n=NT):
                k = NEED[KEY[key]] - 1
                product(key, [(k, tl, tl) for tl in range(KD)], a_hi, a_lo, n)

            RAW_AT = [i for i, k in enumerate(ORDER) if k != "w"]
            raw_at = [0]

            def plain():
                i = RAW_AT[raw_at[0]]
                raw_at[0] += 1
                pe.wait_ge(landed[i % RAW], 16 * (i // RAW + 1))
                return raw[:, i % RAW, :]

            def norm(i):
                out = open_group(("norm", i), NT)
                pe.wait_ge(sq_done, i + 2)
                for k in range(KD):
                    a = pe.matmul(out, ones, h[:, k, :], start=(k == 0), stop=(k == KD - 1))
                close(a)

            pe.wait_ge(small_in, 16)
            out = open_group("mem norm", NMEM)
            pe.wait_ge(sq_done, 1)
            for k in range(KD):
                a = pe.matmul(out, ones, memsq[:, k, :], start=(k == 0), stop=(k == KD - 1))
            close(a)
            for l in range(2):
                pe.wait_ge(ml_done, l + 1)
                for j in range(KD):
                    square(("k", l, j), mem_hi, mem_lo, NMEM)
                for nb in range(2):
                    outs = [open_group(("v", l, nb, m)) for m in range(2)]
                    for c in range(4):
                        hi, lo = weights(NEED[KEY["v", l, nb, 1]] - 4 + c)
                        for kk in range(2):
                            w = slice(kk * 512, (kk + 1) * 512)
                            ka = 2 * c + kk
                            for m in range(2):
                                a = mm3(outs[m], mem_hi[:, ka, m * P:(m + 1) * P], mem_lo[:, ka, m * P:(m + 1) * P],
                                        hi[:, w], lo[:, w], ka == 0, ka == KD - 1)
                                if ka == KD - 1:
                                    close(a)
            norm(0)
            pe.wait_ge(hl_done, 1)
            for j in range(KD):
                square(("gate", j), h_hi, h_lo)
            for j in range(KD):
                square(("xb", j), h_hi, h_lo)
            for kind in ("r", "i"):
                k = NEED[KEY[kind, 0]] - 1
                for j in range(KD):
                    pe.wait_ge(xcl_done, j + 1)
                    product((kind, j), [(k, j, j)], xc_hi, xc_lo)
            pe.wait_ge(yl_done, 1)
            for j in range(KD):
                square(("lru out", j), xc_hi, xc_lo)

            def attention(l):
                norm(3 * l + 1)
                pe.wait_ge(hl_done, 3 * l + 2)
                for j in range(KD):
                    square(("q", l, j), h_hi, h_lo)
                pe.wait_ge(act_freed, FREED[KEY["q", l, KD - 1]][1])
                pe.wait_ge(kv_in, 32 * (l + 1))
                for hd in range(MH):
                    out = open_group(("scores", l, hd))
                    for tt in range(2):
                        for dd in range(2):
                            j = 2 * hd + dd
                            a = pe.matmul(out[:, tt * NMEM:(tt + 1) * NMEM], q[:, j, tt * P:(tt + 1) * P],
                                          kt[:, j, :], start=(dd == 0), stop=(dd == 1))
                    close(a)
                out = open_group(("s scores", l), NMEM)
                for b in range(NB):
                    for half in range(2):
                        keys = plain()
                        for hh in range(2):
                            for m in range(2):
                                col = m * P + b * 16 + (2 * half + hh) * TS
                                for dd in range(2):
                                    a = pe.matmul(out[:, col:col + TS],
                                                  keys[:, (2 * hh + dd) * NMEM + m * P:(2 * hh + dd) * NMEM + (m + 1) * P],
                                                  q[:, 4 * half + 2 * hh + dd, SEQ + b * TS:SEQ + (b + 1) * TS],
                                                  start=(dd == 0), stop=(dd == 1))
                        a.then_inc(raw_used, 1) if (b, half) != (NB - 1, 1) else close(a)
                out = open_group(("s turn", l), NMEM)
                pe.wait_ge(act_freed, FREED[KEY["s scores", l]][1])
                for m in range(2):
                    a = pe.transpose(out[:, m * P:(m + 1) * P], st[:, m, :], ident)
                close(a)
                pe.wait_ge(pn_done, 2 * l + 1)
                for i in range(4):
                    out = open_group(("probs", l, i))
                    m = i // 2
                    for hh in range(2):
                        for tt in range(2):
                            blk = 2 * (2 * (i % 2) + hh) + tt
                            col = hh * SEQ + tt * P
                            a = pe.transpose(out[:, col:col + P], pr[:, blk, m * P:(m + 1) * P], ident)
                    close(a)
                out = open_group(("s probs", l), NMEM)
                pe.wait_ge(pn_done, 2 * l + 2)
                for m in range(2):
                    a = pe.transpose(out[:, m * P:(m + 1) * P], pr[:, 8, m * P:(m + 1) * P], ident)
                close(a)
                pe.wait_ge(dve_freed, FREED[KEY["s probs", l]][1])
                for j in range(KD):
                    out = open_group(("o", l, j), SEQ)
                    for m in range(2):
                        a = pe.matmul(out, vt[:, m, j * P:(j + 1) * P], prt[:, m, j // 2, :],
                                      start=(m == 0), stop=(m == 1))
                    close(a)
                out = open_group(("s o", l), NMEM)
                for b in range(NB):
                    vals = [plain(), plain()]
                    for j in range(KD):
                        for m in range(2):
                            a = pe.matmul(out[:, j * 32 + b * TS:j * 32 + (b + 1) * TS],
                                          vals[m][:, j * P:(j + 1) * P],
                                          sprt[:, m, b * 16 + (j // 2) * TS:b * 16 + (j // 2 + 1) * TS],
                                          start=(m == 0), stop=(m == 1))
                            if j == KD - 1:
                                a.then_inc(raw_used, 1) if (b, m) != (NB - 1, 1) else close(a)
                pe.wait_ge(yl_done, 2 + 2 * l)
                for j in range(KD):
                    square(("mem out", l, j), att_hi, att_lo)

            attention(0)
            norm(2)
            pe.wait_ge(hl_done, 3)
            for f in range(KF):
                square(("f1", f), h_hi, h_lo)
                square(("f3", f), h_hi, h_lo)
            pe.wait_ge(fl_done, KF)
            first = NEED[KEY["f2", 0]] - -(-KF // 8)
            for j in range(KD):
                product(("f2", j), [(first + (j * KF + k) // 8, (j * KF + k) % 8, k) for k in range(KF)],
                        f_hi, f_lo)

            norm(3)
            pe.wait_ge(h_done, 4)
            out = open_group("dt", 96)
            w_dt = par("w_dt").rearrange("p (k m) -> p k m", k=KD)
            for m, (c0, n) in enumerate(TOK):
                for k in range(KD):
                    a = pe.matmul(out[0:n, 32 * m:32 * m + 32], h[:, k, c0:c0 + n], w_dt[:, k, :],
                                  start=(k == 0), stop=(k == KD - 1))
            close(a)
            pe.wait_ge(hl_done, 4)
            for c in range(NXBC):
                square(("xbc", c), h_hi, h_lo)
            for c in range(KI):
                square(("z", c), h_hi, h_lo)
            pe.wait_ge(adt_done, 1)
            pe.wait_ge(silu_done, NXBC)
            for tt, (c0, n) in enumerate(TOK):
                within = tri[0:n, 0:n] if tt < 2 else par("tri_s")[0:n, :]
                out = open_group(("acs", tt), HEADS, n)
                close(pe.matmul(out, within, adt[0:n, tt, :], start=True, stop=True))
                out = open_group(("last", tt), HEADS, n)
                pe.wait_ge(dve_freed, FREED[KEY["acs", tt]][1])
                close(pe.matmul(out, par("last")[0:n, 0:n] if tt < 2 else par("last_s")[0:n, :], acs[0:n, :],
                                start=True, stop=True))
                for i in range(4):
                    out = open_group(("xt", tt, i), rows=n)
                    for k in range(4):
                        a = pe.transpose(out[:, k * P:(k + 1) * P], y[:, 4 * i + k, c0:c0 + n], ident)
                    close(a)
                out = open_group(("bt", tt), rows=n)
                for g in range(GROUPS):
                    a = pe.transpose(out[:, g * P:(g + 1) * P], bc[:, g, c0:c0 + n], ident)
                close(a)
                out = open_group(("cb", tt), 4 * n, n)
                for g in range(GROUPS):
                    a = pe.matmul(out[:, g * n:(g + 1) * n], bc[:, g, c0:c0 + n], bc[:, 4 + g, c0:c0 + n],
                                  start=True, stop=True)
                close(a)

                def sums(hb):
                    out = open_group(("ab", tt, hb), 4 * n)
                    for j in range(4):
                        a = pe.matmul(out[:, j * n:(j + 1) * n],
                                      adt[0:n, tt, 4 * hb + j:4 * hb + j + 1].broadcast_to([n, P]), within,
                                      start=True, stop=True)
                    close(a)

                sums(0)
                for hb in range(8):
                    if hb < 7:
                        sums(hb + 1)
                    if hb == 0:
                        pe.wait_ge(dve_freed, FREED[KEY["xt", tt, 3]][1])
                    out = open_group(("y", tt, hb), 2 * n)
                    pe.wait_ge(mt_done, tt * 8 + hb + 1)
                    if tt == 1:
                        if hb == 0:
                            pe.wait_ge(act_freed, FREED[KEY["state", 0, GROUPS - 1]][1])
                        pe.wait_ge(ce_done, hb + 1)
                    for j in range(4):
                        hd = 4 * hb + j
                        o = out[64 * (hd % 2):64 * (hd % 2) + 64, (j // 2) * n:(j // 2 + 1) * n]
                        a = pe.matmul(o, xt[0:n, hd * 64:(hd + 1) * 64], mt[0:n, (tt * 8 + hb) % 2, j * n:(j + 1) * n],
                                      start=True, stop=(tt != 1))
                        if tt == 1:
                            a = pe.matmul(o, s_a[:, hd * 64:(hd + 1) * 64], ce[:, j * n:(j + 1) * n],
                                          start=False, stop=True)
                    close(a)
                if tt < 2:
                    pe.wait_ge(act_freed, FREED[KEY["bt", tt]][1])
                    pe.wait_ge(xd_done, tt + 1)
                    for g in range(GROUPS):
                        out = open_group(("state", tt, g))
                        close(pe.matmul(out, bt[:, g * P:(g + 1) * P], xd[:, g * 512:(g + 1) * 512],
                                        start=True, stop=True))
            out = open_group("s decay", NB * HEADS)
            pe.wait_ge(sdr_done, 1)
            close(pe.matmul(out, ones[0:32, :], sdr[0:32, :], start=True, stop=True))
            out = open_group("expand")
            pe.wait_ge(dec_done, 5)
            for hd in range(HEADS):
                a = pe.matmul(out[64 * (hd % 2):64 * (hd % 2) + 64, (hd // 2) * 32:(hd // 2 + 1) * 32],
                              ea[0:32, hd:hd + 1].broadcast_to([32, 64]), ident[0:32, 0:32],
                              start=True, stop=True)
            close(a)
            pe.wait_ge(xd_done, 3)
            for b in range(NB):
                out = open_group(("y off", b), 64)
                for half in range(2):
                    states = plain()
                    for i in range(8):
                        k = 8 * half + i
                        a = pe.matmul(out[:, k * TS:(k + 1) * TS], states[:, i * P:(i + 1) * P],
                                      bc[:, 4 + k // 4, SEQ + b * TS:SEQ + (b + 1) * TS], start=True, stop=True)
                    a.then_inc(raw_used, 1) if half == 0 else close(a)
                pe.wait_ge(btm_done, b + 1)
                for g in range(GROUPS):
                    out = open_group(("s state", b, g))
                    close(pe.matmul(out, btm[0:32, b % 2, g * P:(g + 1) * P], xd[0:32, g * 512:(g + 1) * 512],
                                    start=True, stop=True))
            pe.wait_ge(ysq_done, 1)
            for g in range(GROUPS):
                out = open_group(("gn", g), NT)
                for k in range(4):
                    a = pe.matmul(out, ones, ysq[:, 4 * g + k, :], start=(k == 0), stop=(k == 3))
                close(a)
            pe.wait_ge(yl_done, 3)
            for j in range(KD):
                k0 = NEED[KEY["ssd out", j]] - 2
                product(("ssd out", j), [(k0 + k // 8, k % 8, k) for k in range(KI)], y_hi, y_lo)
            attention(1)
            norm(5)
            out = open_group("logits", 24)
            pe.wait_ge(h_done, 6)
            router = par("router").rearrange("p (k m) -> p k m", k=KD)
            for m, (c0, n) in enumerate(TOK):
                for k in range(KD):
                    a = pe.matmul(out[0:n, NE * m:NE * m + NE], h[:, k, c0:c0 + n], router[:, k, :],
                                  start=(k == 0), stop=(k == KD - 1))
            close(a)
            out = open_group("pos", 4 * NE)
            pe.wait_ge(msk_done, 1)
            for m, (_, n) in enumerate(TOK):
                for k in range(m):
                    pe.matmul(out[0:n, NE * m:NE * m + NE], ones[:, 0:n], msk[:, k, 0:NE], start=(k == 0), stop=False)
                pe.matmul(out[0:n, NE * m:NE * m + NE], par("before")[0:n, 0:n], msk[0:n, m, 0:NE],
                          start=(m == 0), stop=True)
            for m, (_, n) in enumerate(TOK):
                a = pe.matmul(out[:, 3 * NE:4 * NE], ones[0:n, :], msk[0:n, m, 0:NE], start=(m == 0), stop=(m == 2))
            close(a)
            for i in range(6):
                c0, n = TOK[i // 2]
                out = open_group(("ht", i), rows=n)
                for k in range(4):
                    a = pe.transpose(out[:, k * P:(k + 1) * P], h[:, 4 * (i % 2) + k, c0:c0 + n], ident)
                close(a)
            pe.wait_ge(dve_freed, freed_n["dve"])

            def experts(c):
                s = PASSES[c]

                def gather(e):
                    pe.wait_ge(s.sel, e + 1)
                    for j in range(KD):
                        for m, (_, n) in enumerate(TOK):
                            a = pe.matmul(ps[:, j // 4, (j % 4) * P:(j % 4 + 1) * P], htok[0:n, m, j * P:(j + 1) * P],
                                          sel[0:n, m, :], start=(m == 0), stop=(m == 2))
                    a.then_inc(s.gather, 1)

                def scatter(e):
                    pe.wait_ge(s.ye, e + 1)
                    for j in range(KD):
                        pe.wait_ge(s.add, e * KD + j + 1)
                        pe.matmul(ps[:, 5 + j % 3, 0:NT], ye[:, j * P:(j + 1) * P], sg[:, :],
                                  start=True, stop=True).then_inc(s.scat, 1)

                nv = VIRTUAL[c][1]
                if c:
                    pe.wait_ge(PASSES[0].add, VIRTUAL[0][1] * KD + KD + 3)
                pe.wait_ge(s.sg, 1)
                for j in range(2):
                    for k in range(2):
                        a = pe.matmul(ps[:, 5 + j, k * 256:(k + 1) * 256], sg[:, 0:P], sg[:, 0:256],
                                      start=True, stop=True)
                a.then_inc(s.used, HL)
                gather(0)
                with pe.Fori(0, nv) as e:
                    pe.wait_ge(s.xl, e + 1)

                    def up(f, which):
                        out = ps[:, 2 * which + f % 2, :]
                        for c4 in range(4):
                            p = 8 * f + 4 * which + c4
                            k = (NSPLIT + p) % HL
                            pe.wait_ge(s.lo, e * CPE + p + 1 + RAW)
                            for kk in range(2):
                                ka, w = 2 * c4 + kk, slice(kk * 512, (kk + 1) * 512)
                                a = mm3(out, xe_hi[:, ka * P:(ka + 1) * P], xe_lo[:, ka * P:(ka + 1) * P],
                                        w_hi[:, k, w], w_lo[:, k, w], ka == 0, ka == KD - 1)
                            a.then_inc(s.used, 1)

                    def turn(f):
                        pe.wait_ge(s.g, e * FB + f + 1 + 2)
                        pe.wait_ge(s.gl, e * FB + f + 1)
                        for k in range(4):
                            a = pe.transpose(ps[:, 4, k * P:(k + 1) * P], ge[:, f % 2, k * P:(k + 1) * P], ident)
                        a.then_inc(s.turn, 1)

                    for f in range(FB):
                        pe.wait_ge(s.g, e * FB + f + 1)
                        up(f, 0)
                        if f == 0:
                            pe.wait_ge(s.sg, e + 1)
                        else:
                            turn(f - 1)
                        up(f, 1)
                        if f == 0:
                            scatter(e)
                    pe.wait_ge(s.add, e * KD + KD + 3)
                    for kt_ in range(KFE):
                        if kt_ == 2:
                            turn(FB - 1)
                        if kt_ == 4:
                            pe.wait_ge(s.sel, e + 1)
                            for m, (c0, n) in enumerate(TOK):
                                a = pe.transpose(ps[:, 2, c0:c0 + n], selg[0:n, m, :], ident[0:n, 0:n])
                            a.then_inc(s.sgt, 1)
                        if kt_ == 16:
                            gather(e + 1)
                        p = 8 * FB + kt_
                        k = (NSPLIT + p) % HL
                        pe.wait_ge(s.gl, e * FB + kt_ // 4 + 2)
                        pe.wait_ge(s.lo, e * CPE + p + 1 + RAW)
                        for nb in range(2):
                            w = slice(nb * 512, (nb + 1) * 512)
                            a = mm3(ps[:, 5 + nb, :], gt_hi[:, kt_, :], gt_lo[:, kt_, :], w_hi[:, k, w], w_lo[:, k, w],
                                    kt_ == 0, kt_ == KFE - 1)
                        a.then_inc(s.used, 1)
                scatter(nv)

            experts(0)
            over = overflow(pe)
            with pe.If(over > P):
                experts(1)
                pe.nop()
            pe.wait_ge(sq_done, 8)
            for k in range(KD):
                a = pe.matmul(ps[:, 0, 0:NT], ones, h[:, k, :], start=(k == 0), stop=(k == KD - 1))
            a.then_inc(full, 1)

        @block.gpsimd
        def _(pool):
            pool.wait_ge(small_in, 16)
            pool.wait_ge(kv_out, 64)
            pool.memset(conv[:, :, 0:CW - 1], 0.0)
            prev = par("lru_prev").rearrange("p (j b w) -> p j b w", b=NB, w=3)
            for j in range(KD):
                a = pool.tensor_copy(samples(conv[:, j, PS0:PADW], TS + CW - 1, 0, CW - 1), prev[:, j, :, :])
            a.then_inc(cinit, 1)
            pool.wait_ge(act_freed, FREED[KEY["xb", KD - 1]][1])
            for j in range(KD):
                pool.tensor_copy(lru_new_c[:, j, 0:3], conv[:, j, SEQ:SEQ + 3])
                a = pool.tensor_copy(lru_new_c[:, j, 3:27].rearrange("p (b w) -> p b w", w=3),
                                     samples(conv[:, j, PS0:PADW], TS + CW - 1, TS, CW - 1))
            a.then_inc(state_ready, 1)
            pool.wait_ge(hs_done, 1)
            pool.tensor_copy(lru_new_h[:, :, 0], hs[:, :, SEQ - 1])
            pool.tensor_copy(lru_new_h[:, :, 1:1 + NB],
                             hs[:, :, SEQ:NT].rearrange("p j (b w) -> p j b w", w=TS)[:, :, :, TS - 1]) \
                .then_inc(state_ready, 1)
            pool.wait_ge(state_ready, 2)
            pool.dma_start(t["out_lru_c"], lru_new_c[:, :, :]).then_inc(out_done, 16)
            pool.dma_start(t["out_lru_h"], lru_new_h[:, :, :]).then_inc(out_done, 16)

            def load_kv(l):
                pool.dma_start(kt[:, :, :], t["out_k"][l]).then_inc(kv_in, 16)
                pool.dma_start(vt[:, :, :], t["out_v"][l]).then_inc(kv_in, 16)

            pool.wait_ge(dve_freed, RESID[1])
            load_kv(0)
            pool.wait_ge(dve_freed, RESID[3])
            pool.dma_start(ssd_prev[:, :, :, :], t["ssd_prev"]).then_inc(prev_in, 16)
            for c in range(3):
                a = pool.memset(cv[:, c, 0:CW - 1], 0.0)
            pool.wait_ge(prev_in, 16)

            def before(c):
                pool.tensor_copy(samples(cv[:, c % 3, PS0:PADW], TS + CW - 1, 0, CW - 1), ssd_prev[:, c, :, :]) \
                    .then_inc(prev_done, 1)

            for c in range(3):
                before(c)
            for c in range(NXBC):
                pool.wait_ge(act_freed, FREED[KEY["xbc", c]][1])
                pool.tensor_copy(ssd_new_c[:, c, 0:3], cv[:, c % 3, SEQ:SEQ + 3])
                pool.tensor_copy(ssd_new_c[:, c, 3:27].rearrange("p (b w) -> p b w", w=3),
                                 samples(cv[:, c % 3, PS0:PADW], TS + CW - 1, TS, CW - 1)) \
                    .then_inc(save_done, 1)
                if c + 3 < NXBC:
                    pool.wait_ge(cvo_done, c + 1)
                    before(c + 3)
            pool.wait_ge(save_done, NXBC)
            pool.dma_start(t["out_ssd_c"], ssd_new_c[:, :, :]).then_inc(out_done, 16)
            for tt, (_, n) in enumerate(TOK):
                pool.wait_ge(xt_done, 4 * (tt + 1))
                pool.wait_ge(dec_done, (1, 2, 4)[tt])
                if tt:
                    pool.wait_ge(full, KEY["state", tt - 1, GROUPS - 1] + 1)
                pool.tensor_tensor(xd[0:n, :].rearrange("p (h f) -> p h f", f=64),
                                   xt[0:n, :].rearrange("p (h f) -> p h f", f=64),
                                   dec[0:n, :].unsqueeze(2).broadcast_to([n, HEADS, 64]), ALU.mult) \
                    .then_inc(xd_done, 1)
                if tt == 1:
                    pool.wait_ge(dec_done, 3)
                    pool.wait_ge(full, KEY["y", 1, 7] + 1)
                    sv = s_a[:, :].rearrange("p (h f) -> p h f", f=64)
                    pool.tensor_tensor(sv, sv, cdec[:, :].unsqueeze(2).broadcast_to([P, HEADS, 64]),
                                       ALU.mult).then_inc(sad_done, 1)
            pool.wait_ge(sb_done, GROUPS)
            pool.dma_start(t["out_ssd_p"], s_b[:, :]).then_inc(state_out[2], 16)
            pool.wait_ge(act_freed, FREED[KEY["s decay"]][1])
            state_at = [i for i, k in enumerate(ORDER) if k == "s"]
            for b in range(NB):
                for half in range(2):
                    i = state_at[2 * b + half]
                    pool.wait_ge(landed[i % RAW], 16 * (i // RAW + 1))
                    pool.wait_ge(state_out[half] if b else state_out[2], 16 * max(b, 1))
                    pool.tensor_tensor(s_new[:, half, :].rearrange("p (h f) -> p h f", f=64),
                                       raw[:, i % RAW, :].rearrange("p (h f) -> p h f", f=64),
                                       sdec[:, b * HEADS + 16 * half:b * HEADS + 16 * half + 16]
                                       .unsqueeze(2).broadcast_to([P, 16, 64]), ALU.mult).then_inc(sn_dec, 1)
                for half in range(2):
                    pool.wait_ge(sn_done, 4 * b + 2 * half + 2)
                    pool.dma_start(t["out_ssd_s"][b, half], s_new[:, half, :]).then_inc(state_out[half], 16)
            for half in range(2):
                pool.wait_ge(state_out[half], 16 * NB)
            pool.wait_ge(dve_freed, RESID[4])
            load_kv(1)
            pool.wait_ge(out_done, 48)


def small_inputs(np, a):
    s = np.zeros((P, NSMALL), np.float32)

    def put(name, v):
        at, n = SMALL[name]
        v = np.asarray(v)
        s[:v.shape[0], at:at + n] = v.reshape(v.shape[0], n)

    def tiles(v):
        v = np.asarray(v)
        v = v.reshape(v.shape[:-1] + (-1, P))
        return np.moveaxis(v, (-1, -2), (0, 1))

    def gains(v):
        return np.asarray(v).reshape(-1, P).T
    put("g_mix", gains(a["norm_mix"]))
    put("g_mem", gains(a["norm_mem"]))
    put("g_memkv", gains(a["norm_memkv"]))
    put("g_ffn", gains(a["norm_ffn"]))
    put("g_fin", gains(a["norm_final"]))
    put("lru_cw", tiles(a["lru_conv_w"][0]))
    put("lru_cb", tiles(a["lru_conv_b"][0]))
    put("b_a", tiles(a["lru_b_a"][0]))
    put("b_x", tiles(a["lru_b_x"][0]))
    put("lam", tiles(a["lru_lam"][0]))
    put("h_prev", tiles(a["state_lru_h"][0]))
    put("lru_prev", tiles(a["state_lru_conv"][0]))
    put("ssd_cw", tiles(a["ssd_conv_w"][0]))
    put("ssd_cb", tiles(a["ssd_conv_b"][0]))
    put("ssd_g", tiles(a["ssd_norm_g"][0]))
    put("ssd_d", tiles(np.repeat(np.asarray(a["ssd_d"][0]), 64)))
    put("dt_b", np.broadcast_to(np.asarray(a["ssd_dt_bias"][0]), (P, HEADS)))
    put("a_log", np.broadcast_to(np.asarray(a["ssd_a_log"][0]), (P, HEADS)))
    put("router", np.asarray(a["moe_router"][0]).reshape(KD, P, NE).transpose(1, 0, 2))
    put("w_dt", np.asarray(a["ssd_w_in"][0])[:, DI + NXBC * P:].reshape(KD, P, HEADS).transpose(1, 0, 2))
    i = np.arange(P)
    j = np.arange(32)
    put("ident", np.eye(P))
    put("tri", i[:, None] <= i[None])
    put("tri_s", (j[:, None] <= j[None]) & (j[:, None] // TS == j[None] // TS))
    put("last", np.broadcast_to(i[:, None] == P - 1, (P, P)))
    put("last_s", j[:, None] == TS * (j[None] // TS) + TS - 1)
    put("is_last", j[:, None] == TS * np.arange(NB)[None] + TS - 1)
    put("in_seq", j[:, None] // TS == np.arange(NB)[None])
    put("ones", np.ones((P, P)))
    put("before", i[:, None] < i[None])
    put("iota", np.broadcast_to(i[None], (P, P)))
    e = np.arange(NE)
    put("lower", np.broadcast_to((e[None] < e[:, None])[None], (P, NE, NE)))
    put("eps", np.full((P, 1), EPS))
    return s


def stream_inputs(np, a):
    def columns(w):
        w = np.asarray(w)
        k, n = w.shape
        return w.reshape(k // P, P, n // P, P).transpose(2, 1, 0, 3).reshape(n // P, P, k)

    def flat(w):
        w = columns(w)
        n, _, k = w.shape
        w = w.reshape(n, P, k // P, P).transpose(0, 2, 1, 3).reshape(-1, 8, P, P)
        return w.transpose(0, 2, 1, 3).reshape(-1, P, CH)

    def rows(w):
        w = np.asarray(w)
        k, n = w.shape
        w = w.reshape(k // (2 * P), 2, P, n // 512, 512)
        return w.transpose(3, 0, 2, 1, 4).reshape(-1, P, CH)

    def keys(c):
        c = np.asarray(c).reshape(NB, NMEM, 2, 4, P)
        return c.transpose(0, 2, 4, 3, 1).reshape(-1, P, CH)

    def values(c):
        return np.asarray(c).reshape(-1, P, CH)

    parts = []
    for l in range(2):
        parts += [columns(a["mem_w_k"][l]), rows(a["mem_w_v"][l])]
    parts += [columns(a["lru_w_in"][0])]
    for w in ("lru_w_a", "lru_w_x"):
        parts += [np.asarray(a[w][0]).transpose(1, 0, 2).reshape(1, P, CH)]
    parts += [columns(a["lru_w_out"][0])]

    def attention(l):
        return [columns(a["mem_w_q"][l]), keys(a["cache_mem_k"][l]), values(a["cache_mem_v"][l]),
                columns(a["mem_w_o"][l])]

    parts += attention(0)
    w1, w3 = columns(a["ffn_w1"][0]), columns(a["ffn_w3"][0])
    parts += [np.stack([w1, w3], 1).reshape(-1, P, CH), flat(a["ffn_w2"][0])]
    w_in = np.asarray(a["ssd_w_in"][0])
    parts += [columns(w_in[:, DI:DI + NXBC * P]), columns(w_in[:, :DI])]
    state = np.asarray(a["state_ssd"][0]).reshape(NB, 2, 16 * 64, P)
    parts += [state.transpose(0, 1, 3, 2).reshape(-1, P, CH)]
    parts += [flat(a["ssd_w_out"][0])]
    parts += attention(1)
    stream = np.concatenate(parts)
    assert stream.shape == (NSTAT, P, CH), stream.shape
    experts = np.empty((NE, CPE, P, CH), np.float32)
    for e in range(NE):
        up = experts[e, :8 * FB].reshape(FB, 2, 4, P, CH)
        up[:, 0] = rows(a["moe_w1"][0][e]).reshape(FB, 4, P, CH)
        up[:, 1] = rows(a["moe_w3"][0][e]).reshape(FB, 4, P, CH)
        experts[e, 8 * FB:] = np.asarray(a["moe_w2"][0][e]).reshape(KFE, P, CH)
    return stream, experts.reshape(NE * CPE, P, CH)


OUTS = {"out_x": (P, KD, NT), "out_k": (2, P, KD, NMEM), "out_v": (2, P, 2, D),
        "out_lru_h": (P, KD, 1 + NB), "out_lru_c": (P, KD, 27), "out_ssd_c": (P, NXBC, 27),
        "out_ssd_p": (P, DI), "out_ssd_s": (NB, 2, P, CH)}


def kernel(**inputs):
    import numpy as np
    import concourse.bacc as bacc
    from concourse.bass_utils import run_bass_kernel_spmd

    a = {k: np.asarray(v) for k, v in inputs.items()}
    stream, experts = stream_inputs(np, a)

    def feature_major(v):
        return np.ascontiguousarray(v.reshape(v.shape[0], KD, P).transpose(2, 1, 0))

    arrays = {
        "stream": stream, "experts": experts, "small": small_inputs(np, a),
        "x": feature_major(np.concatenate([a["x_prompt"][0], a["x_sample"].reshape(NB * TS, D)])),
        "mem": feature_major(a["mem_prompt"][0]),
        "ssd_prev": np.ascontiguousarray(
            a["state_ssd_conv"][0].reshape(NB, 3, NXBC, P).transpose(3, 2, 0, 1)),
    }
    nc = bacc.Bacc("TRN2", target_bir_lowering=False, num_devices=1)
    t = {k: nc.dram_tensor(f"in_{k}", v.shape, F32, kind="ExternalInput").ap() for k, v in arrays.items()}
    t.update({k: nc.dram_tensor(k, s, F32, kind="ExternalOutput").ap() for k, s in OUTS.items()})
    build_program(nc, t)
    r = run_bass_kernel_spmd(nc, [{f"in_{k}": v for k, v in arrays.items()}], core_ids=[0]).results[0]

    def tokens(v):
        return np.asarray(v).transpose(2, 1, 0).reshape(v.shape[2], -1)

    out = tokens(r["out_x"])
    lru_h, lru_c, ssd_c = tokens(r["out_lru_h"]), tokens(r["out_lru_c"]), tokens(r["out_ssd_c"])
    mem_k = np.stack([tokens(r["out_k"][l]) for l in range(2)]).reshape(2, 1, NMEM, MH, 256)
    mem_v = np.asarray(r["out_v"]).transpose(0, 2, 1, 3).reshape(2, 1, NMEM, MH, 256)
    ssd_p = np.asarray(r["out_ssd_p"]).T.reshape(1, 1, HEADS, 64, P)
    ssd_s = np.asarray(r["out_ssd_s"]).transpose(0, 1, 3, 2).reshape(1, NB, HEADS, 64, P)
    return (out[:SEQ].reshape(1, SEQ, D), out[SEQ:].reshape(NB, TS, D),
            lru_h[:1].reshape(1, 1, D), lru_c[:3].reshape(1, 1, 3, D), ssd_p, ssd_c[:3].reshape(1, 1, 3, NXBC * P),
            mem_k, mem_v,
            lru_h[1:].reshape(1, NB, D), lru_c[3:].reshape(1, NB, 3, D), ssd_s,
            ssd_c[3:].reshape(1, NB, 3, NXBC * P))
```

```python
from contextlib import ExitStack

import concourse.bass as bass
from concourse import mybir

F32 = mybir.dt.float32
F32R = mybir.dt.float32r
I32 = mybir.dt.int32
ALU = mybir.AluOpType
ACT = mybir.ActivationFunctionType
AX = mybir.AxisListType

P = 128
D = 1024
KD = D // P
SEQ = 256
NB = 8
TS = 4
NT = SEQ + NB * TS
TOK = [(0, 128), (128, 128), (256, 32)]
CW = 4
PADW = (SEQ + CW - 1) + NB * (TS + CW - 1)
PS0 = SEQ + CW - 1
DI = 2048
KI = DI // P
NXBC = 24
HEADS = 32
GROUPS = 4
MH = 4
NMEM = 256
FF = 2816
KF = FF // P
NE = 8
NV = 3 * NE
FE = 3584
KFE = FE // P
FB = FE // 512
EPS = 1e-6
NEVER = -2.0 ** 60

CH = 1024
RAW = 7
HL = 7
CPE = 3 * KFE
assert CPE % RAW == 0 and CPE % HL == 0

SMALL = {}
_at = 0
for _name, _n in [("g_mix", 16), ("g_mem", 16), ("g_memkv", 16), ("g_ffn", 16), ("g_fin", 8),
                  ("lru_cw", 32), ("lru_cb", 8), ("b_a", 8), ("b_x", 8), ("lam", 8), ("h_prev", 64),
                  ("lru_prev", 192), ("ssd_cw", 96), ("ssd_cb", 24), ("ssd_g", 16), ("ssd_d", 16),
                  ("dt_b", 32), ("a_log", 32), ("router", 64), ("w_dt", 256),
                  ("ident", 128), ("tri", 128), ("tri_s", 32), ("last", 128), ("last_s", 32),
                  ("is_last", 8), ("in_seq", 8), ("ones", 128), ("before", 128), ("iota", 128),
                  ("lower", 64), ("eps", 1)]:
    SMALL[_name] = (_at, _n)
    _at += _n
NSMALL = _at


EARLY = 2


def plan():
    def memory(l):
        q = [(("k", l, j), "dve", 1) for j in range(KD)]
        for nb in range(2):
            q += [(("v", l, nb, 0), "act", 3), (("v", l, nb, 1), "act", 1)]
        return q

    def second(q, key):
        return q[:1] + [(key, "act", 0)] + q[1:]

    p = second(memory(0), "mem norm")
    p += second([(("gate", j), "dve", 1) for j in range(KD)], ("norm", 0))
    p += [(("xb", j), "dve", 1) for j in range(KD)]
    p += memory(1)[:EARLY]
    p += [(("r", j), "act", int(j == 0)) for j in range(KD)]
    p += [(("i", j), "act", int(j == 0)) for j in range(KD)]
    p += memory(1)[EARLY:]
    p += [(("lru out", j), "dve", 1) for j in range(KD)]

    def attention(l):
        q = second([(("q", l, j), "dve", 1) for j in range(KD)], ("norm", 3 * l + 1))
        q += [(("scores", l, h), "act", 0) for h in range(MH)]
        for b in range(NB):
            if b == NB // 2:
                q += [(("probs", l, i), "dve", 0) for i in range(4)]
            q += [(("s scores", l, half, b), "act" if b == NB - 1 else None, 1) for half in range(2)]
        q += [(("o", l, j), "dve", 0) for j in range(KD)]
        q += [(("s probs", l), "dve", 0)]
        q += [(("s o", l, half, b), "act" if b == NB - 1 else None, 1) for b in range(NB) for half in range(2)]
        return q + [(("s o turn", l), "dve", 0)] + [(("mem out", l, j), "dve", 1) for j in range(KD)]

    p += attention(0)
    up = []
    for f in range(KF):
        up += [(("f1", f), "dve", 1), (("f3", f), "dve", 1)]
    p += second(up, ("norm", 2))
    p += [(("f2", j), "dve", -(-KF * (j + 1) // 8) + KF * j // -8) for j in range(KD)]
    p += [(("norm", 3), "act", 0)] + [(("xbc", c), "act", 1) for c in range(3)] + [("dt t", "act", 0), ("dt", "dve", 0)]
    p += [(("xbc", c), "act", 1) for c in range(3, NXBC)] + [(("z", c), "act", 1) for c in range(KI)]
    for t in range(3):
        p += [(("acs", t), "dve", 0), (("last", t), "dve", 0)]
        p += [(("xt", t, i), "dve", 0) for i in range(4)]
        p += [(("bt", t), "act", 0), (("cb", t), "dve", 0)]
        for hb in range(10):
            if hb < 8:
                p += [(("ab", t, hb), "act", 0)] + [(("state ab", hb), "act", 0)] * (t == 1)
            if hb >= 2:
                p += [(("y", t, hb - 2), "dve", 0)]
        if t < 2:
            p += [(("state", t, g), "act" if t == 0 else "dve", 0) for g in range(GROUPS)]
    p += [("s decay", "act", 0)]
    for b in range(NB):
        p += [(("y off", g, b), "dve" if b == NB - 1 else None, (g + 1) % 2) for g in range(GROUPS)]
        p += [(("s state", b, g), "dve", 0) for g in range(GROUPS)]
    p += [("y off turn", "dve", 0)]
    p += [(("gn", g), "act", 0) for g in range(GROUPS)]
    p += [(("ssd out", j), "dve", 2) for j in range(KD)]
    p += attention(1)
    p += [(("norm", 5), "act", 0), ("logits t", "act", 0), ("logits", "dve", 0)]
    p += [(("ht", i), "act", 0) for i in range(6)]
    p += [("pos", "dve", 0)]
    return p


PLAN = plan()
KEY = {key: g for g, (key, _, _) in enumerate(PLAN)}
NSTAT = sum(chunks for _, _, chunks in PLAN)


def build_program(nc, t):
    NEED = []
    for _, _, chunks in PLAN:
        NEED.append((NEED[-1] if NEED else 0) + chunks)
    FREED, BANK, BEFORE = [], [None] * len(PLAN), [None] * len(PLAN)
    freed_n = {"act": 0, "dve": 0}
    turn = [(b, None) for b in range(8)]
    for g, (key, eng, _) in enumerate(PLAN):
        if not eng and key[-1] == 0:
            whole = KEY[key[:-1] + (NB - 1,)]
            BANK[whole], BEFORE[whole] = turn.pop(0)
        if eng:
            if BANK[g] is None:
                BANK[g], BEFORE[g] = turn.pop(0)
            turn.append((BANK[g], g))
            freed_n[eng] += 1
        FREED.append((eng, freed_n[eng]) if eng else None)

    with ExitStack() as ctx:
        def sem(name):
            return ctx.enter_context(nc.semaphore(name))

        base = -(-nc.sbuf_base // 64) * 64
        arena = nc.alloc_sbuf_tensor("arena", [P, (nc.sbuf_usable_end - base) // 4 - 64], F32)

        def at(name, shape, dtype, offset):
            return nc.alloc_sbuf_tensor_at(name, [P] + shape, dtype, offset=offset, align_bytes=4)

        o_raw = base
        o_hi = o_raw + RAW * CH * 4
        o_lo = o_hi + HL * CH * 4
        o_x = o_lo + HL * CH * 4
        o_small = o_x + KD * NT * 4
        area = -(-(o_small + NSMALL * 4) // 64) * 64
        SLOT = KD * NT * 4
        S = [area + i * SLOT for i in range(11)]
        tail = S[10] + SLOT
        end = nc.sbuf_usable_end
        raw = at("raw", [RAW, CH], F32, o_raw)
        w_hi = at("w_hi", [HL, CH], F32R, o_hi)
        w_lo = at("w_lo", [HL, CH], F32R, o_lo)
        x = at("x_res", [KD, NT], F32, o_x)
        small = at("small", [NSMALL], F32, o_small)

        def par(name):
            a, n = SMALL[name]
            return small[:, a:a + n]

        ident, tri, ones = par("ident"), par("tri"), par("ones")
        eps = par("eps")
        h = at("h", [KD, NT], F32, S[0])
        h_hi = at("h_hi", [KD, NT], F32R, S[1])
        h_lo = at("h_lo", [KD, NT], F32R, S[2])
        rt = at("rt", [NT], F32, tail)
        small_t = at("small_t", [NT], F32, tail)
        rs = at("rs", [NT], F32, tail + NT * 4)
        nc8 = at("nc8", [KD], F32, tail + 2 * NT * 4)
        sp = at("sp", [6, 96], F32, tail + 2 * NT * 4 + 64)
        dt_off = tail + 2 * NT * 4 + 64 + 6 * 96 * 4
        dt = at("dt", [3, HEADS], F32, dt_off)
        adt = at("adt", [3, HEADS], F32, dt_off + 384)
        acs = at("acs", [HEADS], F32, dt_off + 768)
        dec = at("dec", [HEADS], F32, dt_off + 896)
        cdec = at("cdec", [HEADS], F32, dt_off + 1024)
        last_dec = at("last_dec", [HEADS], F32, dt_off + 1152)
        assert dt_off + 1280 <= end, (dt_off + 1280, end)

        memx = at("memx", [KD, NMEM], F32, S[5])
        memsq = at("memsq", [KD, NMEM], F32, S[3])
        mem_hi = [at(f"mem_hi{l}", [KD, NMEM], F32R, (S[6], S[4])[l]) for l in range(2)]
        mem_lo = [at(f"mem_lo{l}", [KD, NMEM], F32R, (S[7], S[10] + 1024)[l]) for l in range(2)]
        kmem = [at(f"kmem{l}", [KD, NMEM], F32, (S[9], S[1])[l]) for l in range(2)]
        vmem = [at(f"vmem{l}", [2, D], F32, S[8]) for l in range(2)]
        rmt = at("rmt", [NMEM + 2], F32, dt_off + 1472)
        rm = at("rm", [NMEM + 2], F32, dt_off + 2560)
        assert dt_off + 2560 + (NMEM + 2) * 4 <= end
        gate = at("gate", [KD, NT], F32, S[3])
        conv = at("conv", [KD, PADW], F32, S[9])
        conv_t = at("conv_t", [2, PADW], F32, S[8])
        xc = at("xc", [KD, NT], F32, S[5])
        xc_hi = at("xc_hi", [KD, NT], F32R, S[6])
        xc_lo = at("xc_lo", [KD, NT], F32R, S[7])
        rg = at("rg", [KD, NT], F32, S[8])
        ig = at("ig", [KD, NT], F32, S[2])
        decay = at("decay", [KD, NT], F32, S[0])
        expm = at("expm", [KD, NT], F32, S[9])
        tanh = at("tanh", [KD, NT], F32, S[2])
        y_lru = at("y_lru", [KD, NT], F32, S[2])
        hs_t = at("hs_t", [KD, NB], F32, dt_off)
        lru_new_h = at("lru_new_h", [KD, 1 + NB], F32, dt_off + 256)
        lru_new_c = at("lru_new_c", [KD, 3 * (1 + NB)], F32, dt_off + 256 + 320)
        assert dt_off + 576 + 8 * 27 * 4 <= end
        q = at("q", [KD, NT], F32, S[3])
        kt = at("kt", [KD, NMEM], F32, S[4])
        vt = at("vt", [2, D], F32, S[5])
        pr = at("pr", [8, NMEM], F32, S[6])
        prs = at("prs", [MH, NMEM], F32, S[3])
        prt = at("prt", [2, MH, SEQ], F32, S[7])
        qm = [at("qm_hi", [NB * 260], F32R, S[8]), at("qm_lo", [NB * 260], F32R, S[0])]
        pm = [at("pm_hi", [2, NB * 132], F32R, S[1]), at("pm_lo", [2, NB * 132], F32R, S[2])]
        att_hi = at("att_hi", [KD, NT], F32R, S[9])
        att_lo = at("att_lo", [KD, NT], F32R, S[10])
        so = at("so", [D], F32, S[3] + 4096)
        mx = at("mx", [12], F32, dt_off + 1024)
        nmx = at("nmx", [12], F32, dt_off + 1024 + 64)
        rsum = at("rsum", [12], F32, dt_off + 1152)
        rinv = at("rinv", [12], F32, dt_off + 1216)
        f_hi = at("f_hi", [KF, NT], F32R, S[3])
        f_lo = at("f_lo", [KF, NT], F32R, S[3] + KF * NT * 4)
        f_s = at("f_s", [2, NT], F32, S[3] + 2 * KF * NT * 4)
        f_g = at("f_g", [2, NT], F32, S[3] + 2 * KF * NT * 4 + 2 * NT * 4)
        y = at("y", [KI, NT], F32, S[3])
        bc = at("bc", [8, NT], F32, S[5])
        zs = at("zs", [KI, NT], F32, S[6])
        cv = at("cv", [3, PADW], F32, S[8])
        cv_t = at("cv_t", [2, PADW], F32, S[8] + 3 * PADW * 4)
        cv_o = at("cv_o", [2, NT], F32, S[8] + 5 * PADW * 4)
        ssd_prev = at("ssd_prev", [NXBC, NB, 3], F32, S[9])
        ssd_new_c = at("ssd_new_c", [NXBC, 27], F32, S[9] + NXBC * 24 * 4)
        xt = at("xt", [DI], F32, S[0])
        xd = at("xd", [DI], F32, S[1])
        s_a = at("s_a", [DI], F32, S[2])
        s_b = at("s_b", [DI], F32, S[8])
        s_new = [at(f"s_new{i}", [CH], F32, (S[8], S[5])[i // 2] + i % 2 * 4096) for i in range(4)]
        bt = at("bt", [512], F32, S[9])
        cbm = at("cbm", [512], F32, S[9] + 2048)
        mt = [at(f"mt{k}", [512], F32, (S[10], S[9] + 4096)[k // 2] + k % 2 * 2048) for k in range(4)]
        ident_r = at("ident_r", [P], F32R, S[10] + 8192)
        future_r = at("future_r", [P], F32R, S[10] + 8704)
        future_s = at("future_s", [32], F32R, S[9] + 8192)
        nacs = at("nacs", [HEADS], F32, S[9] + 8448)
        tri_r = at("tri_r", [P], F32R, S[9] + 8576)
        tri_sr = at("tri_sr", [32], F32R, S[9] + 9088)
        adt_s = [at("adt_hi", [3, HEADS], F32R, dt_off + 1472), at("adt_lo", [3, HEADS], F32R, dt_off + 1856)]
        eb = at("eb", [512], F32, S[10] + 4096)
        ce = at("ce", [512], F32, S[10] + 6144)
        btm = at("btm", [2, 512], F32, S[10])
        cm = [at("cm_hi", [NB * 132], F32R, S[2]), at("cm_lo", [NB * 132], F32R, S[0])]
        sdec = at("sdec", [NB * HEADS], F32, S[0] + 8192)
        ea = at("ea", [HEADS], F32, S[1] + 8192)
        sdr = at("sdr", [NB * HEADS], F32, S[2] + 8192)
        yo = [at("yo0", [CH], F32, S[9] + 4096), at("yo1", [CH], F32, S[10] + 4096)]
        ysq = at("ysq", [KI, NT], F32, S[6])
        y_hi = at("y_hi", [KI, NT], F32R, S[6])
        y_lo = at("y_lo", [KI, NT], F32R, S[3])
        grt = at("grt", [GROUPS, NT], F32, S[9])
        grs = at("grs", [GROUPS, NT], F32, S[9] + GROUPS * NT * 4)
        htok = at("htok", [3, D], F32, S[3])
        o_e = S[3] + 3 * D * 4
        sel = at("sel", [3, P], F32, o_e)
        selg = at("selg", [3, P], F32, o_e + 1536)
        sg = at("sg", [NT], F32, o_e + 3072)
        xe_hi = at("xe_hi", [KD * P], F32R, o_e + 3072 + 1152)
        xe_lo = at("xe_lo", [KD * P], F32R, o_e + 3072 + 1152 + 4096)
        o_g = o_e + 3072 + 1152 + 8192
        sil = at("sil", [2, 512], F32, o_g)
        ge = at("ge", [2, 512], F32, o_g + 4096)
        gt_hi = at("gt_hi", [KFE, P], F32R, o_g + 8192)
        gt_lo = at("gt_lo", [KFE, P], F32R, o_g + 8192 + KFE * 512)
        ye = at("ye", [D], F32, o_g + 8192 + KFE * 1024)
        o_r = o_g + 8192 + KFE * 1024 + 4096
        lg = at("lg", [3, NE], F32, o_r)
        cmp1 = at("cmp1", [3, NE, NE], F32, o_r + 128)
        cmp2 = at("cmp2", [3, NE, NE], F32, o_r + 896)
        rank = at("rank", [3, NE], F32, o_r + 1664)
        m1 = at("m1", [3, NE], F32, o_r + 1760)
        m2 = at("m2", [3, NE], F32, o_r + 1856)
        v12 = at("v12", [4, 3], F32, o_r + 1952)
        pos = at("pos", [3, NV + 1], F32, o_r + 2048)
        msk = at("msk", [3, NV + 1], F32, o_r + 2368)
        gts = at("gts", [3, NV + 1], F32, o_r + 2688)
        cmax = at("cmax", [1], F32, o_r + 3008)
        cmax_i = at("cmax_i", [1], I32, o_r + 3072)
        assert o_r + 3104 <= tail

        ps = ctx.enter_context(nc.psum_tensor("ps", [P, 8, 512], F32))

        small_in = sem("small_in")
        x_in = sem("x_in")
        mem_in = sem("mem_in")
        prev_in = sem("prev_in")
        landed = [sem(f"landed{s}") for s in range(RAW)]
        kv_out = sem("kv_out")
        kv_in = sem("kv_in")
        out_done = sem("out_done")
        x_out = sem("x_out")
        hi_done = sem("hi_done")
        lo_done = sem("lo_done")
        full = sem("full")
        act_freed = sem("act_freed")
        dve_freed = sem("dve_freed")
        chain = sem("chain")
        sq_done = sem("sq_done")
        rt_done = sem("rt_done")
        h_done = sem("h_done")
        hh_done = sem("hh_done")
        hl_done = sem("hl_done")
        sp_abs = sem("sp_abs")
        sp_exp = sem("sp_exp")
        sp_sum = sem("sp_sum")
        sp_ln = sem("sp_ln")
        acc_done = sem("acc_done")
        rs_done = sem("rs_done")
        gelu_done = sem("gelu_done")
        cinit = sem("cinit")
        tap_done = sem("tap_done")
        xi_done = sem("xi_done")
        sqr_done = sem("sqr_done")
        xc_done = sem("xc_done")
        xch_done = sem("xch_done")
        xcl_done = sem("xcl_done")
        c8_done = sem("c8_done")
        a_done = sem("a_done")
        e2_done = sem("e2_done")
        q_done = sem("q_done")
        root_done = sem("root_done")
        hs_done = sem("hs_done")
        y_done = sem("y_done")
        yh_done = sem("yh_done")
        yl_done = sem("yl_done")
        resid = sem("resid")
        state_ready = sem("state_ready")
        sh_done = sem("sh_done")
        sl_done = sem("sl_done")
        zero_done = sem("zero_done")
        ah_done = sem("ah_done")
        max_done = sem("max_done")
        pn_done = sem("pn_done")
        fs_done = sem("fs_done")
        fg_done = sem("fg_done")
        fh_done = sem("fh_done")
        fl_done = sem("fl_done")
        prev_done = sem("prev_done")
        save_done = sem("save_done")
        cvo_done = sem("cvo_done")
        silu_done = sem("silu_done")
        adt_done = sem("adt_done")
        alog_exp = sem("alog_exp")
        ld_done = sem("ld_done")
        dec_done = sem("dec_done")
        xt_done = sem("xt_done")
        xd_done = sem("xd_done")
        cbm_done = sem("cbm_done")
        mask_done = sem("mask_done")
        ce_done = sem("ce_done")
        mt_done = sem("mt_done")
        sad_done = sem("sad_done")
        sb_done = sem("sb_done")
        sdr_done = sem("sdr_done")
        btm_done = sem("btm_done")
        sn_dec = sem("sn_dec")
        sn_done = sem("sn_done")
        yz_done = sem("yz_done")
        state_out = [sem(f"state_out{i}") for i in range(5)]
        ysq_done = sem("ysq_done")
        msk_done = sem("msk_done")
        xp_done = sem("xp_done")
        xpe_done = sem("xpe_done")
        cnt_done = sem("cnt_done")
        fin_done = sem("fin_done")

        class Pass:
            def __init__(self, c):
                def s(name):
                    return sem(f"{name}_{c}")
                self.landed = landed if c == 0 else [s(f"e_landed{i}") for i in range(RAW)]
                self.hi = s("e_hi")
                self.lo = s("e_lo")
                self.used = s("e_used")
                self.sel = s("e_sel")
                self.gather = s("e_gather")
                self.xh = s("e_xh")
                self.xl = s("e_xl")
                self.silu = s("e_silu")
                self.g = s("e_g")
                self.turn = s("e_turn")
                self.gh = s("e_gh")
                self.gl = s("e_gl")
                self.ye = s("e_ye")
                self.sgt = s("e_sgt")
                self.sg = s("e_sg")
                self.scat = s("e_scat")
                self.add = s("e_add")
                self.chain = s("e_chain")

        PASSES = [Pass(c) for c in range(2)]
        VIRTUAL = [(0, NE), (NE, 2 * NE)]
        block = ctx.enter_context(nc.Block())

        STATE_AT = NEED[KEY["y off", 0, 0]] - 1
        AHEAD = []
        for g in range(len(PLAN)):
            cap = NSTAT
            for i in reversed(range(2 * NB)):
                before = KEY["s state", i // 2 - 2, GROUPS - 1] if i >= 4 else KEY["s decay"]
                if before >= g:
                    cap = STATE_AT + i + RAW
            AHEAD.append(min(NEED[g] + HL - 1, cap))
            assert AHEAD[g] >= NEED[g]

        def bank(g, n=512, rows=P):
            return ps[0:rows, BANK[g], 0:n]

        def own(buf, n):
            return buf.rearrange("p (b x) -> p b x", x=n * 32 + TS)[:, :, 0:n * 32] \
                .rearrange("p b (j s) -> p b j s", s=32)[:, :, :, 0:TS]

        def by_sequence(ap3):
            return ap3.rearrange("p j (b t) -> p b j t", t=TS)

        def samples(ap2, width, first, n):
            return ap2.rearrange("p (b w) -> p b w", w=width)[:, :, first:first + n]

        CHUNK_GROUP = [g + (key[:2] in (("y off", 0), ("y off", 2)))
                       for g, (key, _, chunks) in enumerate(PLAN) for _ in range(chunks)]
        for j in range(KD):
            for c in range(-(-KF * j // 8) - (1 if KF * j % 8 else 0), -(-KF * (j + 1) // 8)):
                CHUNK_GROUP[NEED[KEY["f2", 0]] - -(-KF // 8) + c] = KEY["f2", j]
        for l in range(2):
            for nb in range(2):
                for c in range(4):
                    CHUNK_GROUP[NEED[KEY["v", l, nb, 1]] - 4 + c] = KEY["v", l, nb, 1]
        for kind in ("r", "i"):
            CHUNK_GROUP[NEED[KEY[kind, 0]] - 1] = KEY[kind, KD - 1]

        def overflow(eng):
            eng.wait_ge(cnt_done, 1)
            return eng.value_load(cmax_i[0:1, 0:1], min_val=0, max_val=NT)

        @block.sync
        def _(sp):
            sp.dma_start(memx[:, :, :], t["mem"]).then_inc(mem_in, 16)
            sp.dma_start(small[:, :], t["small"]).then_inc(small_in, 16)
            for i in range(NSTAT):
                if i >= RAW:
                    sp.wait_ge(lo_done, i - RAW + 1)
                    if 0 <= i - RAW - STATE_AT < 2 * NB:
                        sp.wait_ge(sn_dec, i - RAW - STATE_AT + 1)
                sp.dma_start(raw[:, i % RAW, :], t["stream"][i, :, :]).then_inc(landed[i % RAW], 16)
                if i == 2:
                    sp.dma_start(x[:, :, :], t["x"]).then_inc(x_in, 16)

            def experts(c):
                s = PASSES[c]
                with sp.Fori(0, VIRTUAL[c][1] // NE) as turn:
                    with sp.Fori(0, NE) as e:
                        for p in range(CPE):
                            src = t["experts"][bass.ds(e * CPE + p, 1), :, :].rearrange("a p n -> p (a n)")
                            sp.wait_ge(s.lo, turn * (NE * CPE) + e * CPE + p + 1)
                            sp.dma_start(raw[:, (NSTAT + p) % RAW, :], src) \
                                .then_inc(s.landed[(NSTAT + p) % RAW], 16)

            sp.wait_ge(lo_done, NSTAT)
            experts(0)
            over = overflow(sp)
            with sp.If(over > P):
                experts(1)
                sp.nop()
            sp.nop()

        @block.scalar
        def _(act):
            ptr = [0]

            def hi_upto(n):
                while ptr[0] < min(n, NSTAT):
                    k = ptr[0]
                    act.wait_ge(landed[k % RAW], 16 * (k // RAW + 1))
                    if k >= HL:
                        act.wait_ge(full, CHUNK_GROUP[k - HL] + 1)
                    act.activation(w_hi[:, k % HL, :], raw[:, k % RAW, :], ACT.Copy).then_inc(hi_done, 1)
                    ptr[0] += 1

            def ready(key, n=512, rows=P):
                g = KEY[key]
                hi_upto(AHEAD[g])
                act.wait_ge(full, g + 1)
                return bank(g, n, rows)

            def squares_and_hi(wait_tile, src, sq, hi, gain, first=0, last=KD):
                for j in range(first, last):
                    wait_tile(j)
                    act.activation(sq[:, j, :], src[:, j, :], ACT.Square).then_inc(sq_done, 1)
                    if gain is not None:
                        act.activation(hi[:, j, :], src[:, j, :], ACT.Identity, scale=gain[:, j:j + 1]) \
                            .then_inc(hh_done, 1)

            def residual(key, gain):
                def wait_tile(j):
                    hi_upto(AHEAD[KEY[key + (j,)]])
                    act.wait_ge(dve_freed, FREED[KEY[key + (j,)]][1])
                squares_and_hi(wait_tile, x, h, h_hi, gain)

            def root(key, buf, n):
                b = ready(key, n)
                act.activation(buf[:, 0:n], b, ACT.Sqrt, bias=eps[:, 0:1], scale=1.0 / D).then_inc(act_freed, 1)

            def few(key, cols):
                b = ready(key + " t", NT, cols)
                act.activation(small_t[0:cols, :], b, ACT.Copy).then_inc(act_freed, 1)

            def values(l):
                for nb in range(2):
                    for m in range(2):
                        b = ready(("v", l, nb, m))
                        act.activation(vmem[l][:, m, nb * 512:(nb + 1) * 512], b, ACT.Identity,
                                       scale=rm[:, NMEM + m:NMEM + m + 1]).then_inc(act_freed, 1)
                act.wait_ge(act_freed, FREED[KEY["v", l, 1, 1]][1])
                act.dma_start(t["out_v"][l], vmem[l][:, :, :]).then_inc(kv_out, 16)

            def gains(name, l):
                return par(name)[:, l * KD:(l + 1) * KD]

            act.wait_ge(mem_in, 16)
            act.wait_ge(small_in, 16)
            for j in range(KD):
                act.activation(mem_hi[0][:, j, :], memx[:, j, :], ACT.Identity,
                               scale=gains("g_memkv", 0)[:, j:j + 1]).then_inc(hh_done, 1)
                if j == 3:
                    hi_upto(1)
            for j in range(KD):
                act.activation(memsq[:, j, :], memx[:, j, :], ACT.Square).then_inc(sq_done, 1)
            root("mem norm", rmt, NMEM + 2)
            for j in range(KD):
                hi_upto(AHEAD[KEY["k", 0, j]])
                if j < 4:
                    for k in (2 * j, 2 * j + 1):
                        act.activation(mem_hi[1][:, k, :], memx[:, k, :], ACT.Identity,
                                       scale=gains("g_memkv", 1)[:, k:k + 1]).then_inc(hh_done, 1)
                else:
                    act.wait_ge(x_in, 16)
                    squares_and_hi(lambda j: None, x, h, h_hi, gains("g_mix", 0), 2 * j - 8, 2 * j - 6)
            act.wait_ge(dve_freed, FREED[KEY["k", 0, KD - 1]][1])
            act.dma_start(t["out_k"][0], kmem[0][:, :, :]).then_inc(kv_out, 16)
            act.wait_ge(rs_done, 1)
            values(0)
            act.wait_ge(sp_abs, 1)
            act.activation(sp[:, 1, 0:KD], sp[:, 0, 0:KD], ACT.Exp, scale=-1.0).then_inc(sp_exp, 1)
            act.wait_ge(sp_sum, 1)
            act.activation(sp[:, 3, 0:KD], sp[:, 2, 0:KD], ACT.Ln).then_inc(sp_ln, 1)
            root(("norm", 0), rt, NT)
            for j in range(KD):
                hi_upto(AHEAD[KEY["gate", j]])
                act.wait_ge(dve_freed, FREED[KEY["gate", j]][1])
                act.activation(gate[:, j, :], gate[:, j, :], ACT.Gelu_apprx_tanh).then_inc(gelu_done, 1)

            def first_tap(j):
                hi_upto(AHEAD[KEY["xb", j]])
                act.wait_ge(dve_freed, FREED[KEY["xb", j]][1])
                if j >= 2:
                    act.wait_ge(xc_done, j - 1)
                act.activation(conv_t[:, j % 2, 0:PADW - CW + 1], conv[:, j, 0:PADW - CW + 1], ACT.Identity,
                               scale=par("lru_cw")[:, 4 * j:4 * j + 1], bias=par("lru_cb")[:, j:j + 1]) \
                    .then_inc(tap_done, 1)

            first_tap(0)
            for j in range(KD):
                if j + 1 < KD:
                    first_tap(j + 1)
                act.wait_ge(xc_done, j + 1)
                act.activation(xc_hi[:, j, :], xc[:, j, :], ACT.Copy).then_inc(xch_done, 1)
            hi_upto(AHEAD[KEY["k", 1, EARLY - 1]])
            for j in range(KD):
                b = ready(("r", j), NT)
                act.activation(rg[:, j, :], b, ACT.Sigmoid, bias=par("b_a")[:, j:j + 1]).then_inc(act_freed, 1)
            for j in range(KD):
                b = ready(("i", j), NT)
                act.activation(ig[:, j, :], b, ACT.Sigmoid, bias=par("b_x")[:, j:j + 1]).then_inc(act_freed, 1)
            act.wait_ge(c8_done, 1)
            act.wait_ge(act_freed, FREED[KEY["r", KD - 1]][1])
            for j in range(KD):
                hi_upto(AHEAD[KEY["k", 1, max(j, EARLY)]])
                for k in (2 * (j % 4), 2 * (j % 4) + 1):
                    if j < 4:
                        act.activation(decay[:, k, :], rg[:, k, :], ACT.Exp, scale=nc8[:, k:k + 1]) \
                            .then_inc(a_done, 1)
                        act.wait_ge(xi_done, k + 1)
                        act.activation(tanh[:, k, :], rg[:, k, :], ACT.Tanh, scale=nc8[:, k:k + 1]) \
                            .then_inc(e2_done, 1)
                    else:
                        act.wait_ge(q_done, k + 1)
                        act.activation(expm[:, k, :], expm[:, k, :], ACT.Sqrt, scale=-1.0).then_inc(root_done, 1)
            act.wait_ge(dve_freed, FREED[KEY["k", 1, KD - 1]][1])
            act.dma_start(t["out_k"][1], kmem[1][:, :, :]).then_inc(kv_out, 16)
            hi_upto(AHEAD[KEY["v", 1, 0, 0]])
            for j in range(KD):
                act.wait_ge(y_done, j + 1)
                act.activation(xc_hi[:, j, :], y_lru[:, j, :], ACT.Copy).then_inc(yh_done, 1)
            values(1)
            act.wait_ge(kv_out, 64)
            residual(("lru out",), gains("g_mem", 0))

            def attention(l):
                root(("norm", 3 * l + 1), rt, NT)
                hi_upto(AHEAD[KEY["q", l, KD - 1]])
                act.wait_ge(dve_freed, FREED[KEY["q", l, KD - 1]][1])
                act.wait_ge(zero_done, 1 + 3 * l)
                act.activation(own(qm[0], KD), by_sequence(q[:, :, SEQ:NT]), ACT.Copy).then_inc(sh_done, 1)
                act.wait_ge(kv_in, 32 * (l + 1))
                for hd in range(MH):
                    b = ready(("scores", l, hd))
                    act.wait_ge(max_done, 6 * l + hd + 1)
                    for tt in range(2):
                        k = 2 * hd + tt
                        a = act.activation(pr[:, k, :], b[:, tt * NMEM:(tt + 1) * NMEM], ACT.Exp,
                                           bias=nmx[:, k:k + 1], scale=1.0 / 16, accum_out=rsum[:, k:k + 1])
                    a.then_inc(act_freed, 1)
                for half in range(2):
                    b = ready(("s scores", l, half, NB - 1), 512, 32)
                    act.wait_ge(max_done, 6 * l + 4 + half + 1)
                    for hd in (2 * half, 2 * half + 1):
                        a = act.activation(prs[0:32, hd, :], b[:, (hd % 2) * NMEM:(hd % 2 + 1) * NMEM], ACT.Exp,
                                           bias=nmx[0:32, 8 + hd:9 + hd], scale=1.0 / 16,
                                           accum_out=rsum[0:32, 8 + hd:9 + hd])
                    a.then_inc(act_freed, 1)
                for j in range(KD):
                    b = ready(("o", l, j), SEQ)
                    act.activation(att_hi[:, j, 0:SEQ], b, ACT.Copy).then_inc(ah_done, 1)
                b = ready(("s probs", l), NMEM)
                act.wait_ge(zero_done, 2 + 3 * l)
                for m in range(2):
                    a = act.activation(own(pm[0][:, m, :], MH), by_sequence(
                        b[:, m * P:(m + 1) * P].rearrange("p (h s) -> p h s", h=MH)), ACT.Copy)
                a.then_inc(sh_done, 1)
                for half in range(2):
                    b = ready(("s o", l, half, NB - 1), 512, 32)
                    act.activation(so[0:32, half * 512:(half + 1) * 512], b, ACT.Copy).then_inc(act_freed, 1)
                b = ready(("s o turn", l), NMEM)
                act.activation(att_hi[:, :, SEQ:NT], b.rearrange("p (j s) -> p j s", j=KD), ACT.Copy) \
                    .then_inc(ah_done, 1)

            attention(0)
            residual(("mem out", 0), gains("g_ffn", 0))
            root(("norm", 2), rt, NT)
            for f in range(KF):
                hi_upto(AHEAD[KEY["f1", f]])
                act.wait_ge(dve_freed, FREED[KEY["f1", f]][1])
                act.activation(f_s[:, f % 2, :], f_s[:, f % 2, :], ACT.Silu).then_inc(fs_done, 1)
                if f >= 1:
                    act.wait_ge(fg_done, f)
                    act.activation(f_hi[:, f - 1, :], f_g[:, (f - 1) % 2, :], ACT.Copy).then_inc(fh_done, 1)
                hi_upto(AHEAD[KEY["f3", f]])
            act.wait_ge(fg_done, KF)
            act.activation(f_hi[:, KF - 1, :], f_g[:, (KF - 1) % 2, :], ACT.Copy).then_inc(fh_done, 1)
            residual(("f2",), None)

            root(("norm", 3), rt, NT)
            for j in range(KD):
                act.wait_ge(h_done, j + 1)
                act.activation(h_hi[:, j, :], h[:, j, :], ACT.Copy).then_inc(hh_done, 1)

            def step_sizes():
                few("dt", HEADS)
                hi_upto(AHEAD[KEY["dt"]])
                act.wait_ge(sp_abs, 2)
                act.activation(sp[:, 1, :], sp[:, 0, :], ACT.Exp, scale=-1.0).then_inc(sp_exp, 1)
                act.activation(last_dec[:, :], par("a_log"), ACT.Exp).then_inc(alog_exp, 1)
                act.wait_ge(sp_sum, 2)
                act.activation(sp[:, 3, :], sp[:, 2, :], ACT.Ln).then_inc(sp_ln, 1)

            def silu_tile(c):
                act.wait_ge(cvo_done, c + 1)
                dst = y[:, c, :] if c < KI else bc[:, c - KI, :]
                act.activation(dst, cv_o[:, c % 2, :], ACT.Silu).then_inc(silu_done, 1)

            for c in range(NXBC):
                b = ready(("xbc", c), NT)
                act.wait_ge(prev_done, c + 1)
                act.activation(cv[:, c % 3, CW - 1:PS0], b[:, 0:SEQ], ACT.Copy)
                act.activation(samples(cv[:, c % 3, PS0:PADW], TS + CW - 1, CW - 1, TS),
                               b[:, SEQ:NT].rearrange("p (b w) -> p b w", w=TS), ACT.Copy) \
                    .then_inc(act_freed, 1)
                act.wait_ge(act_freed, FREED[KEY["xbc", c]][1])
                if c >= 2:
                    act.wait_ge(cvo_done, c - 1)
                act.activation(cv_t[:, c % 2, 0:PADW - CW + 1], cv[:, c % 3, 0:PADW - CW + 1], ACT.Identity,
                               scale=par("ssd_cw")[:, 4 * c:4 * c + 1], bias=par("ssd_cb")[:, c:c + 1]) \
                    .then_inc(tap_done, 1)
                if c >= 1:
                    silu_tile(c - 1)
                if c == 2:
                    step_sizes()
            silu_tile(NXBC - 1)
            for c in range(KI):
                b = ready(("z", c), NT)
                act.activation(zs[:, c, :], b, ACT.Silu).then_inc(act_freed, 1)
            act.wait_ge(out_done, 48)
            for tt, (c0, n) in enumerate(TOK):
                act.wait_ge(ld_done, tt + 1)
                act.activation(dec[0:n, :], dec[0:n, :], ACT.Exp).then_inc(dec_done, 1)
                if tt == 1:
                    act.activation(cdec[:, :], last_dec[:, :], ACT.Exp).then_inc(dec_done, 1)
                elif tt == 2:
                    act.activation(ea[0:n, :], acs[0:n, :], ACT.Exp).then_inc(dec_done, 1)
                b = ready(("bt", tt), rows=n)
                act.activation(bt[0:n, :], b, ACT.Copy).then_inc(act_freed, 1)

                def state_part(hb):
                    b = ready(("state ab", hb))
                    if hb:
                        act.wait_ge(ce_done, hb)
                    act.activation(eb[:, :], b, ACT.Exp).then_inc(act_freed, 1)

                for hb in range(8):
                    k = tt * 8 + hb
                    b = ready(("ab", tt, hb), 4 * n, n)
                    if k >= 4:
                        act.wait_ge(full, KEY["y", (k - 4) // 8, (k - 4) % 8] + 1)
                    for j in range(4):
                        a = act.activation(mt[k % 4][0:n, j * n:(j + 1) * n], b[:, j * n:(j + 1) * n], ACT.Exp,
                                           bias=nacs[0:n, 4 * hb + j:4 * hb + j + 1])
                    a.then_inc(act_freed, 1)
                    if tt == 1:
                        state_part(hb)
                if tt == 0:
                    for g in range(GROUPS):
                        b = ready(("state", 0, g))
                        act.activation(s_a[:, g * 512:(g + 1) * 512], b, ACT.Copy).then_inc(act_freed, 1)
            b = ready("s decay", NB * HEADS)
            act.activation(sdec[:, :], b, ACT.Exp).then_inc(act_freed, 1)
            act.wait_ge(zero_done, 3)
            act.activation(own(cm[0], GROUPS), by_sequence(bc[:, 4:8, SEQ:NT]), ACT.Copy).then_inc(sh_done, 1)
            for b_ in range(NB):
                tiles = slice(2 * b_, 2 * b_ + 2)
                hi_upto(AHEAD[KEY["s state", b_, 0]])
                act.wait_ge(yz_done, b_ + 1)
                act.activation(ysq[:, tiles, 0:SEQ], y[:, tiles, 0:SEQ], ACT.Square).then_inc(ysq_done, 1)
            hi_upto(AHEAD[KEY["gn", 0]])
            act.wait_ge(yz_done, NB + 1)
            act.activation(ysq[:, :, SEQ:NT], y[:, :, SEQ:NT], ACT.Square).then_inc(ysq_done, 1)
            for g in range(GROUPS):
                b = ready(("gn", g), NT)
                act.activation(grt[:, g, :], b, ACT.Sqrt, bias=eps[:, 0:1], scale=GROUPS / DI) \
                    .then_inc(act_freed, 1)
            for g in range(GROUPS):
                act.wait_ge(y_done, KD + g + 1)
                act.activation(y_hi[:, 4 * g:4 * g + 4, :], y[:, 4 * g:4 * g + 4, :], ACT.Copy) \
                    .then_inc(yh_done, 1)
            residual(("ssd out",), gains("g_mem", 1))
            attention(1)
            residual(("mem out", 1), None)
            root(("norm", 5), rt, NT)
            act.wait_ge(h_done, KD + 1)
            few("logits", NE)
            for i in range(6):
                rows = TOK[i // 2][1]
                b = ready(("ht", i), rows=rows)
                act.activation(htok[0:rows, i // 2, (i % 2) * 512:(i % 2 + 1) * 512], b, ACT.Copy) \
                    .then_inc(act_freed, 1)
            act.wait_ge(xp_done, 1)
            act.activation(v12[:, 3, :], v12[:, 2, :], ACT.Exp).then_inc(xpe_done, 1)

            def experts(c):
                s = PASSES[c]
                def hi(e, p):
                    slot = (NSTAT + p) % RAW
                    first = 16 * ((NSTAT + p) // RAW) if c == 0 else 16 * (p // RAW)
                    act.wait_ge(s.landed[slot], e * (16 * CPE // RAW) + first + 16)
                    act.wait_ge(s.used, e * CPE + p + 1)
                    act.activation(w_hi[:, (NSTAT + p) % HL, :], raw[:, slot, :], ACT.Copy) \
                        .then_inc(s.hi, 1)

                nv = VIRTUAL[c][1]
                act.wait_ge(s.gather, 1)
                act.activation(xe_hi[:, :], ps[:, 0:2, :], ACT.Copy).then_inc(s.xh, 1)
                with act.Fori(0, nv) as e:
                    done = 0

                    def ahead(n):
                        nonlocal done
                        while done < min(n, CPE):
                            hi(e, done)
                            done += 1

                    ahead(HL - 1)
                    act.wait_ge(s.used, e * CPE + HL)
                    act.activation(ye[:, :], ps[:, 5:7, :], ACT.Copy).then_inc(s.ye, 1)
                    for f in range(FB):
                        ahead(8 * f + 4 + HL - 1)
                        act.wait_ge(s.used, e * CPE + 8 * f + 4 + HL)
                        act.wait_ge(s.g, e * FB + f + 1)
                        act.activation(sil[:, f % 2, :], ps[:, f % 2, :], ACT.Silu).then_inc(s.silu, 1)
                        if f >= 1:
                            ahead(8 * f + 4 + HL)
                            act.wait_ge(s.turn, e * FB + f)
                            act.activation(gt_hi[:, 4 * f - 4:4 * f, :], ps[:, 4, :], ACT.Copy) \
                                .then_inc(s.gh, 1)
                    ahead(8 * FB + 2 + HL - 1)
                    act.wait_ge(s.turn, e * FB + FB)
                    act.activation(gt_hi[:, 4 * FB - 4:4 * FB, :], ps[:, 4, :], ACT.Copy).then_inc(s.gh, 1)
                    ahead(8 * FB + 16 + HL - 1)
                    act.wait_ge(s.gather, e + 2)
                    act.activation(xe_hi[:, :], ps[:, 0:2, :], ACT.Copy).then_inc(s.xh, 1)
                    ahead(CPE)
                act.wait_ge(s.used, nv * CPE + HL)
                act.activation(ye[:, :], ps[:, 5:7, :], ACT.Copy).then_inc(s.ye, 1)

            experts(0)
            over = overflow(act)
            with act.If(over > P):
                experts(1)
                act.nop()
            act.wait_ge(resid, 1)
            squares_and_hi(lambda j: None, x, h, None, None)
            act.wait_ge(full, len(PLAN) + 1)
            act.activation(rt[:, :], ps[:, 0, 0:NT], ACT.Sqrt, bias=eps[:, 0:1], scale=1.0 / D) \
                .then_inc(rt_done, 1)
            for half in range(2):
                tiles = slice(4 * half, 4 * half + 4)
                act.wait_ge(fin_done, half + 1)
                act.dma_start(t["out_x"][:, tiles, :], h[:, tiles, :]).then_inc(x_out, 16)
            act.wait_ge(x_out, 32)

        @block.vector
        def _(dve):
            ptr, steps = [0], [0]

            def lo_upto(n):
                while ptr[0] < min(n, NSTAT):
                    k = ptr[0]
                    dve.wait_ge(hi_done, k + 1)
                    dve.tensor_tensor(w_lo[:, k % HL, :], raw[:, k % RAW, :],
                                      w_hi[:, k % HL, :].bitcast(F32), ALU.subtract).then_inc(lo_done, 1)
                    ptr[0] += 1

            def ready(key, n=512, rows=P):
                g = KEY[key]
                lo_upto(AHEAD[g])
                dve.wait_ge(full, g + 1)
                return bank(g, n, rows)

            def act_read(key):
                lo_upto(AHEAD[KEY[key]])
                dve.wait_ge(act_freed, FREED[KEY[key]][1])

            def link(ins):
                steps[0] += 1
                ins.then_inc(chain, 1)
                dve.wait_ge(chain, steps[0])

            def lo_half(dst, src, hi, done):
                dve.tensor_tensor(dst, src, hi.bitcast(F32), ALU.subtract).then_inc(done, 1)

            def scaled_lo(lo, src, gain, hi, j, count):
                dve.wait_ge(hh_done, count)
                dve.scalar_tensor_tensor(lo[:, j, :], src[:, j, :], gain[:, j:j + 1], hi[:, j, :].bitcast(F32),
                                         ALU.mult, ALU.subtract).then_inc(hl_done, 1)

            def inverse(n):
                link(dve.reciprocal(rs[:, :], rt[:, :]))
                dve.engine_nop().then_inc(rs_done, 1)

            def residual(key, gain, count=None):
                for j in range(KD):
                    b = ready(key + (j,), NT)
                    dve.tensor_tensor(x[:, j, :], x[:, j, :], b, ALU.add).then_inc(dve_freed, 1)
                    if gain is not None and j:
                        scaled_lo(h_lo, x, gain, h_hi, j - 1, count + j)
                    if (key, j) == (("mem out", 1), 1):
                        lo_upto(NSTAT)
                        dve.wait_ge(lo_done, NSTAT)
                        dve.engine_nop().then_inc(PASSES[0].lo, RAW)
                if gain is not None:
                    scaled_lo(h_lo, x, gain, h_hi, KD - 1, count + KD)

            def gains(name, l):
                return par(name)[:, l * KD:(l + 1) * KD]

            def softplus(z, n, turn):
                dve.scalar_tensor_tensor(sp[:, 0, 0:n], z, -1.0, z, ALU.mult, ALU.max).then_inc(sp_abs, 1)
                dve.wait_ge(sp_exp, turn)
                dve.tensor_scalar(sp[:, 2, 0:n], sp[:, 1, 0:n], 1.0, None, ALU.add).then_inc(sp_sum, 1)
                dve.wait_ge(sp_sum, turn)
                link(dve.tensor_scalar(sp[:, 4, 0:n], sp[:, 2, 0:n], -1.0, None, ALU.add))
                link(dve.tensor_scalar(sp[:, 5, 0:n], sp[:, 4, 0:n], 0.0, None, ALU.is_equal))
                link(dve.tensor_tensor(sp[:, 4, 0:n], sp[:, 4, 0:n], sp[:, 5, 0:n], ALU.add))
                link(dve.reciprocal(sp[:, 4, 0:n], sp[:, 4, 0:n]))
                dve.wait_ge(sp_ln, turn)
                link(dve.tensor_tensor(sp[:, 5, 0:n], sp[:, 3, 0:n], sp[:, 5, 0:n], ALU.add))
                link(dve.tensor_tensor(sp[:, 5, 0:n], sp[:, 5, 0:n], sp[:, 4, 0:n], ALU.mult))
                link(dve.tensor_tensor(sp[:, 5, 0:n], sp[:, 5, 0:n], sp[:, 1, 0:n], ALU.mult))
                link(dve.scalar_tensor_tensor(z, z, 0.0, sp[:, 5, 0:n], ALU.max, ALU.add))

            def conv_tile(out, src, tmp, w, done):
                n = PADW - CW + 1
                for k in range(1, CW - 1):
                    link(dve.scalar_tensor_tensor(tmp[:, 0:n], src[:, k:k + n], w[:, k:k + 1], tmp[:, 0:n],
                                                  ALU.mult, ALU.add))
                k = CW - 1
                dve.scalar_tensor_tensor(out[:, 0:SEQ], src[:, k:k + SEQ], w[:, k:k + 1], tmp[:, 0:SEQ],
                                         ALU.mult, ALU.add)
                dve.scalar_tensor_tensor(out[:, SEQ:NT].rearrange("p (b w) -> p b w", w=TS),
                                         samples(src[:, PS0:PADW], TS + CW - 1, k, TS), w[:, k:k + 1],
                                         samples(tmp[:, PS0:PADW], TS + CW - 1, 0, TS),
                                         ALU.mult, ALU.add).then_inc(done, 1)

            dve.wait_ge(small_in, 16)
            for j in range(KD):
                scaled_lo(mem_lo[0], memx, gains("g_memkv", 0), mem_hi[0], j, j + 1)
                if j == 4:
                    lo_upto(1)
            act_read("mem norm")
            link(dve.reciprocal(rm[:, :], rmt[:, :]))
            dve.engine_nop().then_inc(rs_done, 1)

            def key_tile(l, j):
                b = ready(("k", l, j), NMEM)
                dve.tensor_tensor(kmem[l][:, j, :], b, rm[:, 0:NMEM], ALU.mult).then_inc(dve_freed, 1)

            for j in range(KD):
                key_tile(0, j)
                for k in (2 * (j % 4), 2 * (j % 4) + 1):
                    if j < 4:
                        scaled_lo(mem_lo[1], memx, gains("g_memkv", 1), mem_hi[1], k, KD + k + 1)
                    else:
                        scaled_lo(h_lo, x, gains("g_mix", 0), h_hi, k, 2 * KD + k + 1)
            lo_upto(AHEAD[KEY["v", 0, 1, 1]])
            link(dve.tensor_scalar(nc8[:, :], par("lam"), -1.0, None, ALU.mult))
            softplus(nc8[:, :], KD, 1)
            dve.tensor_scalar(nc8[:, :], nc8[:, :], -8.0, None, ALU.mult).then_inc(c8_done, 1)

            act_read(("norm", 0))
            inverse(0)
            dve.wait_ge(kv_out, 32)
            for j in range(KD):
                b = ready(("gate", j), NT)
                dve.tensor_tensor(gate[:, j, :], b, rs[:, :], ALU.mult).then_inc(dve_freed, 1)
            dve.wait_ge(cinit, 1)

            def conv_lo(j):
                dve.wait_ge(xch_done, j + 1)
                lo_half(xc_lo[:, j, :], xc[:, j, :], xc_hi[:, j, :], xcl_done)

            def conv_input(j):
                b = ready(("xb", j), NT)
                dve.tensor_tensor(conv[:, j, CW - 1:PS0], b[:, 0:SEQ], rs[:, 0:SEQ], ALU.mult)
                dve.tensor_tensor(samples(conv[:, j, PS0:PADW], TS + CW - 1, CW - 1, TS),
                                  b[:, SEQ:NT].rearrange("p (b w) -> p b w", w=TS),
                                  rs[:, SEQ:NT].rearrange("p (b w) -> p b w", w=TS), ALU.mult) \
                    .then_inc(dve_freed, 1)

            conv_input(0)
            for j in range(KD):
                if j + 1 < KD:
                    conv_input(j + 1)
                dve.wait_ge(tap_done, j + 1)
                conv_tile(xc[:, j, :], conv[:, j, :], conv_t[:, j % 2, :], par("lru_cw")[:, 4 * j:4 * j + 4], xc_done)
                if j:
                    conv_lo(j - 1)
            conv_lo(KD - 1)
            for j in range(EARLY):
                key_tile(1, j)
            for j in range(KD):
                act_read(("i", j))
                dve.tensor_tensor(xc[:, j, :], xc[:, j, :], ig[:, j, :], ALU.mult).then_inc(xi_done, 1)
            dve.wait_ge(xi_done, KD)
            for j in range(KD):
                if j >= EARLY:
                    key_tile(1, j)
                for k in (2 * (j % 4), 2 * (j % 4) + 1):
                    if j < 4:
                        dve.wait_ge(sqr_done, k + 1)
                        dve.wait_ge(e2_done, k + 1)
                        dve.scalar_tensor_tensor(expm[:, k, :], expm[:, k, :], 1.0, tanh[:, k, :],
                                                 ALU.add, ALU.mult).then_inc(q_done, 1)
                    else:
                        dve.wait_ge(root_done, k + 1)
                        link(dve.tensor_tensor(xc[:, k, :], xc[:, k, :], expm[:, k, :], ALU.mult))
                        dve.tensor_tensor_scan(xc[:, k, 0:SEQ], decay[:, k, 0:SEQ], xc[:, k, 0:SEQ], 0.0,
                                               ALU.mult, ALU.add)

            def tok(buf, k):
                return buf[:, :, SEQ:NT].rearrange("p j (b w) -> p j b w", w=TS)[:, :, :, k]

            before = par("h_prev").rearrange("p (j b) -> p j b", b=NB)
            for k in range(TS):
                link(dve.tensor_tensor(hs_t[:, :, :], tok(decay, k), before, ALU.mult))
                a = dve.tensor_tensor(tok(xc, k), hs_t[:, :, :], tok(xc, k), ALU.add)
                if k < TS - 1:
                    link(a)
                else:
                    a.then_inc(hs_done, 1)
                before = tok(xc, k)
            dve.wait_ge(hs_done, 1)
            dve.wait_ge(gelu_done, KD)
            for j in range(KD + 1):
                if j < KD:
                    dve.tensor_tensor(y_lru[:, j, :], xc[:, j, :], gate[:, j, :], ALU.mult).then_inc(y_done, 1)
                if j:
                    dve.wait_ge(yh_done, j)
                    lo_half(xc_lo[:, j - 1, :], y_lru[:, j - 1, :], xc_hi[:, j - 1, :], yl_done)
            residual(("lru out",), gains("g_mem", 0), 3 * KD)

            def attention(l):
                act_read(("norm", 3 * l + 1))
                inverse(3 * l + 1)
                for j in range(KD):
                    b = ready(("q", l, j), NT)
                    dve.tensor_tensor(q[:, j, :], b, rs[:, :], ALU.mult).then_inc(dve_freed, 1)
                dve.wait_ge(sh_done, 1 + 3 * l)
                lo_half(own(qm[1], KD), by_sequence(q[:, :, SEQ:NT]), own(qm[0], KD), sl_done)
                for hd in range(MH):
                    b = ready(("scores", l, hd))
                    link(dve.tensor_reduce(mx[:, 2 * hd:2 * hd + 2],
                                           b.rearrange("p (a m) -> p a m", a=2), AX.X, ALU.max))
                    dve.tensor_scalar(nmx[:, 2 * hd:2 * hd + 2], mx[:, 2 * hd:2 * hd + 2], -1.0 / 16, None,
                                      ALU.mult).then_inc(max_done, 1)
                act_read(("scores", l, MH - 1))
                link(dve.reciprocal(rinv[:, 0:8], rsum[:, 0:8]))
                dve.tensor_tensor(pr[:, 0:8, :], pr[:, 0:8, :],
                                  rinv[:, 0:8].unsqueeze(2).broadcast_to([P, 8, NMEM]), ALU.mult) \
                    .then_inc(pn_done, 1)
                for i in range(4):
                    b = ready(("probs", l, i))
                    dve.tensor_copy(prt[:, i // 2, 2 * (i % 2):2 * (i % 2) + 2, :], b).then_inc(dve_freed, 1)
                for half in range(2):
                    b = ready(("s scores", l, half, NB - 1), 512, 32)
                    heads = slice(8 + 2 * half, 10 + 2 * half)
                    link(dve.tensor_reduce(mx[0:32, heads], b.rearrange("p (a m) -> p a m", a=2), AX.X, ALU.max))
                    dve.tensor_scalar(nmx[0:32, heads], mx[0:32, heads], -1.0 / 16, None, ALU.mult) \
                        .then_inc(max_done, 1)
                act_read(("s scores", l, 1, NB - 1))
                link(dve.reciprocal(rinv[0:32, 8:12], rsum[0:32, 8:12]))
                dve.tensor_tensor(prs[0:32, :, :], prs[0:32, :, :],
                                  rinv[0:32, 8:12].unsqueeze(2).broadcast_to([32, MH, NMEM]), ALU.mult) \
                    .then_inc(pn_done, 1)
                for j in range(KD):
                    b = ready(("o", l, j), SEQ)
                    dve.wait_ge(ah_done, (KD + 1) * l + j + 1)
                    lo_half(att_lo[:, j, 0:SEQ], b, att_hi[:, j, 0:SEQ], dve_freed)
                b = ready(("s probs", l), NMEM)
                dve.wait_ge(sh_done, 2 + 3 * l)
                for m in range(2):
                    a = dve.tensor_tensor(own(pm[1][:, m, :], MH), by_sequence(
                        b[:, m * P:(m + 1) * P].rearrange("p (h s) -> p h s", h=MH)),
                        own(pm[0][:, m, :], MH).bitcast(F32), ALU.subtract)
                a.then_inc(sl_done, 1)
                dve.engine_nop().then_inc(dve_freed, 1)
                b = ready(("s o turn", l), NMEM)
                dve.wait_ge(ah_done, (KD + 1) * (l + 1))
                lo_half(att_lo[:, :, SEQ:NT], b.rearrange("p (j s) -> p j s", j=KD), att_hi[:, :, SEQ:NT], dve_freed)

            attention(0)
            residual(("mem out", 0), gains("g_ffn", 0), 4 * KD)

            act_read(("norm", 2))
            inverse(2)

            def gated_lo(f):
                dve.wait_ge(fh_done, f + 1)
                lo_half(f_lo[:, f, :], f_g[:, f % 2, :], f_hi[:, f, :], fl_done)

            for f in range(KF):
                b = ready(("f1", f), NT)
                if f >= 2:
                    dve.wait_ge(fg_done, f - 1)
                dve.tensor_tensor(f_s[:, f % 2, :], b, rs[:, :], ALU.mult).then_inc(dve_freed, 1)
                if f:
                    gated_lo(f - 1)
                b = ready(("f3", f), NT)
                link(dve.tensor_tensor(f_g[:, f % 2, :], b, rs[:, :], ALU.mult))
                dve.engine_nop().then_inc(dve_freed, 1)
                dve.wait_ge(fs_done, f + 1)
                dve.tensor_tensor(f_g[:, f % 2, :], f_g[:, f % 2, :], f_s[:, f % 2, :], ALU.mult).then_inc(fg_done, 1)
            gated_lo(KF - 1)
            residual(("f2",), None)

            act_read(("norm", 3))
            inverse(3)
            for k in range(KD + 1):
                if k < KD:
                    dve.scalar_tensor_tensor(h[:, k, :], x[:, k, :], gains("g_mix", 1)[:, k:k + 1], rs[:, :],
                                             ALU.mult, ALU.mult).then_inc(h_done, 1)
                if k:
                    dve.wait_ge(hh_done, 5 * KD + k)
                    lo_half(h_lo[:, k - 1, :], h[:, k - 1, :], h_hi[:, k - 1, :], hl_done)

            def step_sizes():
                b = ready("dt", 96)
                link(dve.memset(dt[:, :, :], 0.0))
                dtb = par("dt_b")
                dve.tensor_tensor(dt[:, 0:2, :], b[:, 0:64].rearrange("p (a m) -> p a m", a=2),
                                  dtb.unsqueeze(1).broadcast_to([P, 2, HEADS]), ALU.add)
                link(dve.tensor_tensor(dt[0:32, 2, :], b[0:32, 64:96], dtb[0:32, :], ALU.add))
                dve.engine_nop().then_inc(dve_freed, 1)
                softplus(dt[:, :, :].rearrange("p a m -> p (a m)"), 96, 2)
                dve.wait_ge(alog_exp, 1)
                for k in range(3):
                    a = dve.scalar_tensor_tensor(adt[:, k, :], dt[:, k, :], -1.0, last_dec[:, :],
                                                 ALU.mult, ALU.mult)
                a.then_inc(adt_done, 1)

            for c in range(NXBC):
                act_read(("xbc", c))
                if c >= 2:
                    dve.wait_ge(silu_done, c - 1)
                dve.wait_ge(tap_done, KD + c + 1)
                conv_tile(cv_o[:, c % 2, :], cv[:, c % 3, :], cv_t[:, c % 2, :], par("ssd_cw")[:, 4 * c:4 * c + 4],
                          cvo_done)
                if c == 2:
                    step_sizes()
            act_read(("z", KI - 1))
            dve.wait_ge(out_done, 48)
            dve.tensor_copy(ident_r[:, :], ident)
            dve.tensor_copy(tri_r[:, :], tri)
            dve.tensor_copy(tri_sr[0:32, :], par("tri_s")[0:32, :])
            dve.wait_ge(adt_done, 1)
            link(dve.tensor_copy(adt_s[0][:, :, :], adt[:, :, :]))
            dve.tensor_tensor(adt_s[1][:, :, :], adt[:, :, :], adt_s[0][:, :, :].bitcast(F32), ALU.subtract)
            dve.tensor_scalar(future_r[:, :], tri, -1.0, -NEVER, ALU.add, ALU.mult)
            dve.tensor_scalar(future_s[0:32, :], par("tri_s")[0:32, :], -1.0, -NEVER, ALU.add, ALU.mult) \
                .then_inc(mask_done, 1)
            for tt, (c0, n) in enumerate(TOK):
                b = ready(("acs", tt), HEADS, n)
                if tt:
                    dve.wait_ge(xd_done, tt)
                if tt:
                    act_read(("ab", tt - 1, 7))
                dve.tensor_scalar(nacs[0:n, :], b, -1.0, None, ALU.mult)
                dve.tensor_copy(acs[0:n, :], b).then_inc(dve_freed, 1)
                b = ready(("last", tt), HEADS, n)
                dve.tensor_copy(last_dec[0:n, :], b)
                dve.tensor_tensor(dec[0:n, :], b, acs[0:n, :], ALU.subtract).then_inc(ld_done, 1)
                dve.engine_nop().then_inc(dve_freed, 1)
                for i in range(4):
                    b = ready(("xt", tt, i), rows=n)
                    dve.tensor_tensor(xt[0:n, i * 512:(i + 1) * 512].rearrange("p (h f) -> p h f", f=64),
                                      b.rearrange("p (h f) -> p h f", f=64),
                                      dt[0:n, tt, 8 * i:8 * i + 8].unsqueeze(2).broadcast_to([n, 8, 64]),
                                      ALU.mult).then_inc(xt_done, 1)
                    dve.engine_nop().then_inc(dve_freed, 1)
                b = ready(("cb", tt), 4 * n, n)
                mask = tri[0:n, 0:n] if tt < 2 else par("tri_s")[0:n, :]
                dve.tensor_tensor(cbm[0:n, 0:4 * n].rearrange("p (g l) -> p g l", g=4),
                                  b.rearrange("p (g l) -> p g l", g=4),
                                  mask.unsqueeze(1).broadcast_to([n, 4, n]), ALU.mult).then_inc(cbm_done, 1)
                dve.engine_nop().then_inc(dve_freed, 1)

                def mix(hb):
                    k = tt * 8 + hb
                    g = hb // 2
                    act_read(("ab", tt, hb))
                    dve.wait_ge(cbm_done, tt + 1)
                    m = mt[k % 4][0:n, 0:4 * n].rearrange("p (h l) -> p h l", h=4)
                    dve.tensor_tensor(m, m, cbm[0:n, g * n:(g + 1) * n].unsqueeze(1).broadcast_to([n, 4, n]),
                                      ALU.mult).then_inc(mt_done, 1)
                    if tt == 1:
                        act_read(("state ab", hb))
                        if hb:
                            dve.wait_ge(full, KEY["y", 1, hb - 1] + 1)
                        dve.tensor_tensor(ce[:, :].rearrange("p (h l) -> p h l", h=4),
                                          eb[:, :].rearrange("p (h l) -> p h l", h=4),
                                          bc[:, 4 + g, c0:c0 + n].unsqueeze(1).broadcast_to([P, 4, n]),
                                          ALU.mult).then_inc(ce_done, 1)

                def outputs(hb):
                    b = ready(("y", tt, hb), 2 * n)
                    for j in range(2):
                        i = 2 * hb + j
                        a = dve.scalar_tensor_tensor(y[:, i, c0:c0 + n], y[:, i, c0:c0 + n],
                                                     par("ssd_d")[:, i:i + 1], b[:, j * n:(j + 1) * n],
                                                     ALU.mult, ALU.add)
                    a.then_inc(dve_freed, 1)

                for hb in range(9):
                    if hb < 8:
                        mix(hb)
                    if hb:
                        outputs(hb - 1)
                if tt == 1:
                    dve.wait_ge(sad_done, 1)
                    for g in range(GROUPS):
                        b = ready(("state", 1, g))
                        dve.tensor_tensor(s_b[:, g * 512:(g + 1) * 512], s_a[:, g * 512:(g + 1) * 512], b,
                                          ALU.add).then_inc(sb_done, 1)
                        dve.engine_nop().then_inc(dve_freed, 1)
            for bq in range(NB):
                a = dve.tensor_scalar(sdr[0:32, bq * HEADS:(bq + 1) * HEADS], acs[0:32, :],
                                      par("is_last")[0:32, bq:bq + 1], None, ALU.mult)
            a.then_inc(sdr_done, 1)
            act_read("s decay")
            dve.wait_ge(sh_done, 3)
            lo_half(own(cm[1], GROUPS), by_sequence(bc[:, 4:8, SEQ:NT]), own(cm[0], GROUPS), sl_done)
            for bq in range(NB):
                if bq >= 2:
                    dve.wait_ge(full, KEY["s state", bq - 2, GROUPS - 1] + 1)
                dve.tensor_scalar(btm[0:32, bq % 2, :], bt[0:32, :], par("in_seq")[0:32, bq:bq + 1], None,
                                  ALU.mult).then_inc(btm_done, 1)
                tiles = slice(2 * bq, 2 * bq + 2)
                dve.tensor_tensor(y[:, tiles, 0:SEQ], y[:, tiles, 0:SEQ], zs[:, tiles, 0:SEQ], ALU.mult) \
                    .then_inc(yz_done, 1)
                if bq == NB - 1:
                    dve.wait_ge(dec_done, 5)
                    for g in range(GROUPS):
                        b = ready(("y off", g, NB - 1), 512, 32)
                        dst = yo[g // 2][0:32, (g % 2) * 512:(g % 2 + 1) * 512]
                        dve.tensor_tensor(dst.rearrange("p (h f) -> p h f", f=64),
                                          b.rearrange("p (h f) -> p h f", f=64),
                                          ea[0:32, 8 * g:8 * g + 8].unsqueeze(2).broadcast_to([32, 8, 64]), ALU.mult) \
                            .then_inc(dve_freed, 1)
                for g in range(GROUPS):
                    b = ready(("s state", bq, g))
                    dve.wait_ge(sn_dec, 2 * bq + g // 2 + 1)
                    dst = s_new[2 * (bq % 2) + g // 2][:, (g % 2) * 512:(g % 2 + 1) * 512]
                    dve.tensor_tensor(dst, dst, b, ALU.add).then_inc(sn_done, 1)
                    dve.engine_nop().then_inc(dve_freed, 1)
            b = ready("y off turn")
            link(dve.tensor_tensor(y[:, :, SEQ:NT], y[:, :, SEQ:NT], b.rearrange("p (i s) -> p i s", i=KI), ALU.add))
            dve.engine_nop().then_inc(dve_freed, 1)
            dve.tensor_tensor(y[:, :, SEQ:NT], y[:, :, SEQ:NT], zs[:, :, SEQ:NT], ALU.mult).then_inc(yz_done, 1)
            for g in range(GROUPS + 1):
                if g < GROUPS:
                    act_read(("gn", g))
                    link(dve.reciprocal(grs[:, g, :], grt[:, g, :]))
                    for i in range(4 * g, 4 * g + 4):
                        a = dve.scalar_tensor_tensor(y[:, i, :], y[:, i, :], par("ssd_g")[:, i:i + 1],
                                                     grs[:, g, :], ALU.mult, ALU.mult)
                    a.then_inc(y_done, 1)
                if g:
                    tiles = slice(4 * g - 4, 4 * g)
                    dve.wait_ge(yh_done, KD + g)
                    lo_half(y_lo[:, tiles, :], y[:, tiles, :], y_hi[:, tiles, :], yl_done)
            residual(("ssd out",), gains("g_mem", 1), 6 * KD)
            attention(1)

            residual(("mem out", 1), None)
            act_read(("norm", 5))
            inverse(5)
            for k in range(KD):
                dve.scalar_tensor_tensor(h[:, k, :], x[:, k, :], gains("g_ffn", 1)[:, k:k + 1], rs[:, :],
                                         ALU.mult, ALU.mult).then_inc(h_done, 1)
            b = ready("logits", 24)
            link(dve.memset(lg[:, :, :], 0.0))
            dve.tensor_copy(lg[:, 0:2, :], b[:, 0:16].rearrange("p (a m) -> p a m", a=2))
            link(dve.tensor_copy(lg[0:32, 2, :], b[0:32, 16:24]))
            dve.engine_nop().then_inc(dve_freed, 1)
            wide = [P, 3, NE, NE]
            mine, other = lg[:, :, :].unsqueeze(3).broadcast_to(wide), lg[:, :, :].unsqueeze(2).broadcast_to(wide)
            lower = par("lower").rearrange("p (e j) -> p e j", e=NE).unsqueeze(1).broadcast_to(wide)
            dve.tensor_tensor(cmp1[:, :, :, :], other, mine, ALU.is_gt)
            link(dve.tensor_tensor(cmp2[:, :, :, :], other, mine, ALU.is_equal))
            link(dve.tensor_tensor(cmp2[:, :, :, :], cmp2[:, :, :, :], lower, ALU.mult))
            link(dve.tensor_tensor(cmp1[:, :, :, :], cmp1[:, :, :, :], cmp2[:, :, :, :], ALU.add))
            link(dve.tensor_reduce(rank[:, :, :], cmp1[:, :, :, :], AX.X, ALU.add))
            dve.memset(msk[:, :, :], 0.0)
            dve.memset(gts[:, :, :], 0.0)
            dve.memset(pos[:, :, :], 0.0)
            dve.tensor_scalar(m1[:, :, :], rank[:, :, :], 0.0, None, ALU.is_equal)
            link(dve.tensor_scalar(m2[:, :, :], rank[:, :, :], 1.0, None, ALU.is_equal))
            dve.tensor_tensor(msk[:, :, 0:NE], m1[:, :, :], m2[:, :, :], ALU.add).then_inc(msk_done, 1)
            dve.wait_ge(msk_done, 1)
            dve.tensor_tensor(cmp1[:, :, 0, :], m1[:, :, :], lg[:, :, :], ALU.mult)
            link(dve.tensor_tensor(cmp1[:, :, 1, :], m2[:, :, :], lg[:, :, :], ALU.mult))
            dve.tensor_reduce(v12[:, 0, :], cmp1[:, :, 0, :], AX.X, ALU.add)
            link(dve.tensor_reduce(v12[:, 1, :], cmp1[:, :, 1, :], AX.X, ALU.add))
            dve.tensor_tensor(v12[:, 2, :], v12[:, 1, :], v12[:, 0, :], ALU.subtract).then_inc(xp_done, 1)
            dve.wait_ge(xpe_done, 1)
            link(dve.tensor_scalar(v12[:, 0, :], v12[:, 3, :], 1.0, None, ALU.add))
            link(dve.reciprocal(v12[:, 0, :], v12[:, 0, :]))
            link(dve.tensor_tensor(m2[:, :, :], m2[:, :, :],
                                   v12[:, 3, :].unsqueeze(2).broadcast_to([P, 3, NE]), ALU.mult))
            link(dve.tensor_tensor(m1[:, :, :], m1[:, :, :], m2[:, :, :], ALU.add))
            link(dve.tensor_tensor(gts[:, :, 0:NE], m1[:, :, :],
                                   v12[:, 0, :].unsqueeze(2).broadcast_to([P, 3, NE]), ALU.mult))
            for c in range(1, 3):
                vs = slice(c * NE, (c + 1) * NE)
                dve.tensor_copy(gts[:, :, vs], gts[:, :, 0:NE])
                dve.tensor_copy(msk[:, :, vs], msk[:, :, 0:NE])
            b = ready("pos", 4 * NE)
            for c in range(3):
                vs = slice(c * NE, (c + 1) * NE)
                dve.tensor_scalar(pos[:, 0:2, vs], b[:, 0:2 * NE].rearrange("p (a m) -> p a m", a=2),
                                  float(-c * P), None, ALU.add)
                dve.tensor_scalar(pos[0:32, 2, vs], b[0:32, 2 * NE:3 * NE], float(-c * P), None, ALU.add)
            link(dve.tensor_reduce(cmax[:, :], b[:, 3 * NE:4 * NE], AX.X, ALU.max))
            dve.tensor_copy(cmax_i[:, :], cmax[:, :]).then_inc(cnt_done, 1)
            dve.engine_nop().then_inc(dve_freed, 1)
            def experts(c):
                s = PASSES[c]
                links = [0]

                def select(e):
                    for m, (_, n) in enumerate(TOK):
                        for dst, val in ((sel, msk), (selg, gts)):
                            a = dve.tensor_scalar(dst[0:n, m, :], par("iota")[0:n, :],
                                                  pos[0:n, m, bass.ds(e, 1)], val[0:n, m, bass.ds(e, 1)],
                                                  ALU.is_equal, ALU.mult)
                    a.then_inc(s.sel, 1)

                def lo(e, p):
                    dve.wait_ge(s.hi, e * CPE + p + 1)
                    dve.tensor_tensor(w_lo[:, (NSTAT + p) % HL, :], raw[:, (NSTAT + p) % RAW, :],
                                      w_hi[:, (NSTAT + p) % HL, :].bitcast(F32), ALU.subtract) \
                        .then_inc(s.lo, 1)

                def add_back(e, j):
                    dve.wait_ge(s.scat, e * KD + j + 1)
                    dve.tensor_tensor(x[:, j, :], x[:, j, :], ps[:, 5 + j % 3, 0:NT], ALU.add) \
                        .then_inc(s.add, 1)

                dve.memset(sg[:, :], 0.0).then_inc(s.sg, 1)
                v0, nv = VIRTUAL[c]
                if c:
                    dve.engine_nop().then_inc(s.lo, RAW)
                dve.engine_nop().then_inc(s.g, 2)
                dve.engine_nop().then_inc(s.gl, 1)
                dve.engine_nop().then_inc(s.add, 3)
                select(v0)
                dve.wait_ge(s.xh, 1)
                lo_half(xe_lo[:, :], ps[:, 0:2, :], xe_hi[:, :], s.xl)
                with dve.Fori(0, nv) as e:
                    done = 0

                    def ahead(n):
                        nonlocal done
                        while done < min(n, CPE):
                            lo(e, done)
                            done += 1

                    def turned(f):
                        dve.wait_ge(s.gh, e * FB + f + 1)
                        lo_half(gt_lo[:, 4 * f:4 * f + 4, :], ps[:, 4, :].rearrange("p (a m) -> p a m", a=4),
                                gt_hi[:, 4 * f:4 * f + 4, :], s.gl)

                    for f in range(FB):
                        if f >= 1:
                            ahead(8 * f + 4 + HL - 1)
                            turned(f - 1)
                        ahead(8 * f + 8 + HL - 1)
                        dve.wait_ge(s.used, e * CPE + 8 * f + 8 + HL)
                        dve.wait_ge(s.silu, e * FB + f + 1)
                        dve.tensor_tensor(ge[:, f % 2, :], sil[:, f % 2, :], ps[:, 2 + f % 2, :], ALU.mult) \
                            .then_inc(s.g, 1)
                        if f == 0:
                            for j in range(KD):
                                add_back(e, j)
                    ahead(8 * FB + 2 + HL - 1)
                    turned(FB - 1)
                    ahead(8 * FB + 4 + HL - 1)
                    dve.wait_ge(s.sgt, e + 1)
                    dve.tensor_copy(sg[:, :], ps[:, 2, 0:NT]).then_inc(s.sg, 1)
                    select(e + v0 + 1)
                    ahead(8 * FB + 16 + HL - 1)
                    dve.wait_ge(s.xh, e + 2)
                    lo_half(xe_lo[:, :], ps[:, 0:2, :], xe_hi[:, :], s.xl)
                    ahead(CPE)
                for j in range(KD):
                    add_back(nv, j)

            experts(0)
            over = overflow(dve)
            with dve.If(over > P):
                experts(1)
                dve.nop()
            dve.engine_nop().then_inc(resid, 1)
            dve.wait_ge(rt_done, 1)
            link(dve.reciprocal(rs[:, :], rt[:, :]))
            for k in range(KD):
                a = dve.scalar_tensor_tensor(h[:, k, :], x[:, k, :], par("g_fin")[:, k:k + 1], rs[:, :],
                                             ALU.mult, ALU.mult)
                if k % 4 == 3:
                    a.then_inc(fin_done, 1)

        @block.tensor
        def _(pe):
            opened, used = [0], [0]

            def claim(key, n=512, rows=P):
                g = KEY[key]
                if BEFORE[g] is not None:
                    eng, v = FREED[BEFORE[g]]
                    pe.wait_ge(act_freed if eng == "act" else dve_freed, v)
                return bank(g, n, rows)

            def count(key):
                assert KEY[key] == opened[0], (key, KEY[key], opened[0])
                opened[0] += 1

            def open_group(key, n=512, rows=P):
                count(key)
                return claim(key, n, rows)

            def close(ins):
                ins.then_inc(full, 1)

            def weights(k):
                if k >= used[0]:
                    pe.wait_ge(lo_done, k + 1)
                    used[0] = k + 1
                return w_hi[:, k % HL, :], w_lo[:, k % HL, :]

            def mm3(out, l_hi, l_lo, r_hi, r_lo, start, stop):
                pe.matmul(out, l_hi, r_hi, start=start, stop=False)
                pe.matmul(out, l_hi, r_lo, start=False, stop=False)
                return pe.matmul(out, l_lo, r_hi, start=False, stop=stop)

            def product(key, tiles, a_hi, a_lo, n=NT, halves=None, base=0, per=1):
                out = open_group(key, n)
                for m, (k, tl, ka) in enumerate(tiles):
                    hi, lo = weights(k)
                    if halves is not None and m % per == 0:
                        pe.wait_ge(halves, base + m // per + 1)
                    a = mm3(out, hi[:, tl * P:(tl + 1) * P], lo[:, tl * P:(tl + 1) * P],
                            a_hi[:, ka, :], a_lo[:, ka, :], m == 0, m == len(tiles) - 1)
                close(a)

            def square(key, a_hi, a_lo, n=NT, halves=None, base=0):
                k = NEED[KEY[key]] - 1
                product(key, [(k, tl, tl) for tl in range(KD)], a_hi, a_lo, n, halves, base)

            def norm(key, i):
                out = open_group(key, NT)
                pe.wait_ge(acc_done, (KD - 1) * (i + 2))
                close(pe.matmul(out, ones, rt[:, :], start=True, stop=True))

            def few(key, w, cols):
                out = open_group(key + " t", NT, cols)
                w = w.rearrange("p (k m) -> p k m", k=KD)
                for k in range(KD):
                    pe.wait_ge(h_done, (0 if key == "dt" else KD) + k + 1)
                    a = pe.matmul(out, w[:, k, :], h[:, k, :], start=(k == 0), stop=(k == KD - 1))
                close(a)
                pe.wait_ge(act_freed, FREED[KEY[key + " t"]][1])
                out = open_group(key, 3 * cols)
                for m, (c0, n) in enumerate(TOK):
                    a = pe.transpose(out[0:n, cols * m:cols * (m + 1)], small_t[0:cols, c0:c0 + n],
                                     ident[0:cols, 0:cols])
                close(a)

            def keys(l, js):
                for j in js:
                    square(("k", l, j), mem_hi[l], mem_lo[l], NMEM, hl_done if j == 0 else None, KD * l)
                    if l == 0 and j == 0:
                        out = open_group("mem norm", NMEM + 2)
                        pe.wait_ge(acc_done, KD - 1)
                        pe.matmul(out[:, 0:NMEM], ones, rt[:, 0:NMEM], start=True, stop=True)
                        for m in range(2):
                            a = pe.matmul(out[:, NMEM + m:NMEM + m + 1], rt[:, m * P:(m + 1) * P], ones[:, 0:1],
                                          start=True, stop=True)
                        close(a)

            def values(l):
                for nb in range(2):
                    outs = [open_group(("v", l, nb, m)) for m in range(2)]
                    for c in range(4):
                        hi, lo = weights(NEED[KEY["v", l, nb, 1]] - 4 + c)
                        for kk in range(2):
                            w = slice(kk * 512, (kk + 1) * 512)
                            ka = 2 * c + kk
                            for m in range(2):
                                a = mm3(outs[m], mem_hi[l][:, ka, m * P:(m + 1) * P],
                                        mem_lo[l][:, ka, m * P:(m + 1) * P], hi[:, w], lo[:, w], ka == 0, ka == KD - 1)
                                if ka == KD - 1:
                                    close(a)

            pe.wait_ge(small_in, 16)
            keys(0, range(KD))
            values(0)
            for j in range(KD):
                square(("gate", j), h_hi, h_lo, NT, hl_done if j == 0 else None, 2 * KD)
                if j == 0:
                    norm(("norm", 0), 0)
            for j in range(KD):
                square(("xb", j), h_hi, h_lo)
            keys(1, range(EARLY))
            for kind in ("r", "i"):
                k = NEED[KEY[kind, 0]] - 1
                for j in range(KD):
                    pe.wait_ge(xcl_done, j + 1)
                    product((kind, j), [(k, j, j)], xc_hi, xc_lo)
            keys(1, range(EARLY, KD))
            values(1)
            for j in range(KD):
                square(("lru out", j), xc_hi, xc_lo, NT, yl_done if j == 0 else None)

            def attention(l):
                for j in range(KD):
                    square(("q", l, j), h_hi, h_lo, NT, hl_done if j == 0 else None, (3 + 3 * l) * KD)
                    if j == 0:
                        norm(("norm", 3 * l + 1), 3 * l + 1)
                pe.wait_ge(dve_freed, FREED[KEY["q", l, KD - 1]][1])
                pe.wait_ge(kv_in, 32 * (l + 1))
                for hd in range(MH):
                    out = open_group(("scores", l, hd))
                    for tt in range(2):
                        for dd in range(2):
                            j = 2 * hd + dd
                            a = pe.matmul(out[:, tt * NMEM:(tt + 1) * NMEM], q[:, j, tt * P:(tt + 1) * P],
                                          kt[:, j, :], start=(dd == 0), stop=(dd == 1))
                    close(a)
                pe.wait_ge(sl_done, 1 + 3 * l)
                outs = [claim(("s scores", l, half, NB - 1), 512, 32) for half in range(2)]
                for b in range(NB):
                    if b == NB // 2:
                        pe.wait_ge(pn_done, 2 * l + 1)
                        for i in range(4):
                            turned = open_group(("probs", l, i))
                            m = i // 2
                            for hh in range(2):
                                for tt in range(2):
                                    blk = 2 * (2 * (i % 2) + hh) + tt
                                    col = hh * SEQ + tt * P
                                    a = pe.transpose(turned[:, col:col + P], pr[:, blk, m * P:(m + 1) * P], ident)
                            close(a)
                    for half in range(2):
                        count(("s scores", l, half, b))
                        k_hi, k_lo = weights(NEED[KEY["s scores", l, half, b]] - 1)
                        for hh in range(2):
                            hd = 2 * half + hh
                            for dd in range(2):
                                w = slice((2 * hh + dd) * NMEM, (2 * hh + dd + 1) * NMEM)
                                q_hi, q_lo = [v[:, (b * KD + 2 * hd + dd) * 32:(b * KD + 2 * hd + dd + 1) * 32]
                                              for v in qm]
                                a = mm3(outs[half][:, hh * NMEM:(hh + 1) * NMEM], q_hi, q_lo, k_hi[:, w], k_lo[:, w],
                                        b == 0 and hh == 0 and dd == 0, b == NB - 1 and hh == 1 and dd == 1)
                        close(a)
                for j in range(KD):
                    out = open_group(("o", l, j), SEQ)
                    if j == 0:
                        pe.wait_ge(dve_freed, FREED[KEY["probs", l, 3]][1])
                    for m in range(2):
                        a = pe.matmul(out, vt[:, m, j * P:(j + 1) * P], prt[:, m, j // 2, :],
                                      start=(m == 0), stop=(m == 1))
                    close(a)
                out = open_group(("s probs", l), NMEM)
                pe.wait_ge(pn_done, 2 * l + 2)
                for m in range(2):
                    for hd in range(MH):
                        a = pe.transpose(out[:, m * P + hd * 32:m * P + hd * 32 + 32],
                                         prs[0:32, hd, m * P:(m + 1) * P], ident[0:32, 0:32])
                close(a)
                outs = [claim(("s o", l, half, NB - 1), 512, 32) for half in range(2)]
                pe.wait_ge(sl_done, 2 + 3 * l)
                for b in range(NB):
                    for half in range(2):
                        count(("s o", l, half, b))
                        v_hi, v_lo = weights(NEED[KEY["s o", l, half, b]] - 1)
                        for hh in range(2):
                            hd = 2 * half + hh
                            for m in range(2):
                                w = slice(m * 512 + hh * NMEM, m * 512 + (hh + 1) * NMEM)
                                p_hi, p_lo = [v[:, m, (b * MH + hd) * 32:(b * MH + hd + 1) * 32] for v in pm]
                                a = mm3(outs[half][:, hh * NMEM:(hh + 1) * NMEM], p_hi, p_lo, v_hi[:, w], v_lo[:, w],
                                        b == 0 and hh == 0 and m == 0, b == NB - 1 and hh == 1 and m == 1)
                        close(a)
                out = open_group(("s o turn", l), NMEM)
                pe.wait_ge(act_freed, FREED[KEY["s o", l, 1, NB - 1]][1])
                for j in range(KD):
                    a = pe.transpose(out[:, j * 32:(j + 1) * 32], so[0:32, j * P:(j + 1) * P], ident[0:32, 0:32])
                close(a)
                pe.wait_ge(dve_freed, FREED[KEY["s o turn", l]][1])
                for j in range(KD):
                    square(("mem out", l, j), att_hi, att_lo)

            attention(0)
            for f in range(KF):
                square(("f1", f), h_hi, h_lo, NT, hl_done if f == 0 else None, 4 * KD)
                if f == 0:
                    norm(("norm", 2), 2)
                square(("f3", f), h_hi, h_lo)
            pe.wait_ge(fl_done, KF)
            first = NEED[KEY["f2", 0]] - -(-KF // 8)
            for j in range(KD):
                product(("f2", j), [(first + (j * KF + k) // 8, (j * KF + k) % 8, k) for k in range(KF)],
                        f_hi, f_lo)

            norm(("norm", 3), 3)
            for c in range(NXBC):
                square(("xbc", c), h_hi, h_lo, NT, hl_done if c == 0 else None, 5 * KD)
                if c == 2:
                    few("dt", par("w_dt"), HEADS)
            for c in range(KI):
                square(("z", c), h_hi, h_lo)
            pe.wait_ge(adt_done, 1)
            pe.wait_ge(silu_done, NXBC)
            for tt, (c0, n) in enumerate(TOK):
                within = tri[0:n, 0:n] if tt < 2 else par("tri_s")[0:n, :]
                out = open_group(("acs", tt), HEADS, n)
                close(pe.matmul(out, within, adt[0:n, tt, :], start=True, stop=True))
                out = open_group(("last", tt), HEADS, n)
                pe.wait_ge(dve_freed, FREED[KEY["acs", tt]][1])
                close(pe.matmul(out, par("last")[0:n, 0:n] if tt < 2 else par("last_s")[0:n, :], acs[0:n, :],
                                start=True, stop=True))
                for i in range(4):
                    out = open_group(("xt", tt, i), rows=n)
                    for k in range(4):
                        a = pe.transpose(out[:, k * P:(k + 1) * P], y[:, 4 * i + k, c0:c0 + n], ident)
                    close(a)
                out = open_group(("bt", tt), rows=n)
                for g in range(GROUPS):
                    a = pe.transpose(out[:, g * P:(g + 1) * P], bc[:, g, c0:c0 + n], ident)
                close(a)
                out = open_group(("cb", tt), 4 * n, n)
                for g in range(GROUPS):
                    a = pe.matmul(out[:, g * n:(g + 1) * n], bc[:, g, c0:c0 + n], bc[:, 4 + g, c0:c0 + n],
                                  start=True, stop=True)
                close(a)

                def sums(key, hb, mask):
                    out = open_group(key, 4 * n, n)
                    for j in range(4):
                        for half in range(2):
                            a = pe.matmul(out[:, j * n:(j + 1) * n],
                                          adt_s[half][0:n, tt, 4 * hb + j:4 * hb + j + 1].broadcast_to([n, n]),
                                          tri_r[:, :] if tt < 2 else tri_sr[0:32, :],
                                          start=(j == 0 and half == 0), stop=(j == 3 and half == 1 and not mask))
                    if mask:
                        later = future_r[:, :] if tt < 2 else future_s[0:32, :]
                        for j in range(4):
                            a = pe.matmul(out[:, j * n:(j + 1) * n], ident_r[0:n, 0:n], later,
                                          start=False, stop=(j == 3))
                    close(a)

                pe.wait_ge(mask_done, 1)
                for hb in range(10):
                    if hb < 8:
                        sums(("ab", tt, hb), hb, True)
                        if tt == 1:
                            sums(("state ab", hb), hb, False)
                    if hb < 2:
                        continue
                    hb -= 2
                    if hb == 0:
                        pe.wait_ge(dve_freed, FREED[KEY["xt", tt, 3]][1])
                    out = open_group(("y", tt, hb), 2 * n)
                    pe.wait_ge(mt_done, tt * 8 + hb + 1)
                    if tt == 1:
                        if hb == 0:
                            pe.wait_ge(act_freed, FREED[KEY["state", 0, GROUPS - 1]][1])
                        pe.wait_ge(ce_done, hb + 1)
                    for j in range(4):
                        hd = 4 * hb + j
                        o = out[64 * (hd % 2):64 * (hd % 2) + 64, (j // 2) * n:(j // 2 + 1) * n]
                        a = pe.matmul(o, xt[0:n, hd * 64:(hd + 1) * 64], mt[(tt * 8 + hb) % 4][0:n, j * n:(j + 1) * n],
                                      start=True, stop=(tt != 1))
                        if tt == 1:
                            a = pe.matmul(o, s_a[:, hd * 64:(hd + 1) * 64], ce[:, j * n:(j + 1) * n],
                                          start=False, stop=True)
                    close(a)
                if tt < 2:
                    pe.wait_ge(act_freed, FREED[KEY["bt", tt]][1])
                    pe.wait_ge(xd_done, tt + 1)
                    for g in range(GROUPS):
                        out = open_group(("state", tt, g))
                        close(pe.matmul(out, bt[:, g * P:(g + 1) * P], xd[:, g * 512:(g + 1) * 512],
                                        start=True, stop=True))
            out = open_group("s decay", NB * HEADS)
            pe.wait_ge(sdr_done, 1)
            close(pe.matmul(out, ones[0:32, :], sdr[0:32, :], start=True, stop=True))
            pe.wait_ge(xd_done, 3)
            pe.wait_ge(sl_done, 3)
            off = [claim(("y off", g, NB - 1), 512, 32) for g in range(GROUPS)]
            for b in range(NB):
                for g in range(GROUPS):
                    count(("y off", g, b))
                    s_hi, s_lo = weights(NEED[KEY["y off", g, b]] - 1)
                    w = slice((g % 2) * 512, (g % 2 + 1) * 512)
                    c_hi, c_lo = [v[:, (b * GROUPS + g) * 32:(b * GROUPS + g + 1) * 32] for v in cm]
                    close(mm3(off[g], c_hi, c_lo, s_hi[:, w], s_lo[:, w], b == 0, b == NB - 1))
                pe.wait_ge(btm_done, b + 1)
                for g in range(GROUPS):
                    out = open_group(("s state", b, g))
                    close(pe.matmul(out, btm[0:32, b % 2, g * P:(g + 1) * P], xd[0:32, g * 512:(g + 1) * 512],
                                    start=True, stop=True))
            out = open_group("y off turn")
            pe.wait_ge(dve_freed, FREED[KEY["y off", GROUPS - 1, NB - 1]][1])
            for i in range(KI):
                a = pe.transpose(out[:, i * 32:(i + 1) * 32], yo[i // 8][0:32, (i % 8) * P:(i % 8 + 1) * P],
                                 ident[0:32, 0:32])
            close(a)
            for g in range(GROUPS):
                out = open_group(("gn", g), NT)
                pe.wait_ge(ysq_done, NB + 1)
                for k in range(4):
                    a = pe.matmul(out, ones, ysq[:, 4 * g + k, :], start=(k == 0), stop=(k == 3))
                close(a)
            for j in range(KD):
                k0 = NEED[KEY["ssd out", j]] - 2
                product(("ssd out", j), [(k0 + k // 8, k % 8, k) for k in range(KI)], y_hi, y_lo, NT,
                        yl_done if j == 0 else None, KD, 4)
            attention(1)
            norm(("norm", 5), 5)
            few("logits", par("router"), NE)
            for i in range(6):
                c0, n = TOK[i // 2]
                out = open_group(("ht", i), rows=n)
                for k in range(4):
                    a = pe.transpose(out[:, k * P:(k + 1) * P], h[:, 4 * (i % 2) + k, c0:c0 + n], ident)
                close(a)
            out = open_group("pos", 4 * NE)
            pe.wait_ge(msk_done, 1)
            for m, (_, n) in enumerate(TOK):
                for k in range(m):
                    pe.matmul(out[0:n, NE * m:NE * m + NE], ones[:, 0:n], msk[:, k, 0:NE], start=(k == 0), stop=False)
                pe.matmul(out[0:n, NE * m:NE * m + NE], par("before")[0:n, 0:n], msk[0:n, m, 0:NE],
                          start=(m == 0), stop=True)
            for m, (_, n) in enumerate(TOK):
                a = pe.matmul(out[:, 3 * NE:4 * NE], ones[0:n, :], msk[0:n, m, 0:NE], start=(m == 0), stop=(m == 2))
            close(a)
            pe.wait_ge(act_freed, freed_n["act"])
            pe.wait_ge(dve_freed, freed_n["dve"])

            def experts(c):
                s = PASSES[c]

                def gather(e):
                    pe.wait_ge(s.sel, e + 1)
                    for j in range(KD):
                        for m, (_, n) in enumerate(TOK):
                            a = pe.matmul(ps[:, j // 4, (j % 4) * P:(j % 4 + 1) * P], htok[0:n, m, j * P:(j + 1) * P],
                                          sel[0:n, m, :], start=(m == 0), stop=(m == 2))
                    a.then_inc(s.gather, 1)

                def scatter(e):
                    pe.wait_ge(s.ye, e + 1)
                    for j in range(KD):
                        pe.wait_ge(s.add, e * KD + j + 1)
                        pe.matmul(ps[:, 5 + j % 3, 0:NT], ye[:, j * P:(j + 1) * P], sg[:, :],
                                  start=True, stop=True).then_inc(s.scat, 1)

                nv = VIRTUAL[c][1]
                if c:
                    pe.wait_ge(PASSES[0].add, VIRTUAL[0][1] * KD + KD + 3)
                pe.wait_ge(s.sg, 1)
                for j in range(2):
                    for k in range(2):
                        a = pe.matmul(ps[:, 5 + j, k * 256:(k + 1) * 256], sg[:, 0:P], sg[:, 0:256],
                                      start=True, stop=True)
                a.then_inc(s.used, HL)
                gather(0)
                with pe.Fori(0, nv) as e:
                    pe.wait_ge(s.xl, e + 1)

                    def up(f, which):
                        out = ps[:, 2 * which + f % 2, :]
                        for c4 in range(4):
                            p = 8 * f + 4 * which + c4
                            k = (NSTAT + p) % HL
                            pe.wait_ge(s.lo, e * CPE + p + 1 + RAW)
                            for kk in range(2):
                                ka, w = 2 * c4 + kk, slice(kk * 512, (kk + 1) * 512)
                                a = mm3(out, xe_hi[:, ka * P:(ka + 1) * P], xe_lo[:, ka * P:(ka + 1) * P],
                                        w_hi[:, k, w], w_lo[:, k, w], ka == 0, ka == KD - 1)
                            a.then_inc(s.used, 1)

                    def turn(f):
                        pe.wait_ge(s.g, e * FB + f + 1 + 2)
                        pe.wait_ge(s.gl, e * FB + f + 1)
                        for k in range(4):
                            a = pe.transpose(ps[:, 4, k * P:(k + 1) * P], ge[:, f % 2, k * P:(k + 1) * P], ident)
                        a.then_inc(s.turn, 1)

                    for f in range(FB):
                        pe.wait_ge(s.g, e * FB + f + 1)
                        up(f, 0)
                        if f == 0:
                            pe.wait_ge(s.sg, e + 1)
                        else:
                            turn(f - 1)
                        up(f, 1)
                        if f == 0:
                            scatter(e)
                    pe.wait_ge(s.add, e * KD + KD + 3)
                    for kt_ in range(KFE):
                        if kt_ == 2:
                            turn(FB - 1)
                        if kt_ == 4:
                            pe.wait_ge(s.sel, e + 1)
                            for m, (c0, n) in enumerate(TOK):
                                a = pe.transpose(ps[:, 2, c0:c0 + n], selg[0:n, m, :], ident[0:n, 0:n])
                            a.then_inc(s.sgt, 1)
                        if kt_ == 16:
                            gather(e + 1)
                        p = 8 * FB + kt_
                        k = (NSTAT + p) % HL
                        pe.wait_ge(s.gl, e * FB + kt_ // 4 + 2)
                        pe.wait_ge(s.lo, e * CPE + p + 1 + RAW)
                        for nb in range(2):
                            w = slice(nb * 512, (nb + 1) * 512)
                            a = mm3(ps[:, 5 + nb, :], gt_hi[:, kt_, :], gt_lo[:, kt_, :], w_hi[:, k, w], w_lo[:, k, w],
                                    kt_ == 0, kt_ == KFE - 1)
                        a.then_inc(s.used, 1)
                scatter(nv)

            experts(0)
            over = overflow(pe)
            with pe.If(over > P):
                experts(1)
                pe.nop()
            for k in range(KD):
                pe.wait_ge(sq_done, 7 * KD + k + 1)
                a = pe.matmul(ps[:, 0, 0:NT], ones, h[:, k, :], start=(k == 0), stop=(k == KD - 1))
            a.then_inc(full, 1)

        @block.gpsimd
        def _(pool):
            def add_squares(i, sq):
                n = sq.shape[-1]
                for j in range(1, KD):
                    pool.wait_ge(sq_done, KD * (i + 1) + j + 1)
                    if j > 1:
                        pool.wait_ge(acc_done, (KD - 1) * (i + 1) + j - 1)
                    elif i > 0:
                        pool.wait_ge(rs_done, i + 1)
                    pool.tensor_tensor(rt[:, 0:n], sq[:, 0, :] if j == 1 else rt[:, 0:n], sq[:, j, :], ALU.add) \
                        .then_inc(acc_done, 1)

            add_squares(-1, memsq)
            pool.wait_ge(full, KEY["mem norm"] + 1)
            add_squares(0, h)
            pool.wait_ge(small_in, 16)
            pool.wait_ge(kv_out, 32)
            pool.memset(conv[:, :, 0:CW - 1], 0.0)
            prev = par("lru_prev").rearrange("p (j b w) -> p j b w", b=NB, w=3)
            for j in range(KD):
                a = pool.tensor_copy(samples(conv[:, j, PS0:PADW], TS + CW - 1, 0, CW - 1), prev[:, j, :, :])
            a.then_inc(cinit, 1)
            pool.wait_ge(dve_freed, FREED[KEY["xb", KD - 1]][1])
            for j in range(KD):
                pool.tensor_copy(lru_new_c[:, j, 0:3], conv[:, j, SEQ:SEQ + 3])
                a = pool.tensor_copy(lru_new_c[:, j, 3:27].rearrange("p (b w) -> p b w", w=3),
                                     samples(conv[:, j, PS0:PADW], TS + CW - 1, TS, CW - 1))
            a.then_inc(state_ready, 1)
            pool.wait_ge(state_ready, 1)
            for k in range(KD):
                pool.wait_ge(a_done, k + 1)
                pool.tensor_tensor(expm[:, k, :], decay[:, k, :], decay[:, k, :], ALU.mult).then_inc(sqr_done, 1)
            pool.wait_ge(hs_done, 1)
            pool.tensor_copy(lru_new_h[:, :, 0], xc[:, :, SEQ - 1])
            pool.tensor_copy(lru_new_h[:, :, 1:1 + NB],
                             xc[:, :, SEQ:NT].rearrange("p j (b w) -> p j b w", w=TS)[:, :, :, TS - 1]) \
                .then_inc(state_ready, 1)
            pool.wait_ge(state_ready, 2)
            pool.dma_start(t["out_lru_c"], lru_new_c[:, :, :]).then_inc(out_done, 16)
            pool.dma_start(t["out_lru_h"], lru_new_h[:, :, :]).then_inc(out_done, 16)

            def load_kv(l):
                pool.dma_start(kt[:, :, :], t["out_k"][l]).then_inc(kv_in, 16)
                pool.dma_start(vt[:, :, :], t["out_v"][l]).then_inc(kv_in, 16)

            def zero_attention(l):
                add_squares(3 * l + 1, h)
                pool.wait_ge(full, KEY["norm", 3 * l + 1] + 1)
                pool.memset(qm[0][:, :].bitcast(F32), 0.0)
                pool.memset(qm[1][:, :].bitcast(F32), 0.0).then_inc(zero_done, 1)
                pool.wait_ge(full, KEY["q", l, KD - 1] + 1)
                pool.memset(pm[0][:, :, :].bitcast(F32), 0.0)
                pool.memset(pm[1][:, :, :].bitcast(F32), 0.0).then_inc(zero_done, 1)

            pool.wait_ge(y_done, KD)
            pool.wait_ge(full, KEY["v", 1, 1, 1] + 1)
            pool.wait_ge(kv_out, 64)
            load_kv(0)
            zero_attention(0)
            add_squares(2, h)
            add_squares(3, h)
            pool.wait_ge(dve_freed, FREED[KEY["f2", KD - 1]][1])
            pool.dma_start(ssd_prev[:, :, :, :], t["ssd_prev"]).then_inc(prev_in, 16)
            for c in range(3):
                a = pool.memset(cv[:, c, 0:CW - 1], 0.0)
            pool.wait_ge(prev_in, 16)

            def before(c):
                pool.tensor_copy(samples(cv[:, c % 3, PS0:PADW], TS + CW - 1, 0, CW - 1), ssd_prev[:, c, :, :]) \
                    .then_inc(prev_done, 1)

            for c in range(3):
                before(c)
            for c in range(NXBC):
                pool.wait_ge(act_freed, FREED[KEY["xbc", c]][1])
                pool.tensor_copy(ssd_new_c[:, c, 0:3], cv[:, c % 3, SEQ:SEQ + 3])
                pool.tensor_copy(ssd_new_c[:, c, 3:27].rearrange("p (b w) -> p b w", w=3),
                                 samples(cv[:, c % 3, PS0:PADW], TS + CW - 1, TS, CW - 1)) \
                    .then_inc(save_done, 1)
                if c + 3 < NXBC:
                    pool.wait_ge(cvo_done, c + 1)
                    before(c + 3)
            pool.wait_ge(save_done, NXBC)
            pool.dma_start(t["out_ssd_c"], ssd_new_c[:, :, :]).then_inc(out_done, 16)
            for tt, (_, n) in enumerate(TOK):
                pool.wait_ge(xt_done, 4 * (tt + 1))
                pool.wait_ge(dec_done, (1, 2, 4)[tt])
                if tt:
                    pool.wait_ge(full, KEY["state", tt - 1, GROUPS - 1] + 1)
                pool.tensor_tensor(xd[0:n, :].rearrange("p (h f) -> p h f", f=64),
                                   xt[0:n, :].rearrange("p (h f) -> p h f", f=64),
                                   dec[0:n, :].unsqueeze(2).broadcast_to([n, HEADS, 64]), ALU.mult) \
                    .then_inc(xd_done, 1)
                if tt == 1:
                    pool.wait_ge(dec_done, 3)
                    pool.wait_ge(full, KEY["y", 1, 7] + 1)
                    sv = s_a[:, :].rearrange("p (h f) -> p h f", f=64)
                    pool.tensor_tensor(sv, sv, cdec[:, :].unsqueeze(2).broadcast_to([P, HEADS, 64]),
                                       ALU.mult).then_inc(sad_done, 1)
            pool.wait_ge(sb_done, GROUPS)
            pool.dma_start(t["out_ssd_p"], s_b[:, :]).then_inc(state_out[4], 16)
            pool.wait_ge(full, KEY["y", 2, 7] + 1)
            pool.wait_ge(xd_done, 3)
            pool.memset(cm[0][:, :].bitcast(F32), 0.0)
            pool.memset(cm[1][:, :].bitcast(F32), 0.0).then_inc(zero_done, 1)
            pool.wait_ge(act_freed, FREED[KEY["s decay"]][1])
            pool.wait_ge(sl_done, 3)

            def decayed(b):
                for half in range(2):
                    i, k = STATE_AT + 2 * b + half, 2 * (b % 2) + half
                    pool.wait_ge(landed[i % RAW], 16 * (i // RAW + 1))
                    if b >= 2:
                        pool.wait_ge(state_out[k], 16 * (b // 2))
                    else:
                        pool.wait_ge(state_out[4], 16)
                    pool.tensor_tensor(s_new[k][:, :].rearrange("p (h f) -> p h f", f=64),
                                       raw[:, i % RAW, :].rearrange("p (h f) -> p h f", f=64),
                                       sdec[:, b * HEADS + 16 * half:b * HEADS + 16 * half + 16]
                                       .unsqueeze(2).broadcast_to([P, 16, 64]), ALU.mult).then_inc(sn_dec, 1)

            decayed(0)
            for b in range(NB):
                if b + 1 < NB:
                    decayed(b + 1)
                for half in range(2):
                    k = 2 * (b % 2) + half
                    pool.wait_ge(sn_done, 4 * b + 2 * half + 2)
                    pool.dma_start(t["out_ssd_s"][b, half], s_new[k][:, :]).then_inc(state_out[k], 16)
            for k in range(4):
                pool.wait_ge(state_out[k], 16 * (NB // 2))
            pool.wait_ge(full, KEY["ssd out", KD - 1] + 1)
            load_kv(1)
            zero_attention(1)
            add_squares(5, h)
            pool.wait_ge(out_done, 48)


def small_inputs(np, a):
    s = np.zeros((P, NSMALL), np.float32)

    def put(name, v):
        at, n = SMALL[name]
        v = np.asarray(v)
        s[:v.shape[0], at:at + n] = v.reshape(v.shape[0], n)

    def tiles(v):
        v = np.asarray(v)
        v = v.reshape(v.shape[:-1] + (-1, P))
        return np.moveaxis(v, (-1, -2), (0, 1))

    def gains(v):
        return np.asarray(v).reshape(-1, P).T
    put("g_mix", gains(a["norm_mix"]))
    put("g_mem", gains(a["norm_mem"]))
    put("g_memkv", gains(a["norm_memkv"]))
    put("g_ffn", gains(a["norm_ffn"]))
    put("g_fin", gains(a["norm_final"]))
    put("lru_cw", tiles(a["lru_conv_w"][0]))
    put("lru_cb", tiles(a["lru_conv_b"][0]))
    put("b_a", tiles(a["lru_b_a"][0]))
    put("b_x", tiles(a["lru_b_x"][0]))
    put("lam", tiles(a["lru_lam"][0]))
    put("h_prev", tiles(a["state_lru_h"][0]))
    put("lru_prev", tiles(a["state_lru_conv"][0]))
    put("ssd_cw", tiles(a["ssd_conv_w"][0]))
    put("ssd_cb", tiles(a["ssd_conv_b"][0]))
    put("ssd_g", tiles(a["ssd_norm_g"][0]))
    put("ssd_d", tiles(np.repeat(np.asarray(a["ssd_d"][0]), 64)))
    put("dt_b", np.broadcast_to(np.asarray(a["ssd_dt_bias"][0]), (P, HEADS)))
    put("a_log", np.broadcast_to(np.asarray(a["ssd_a_log"][0]), (P, HEADS)))
    put("router", np.asarray(a["moe_router"][0]).reshape(KD, P, NE).transpose(1, 0, 2))
    put("w_dt", np.asarray(a["ssd_w_in"][0])[:, DI + NXBC * P:].reshape(KD, P, HEADS).transpose(1, 0, 2))
    i = np.arange(P)
    j = np.arange(32)
    put("ident", np.eye(P))
    put("tri", i[:, None] <= i[None])
    put("tri_s", (j[:, None] <= j[None]) & (j[:, None] // TS == j[None] // TS))
    put("last", np.broadcast_to(i[:, None] == P - 1, (P, P)))
    put("last_s", j[:, None] == TS * (j[None] // TS) + TS - 1)
    put("is_last", j[:, None] == TS * np.arange(NB)[None] + TS - 1)
    put("in_seq", j[:, None] // TS == np.arange(NB)[None])
    put("ones", np.ones((P, P)))
    put("before", i[:, None] < i[None])
    put("iota", np.broadcast_to(i[None], (P, P)))
    e = np.arange(NE)
    put("lower", np.broadcast_to((e[None] < e[:, None])[None], (P, NE, NE)))
    put("eps", np.full((P, 1), EPS))
    return s


def stream_inputs(np, a):
    def columns(w):
        w = np.asarray(w)
        k, n = w.shape
        return w.reshape(k // P, P, n // P, P).transpose(2, 1, 0, 3).reshape(n // P, P, k)

    def flat(w):
        w = columns(w)
        n, _, k = w.shape
        w = w.reshape(n, P, k // P, P).transpose(0, 2, 1, 3).reshape(-1, 8, P, P)
        return w.transpose(0, 2, 1, 3).reshape(-1, P, CH)

    def rows(w):
        w = np.asarray(w)
        k, n = w.shape
        w = w.reshape(k // (2 * P), 2, P, n // 512, 512)
        return w.transpose(3, 0, 2, 1, 4).reshape(-1, P, CH)

    def keys(c):
        c = np.asarray(c).reshape(NB, NMEM, 2, 4, P)
        return c.transpose(0, 2, 4, 3, 1).reshape(-1, P, CH)

    def values(c):
        c = np.asarray(c).reshape(NB, 2, P, 2, 512)
        return c.transpose(0, 3, 2, 1, 4).reshape(-1, P, CH)

    def memory(l):
        return [columns(a["mem_w_k"][l]), rows(a["mem_w_v"][l])]

    parts = memory(0) + [columns(a["lru_w_in"][0])]
    keys_1, values_1 = memory(1)
    parts += [keys_1[:EARLY]]
    for w in ("lru_w_a", "lru_w_x"):
        parts += [np.asarray(a[w][0]).transpose(1, 0, 2).reshape(1, P, CH)]
    parts += [keys_1[EARLY:], values_1, columns(a["lru_w_out"][0])]

    def attention(l):
        return [columns(a["mem_w_q"][l]), keys(a["cache_mem_k"][l]), values(a["cache_mem_v"][l]),
                columns(a["mem_w_o"][l])]

    parts += attention(0)
    w1, w3 = columns(a["ffn_w1"][0]), columns(a["ffn_w3"][0])
    parts += [np.stack([w1, w3], 1).reshape(-1, P, CH), flat(a["ffn_w2"][0])]
    w_in = np.asarray(a["ssd_w_in"][0])
    parts += [columns(w_in[:, DI:DI + NXBC * P]), columns(w_in[:, :DI])]
    state = np.asarray(a["state_ssd"][0]).reshape(NB, 2, 16 * 64, P)
    parts += [state.transpose(0, 1, 3, 2).reshape(-1, P, CH)]
    parts += [flat(a["ssd_w_out"][0])]
    parts += attention(1)
    stream = np.concatenate(parts)
    assert stream.shape == (NSTAT, P, CH), stream.shape
    experts = np.empty((NE, CPE, P, CH), np.float32)
    for e in range(NE):
        up = experts[e, :8 * FB].reshape(FB, 2, 4, P, CH)
        up[:, 0] = rows(a["moe_w1"][0][e]).reshape(FB, 4, P, CH)
        up[:, 1] = rows(a["moe_w3"][0][e]).reshape(FB, 4, P, CH)
        experts[e, 8 * FB:] = np.asarray(a["moe_w2"][0][e]).reshape(KFE, P, CH)
    return stream, experts.reshape(NE * CPE, P, CH)


OUTS = {"out_x": (P, KD, NT), "out_k": (2, P, KD, NMEM), "out_v": (2, P, 2, D),
        "out_lru_h": (P, KD, 1 + NB), "out_lru_c": (P, KD, 27), "out_ssd_c": (P, NXBC, 27),
        "out_ssd_p": (P, DI), "out_ssd_s": (NB, 2, P, CH)}


def kernel(**inputs):
    import numpy as np
    import concourse.bacc as bacc
    from concourse.bass_utils import run_bass_kernel_spmd

    a = {k: np.asarray(v) for k, v in inputs.items()}
    stream, experts = stream_inputs(np, a)

    def feature_major(v):
        return np.ascontiguousarray(v.reshape(v.shape[0], KD, P).transpose(2, 1, 0))

    arrays = {
        "stream": stream, "experts": experts, "small": small_inputs(np, a),
        "x": feature_major(np.concatenate([a["x_prompt"][0], a["x_sample"].reshape(NB * TS, D)])),
        "mem": feature_major(a["mem_prompt"][0]),
        "ssd_prev": np.ascontiguousarray(
            a["state_ssd_conv"][0].reshape(NB, 3, NXBC, P).transpose(3, 2, 0, 1)),
    }
    nc = bacc.Bacc("TRN2", target_bir_lowering=False, num_devices=1)
    t = {k: nc.dram_tensor(f"in_{k}", v.shape, F32, kind="ExternalInput").ap() for k, v in arrays.items()}
    t.update({k: nc.dram_tensor(k, s, F32, kind="ExternalOutput").ap() for k, s in OUTS.items()})
    build_program(nc, t)
    r = run_bass_kernel_spmd(nc, [{f"in_{k}": v for k, v in arrays.items()}], core_ids=[0]).results[0]

    def tokens(v):
        return np.asarray(v).transpose(2, 1, 0).reshape(v.shape[2], -1)

    out = tokens(r["out_x"])
    lru_h, lru_c, ssd_c = tokens(r["out_lru_h"]), tokens(r["out_lru_c"]), tokens(r["out_ssd_c"])
    mem_k = np.stack([tokens(r["out_k"][l]) for l in range(2)]).reshape(2, 1, NMEM, MH, 256)
    mem_v = np.asarray(r["out_v"]).transpose(0, 2, 1, 3).reshape(2, 1, NMEM, MH, 256)
    ssd_p = np.asarray(r["out_ssd_p"]).T.reshape(1, 1, HEADS, 64, P)
    ssd_s = np.asarray(r["out_ssd_s"]).transpose(0, 1, 3, 2).reshape(1, NB, HEADS, 64, P)
    return (out[:SEQ].reshape(1, SEQ, D), out[SEQ:].reshape(NB, TS, D),
            lru_h[:1].reshape(1, 1, D), lru_c[:3].reshape(1, 1, 3, D), ssd_p, ssd_c[:3].reshape(1, 1, 3, NXBC * P),
            mem_k, mem_v,
            lru_h[1:].reshape(1, NB, D), lru_c[3:].reshape(1, NB, 3, D), ssd_s,
            ssd_c[3:].reshape(1, NB, 3, NXBC * P))
```
